# Optimizing a Trainium2 kernel written in Bass

```python
import math, functools
import jax, jax.numpy as jnp
from jax import lax
import numpy as np

D_MODEL = 1024
BATCH = 1
SEQ = 512
DEPTH = 2
DEC_BATCH = 8
DEC_SEQ = 1
PAST_LEN = 256
PAGE_SIZE = 128

GROUP_W = D_MODEL // 4
HEAD_DIM = 64
N_HEADS_A = GROUP_W // HEAD_DIM
N_KV_HEADS = N_HEADS_A
N_IDX_HEADS = 8
IDX_DIM = 32
TOPK_MAX = 256
Q_BLOCK = 128
ROPE_THETA = 500000.0
B_W = GROUP_W
B_CONV = 3
C_W = GROUP_W
C_CONV = 31
D_HEAD_DIM = 64
D_HEADS = GROUP_W // D_HEAD_DIM
D_W = D_HEADS * D_HEAD_DIM
D_GROUPS = 2
D_STATE = 128
D_CONV = 4
D_XBC = D_W + 2 * D_GROUPS * D_STATE
SSD_CHUNK = 128
A_W = N_HEADS_A * HEAD_DIM
KV_W = N_KV_HEADS * HEAD_DIM
MIX_W = A_W + B_W + C_W + D_W
IN_SIZES = (A_W, KV_W, KV_W, N_IDX_HEADS * IDX_DIM, IDX_DIM, N_IDX_HEADS, B_W, B_W, B_W, 2 * C_W, D_W, D_XBC, D_HEADS)
IN_W = sum(IN_SIZES)
D_FF = -(-8 * D_MODEL // (3 * 256)) * 256
RMS_EPS = 1e-6
LN_EPS = 1e-5

kernel_name = 'hybrid_dsa_conv_ssd_decoder_step'

def rms_norm(x, g):
    xf = x.astype(jnp.float32)
    y = xf * lax.rsqrt(jnp.mean(xf * xf, axis=-1, keepdims=True) + RMS_EPS)
    return (y * g.astype(jnp.float32)).astype(x.dtype)

def layer_norm(x, g, b):
    xf = x.astype(jnp.float32)
    mu = jnp.mean(xf, axis=-1, keepdims=True)
    var = jnp.mean(jnp.square(xf - mu), axis=-1, keepdims=True)
    return ((xf - mu) * lax.rsqrt(var + LN_EPS) * g.astype(jnp.float32) + b.astype(jnp.float32)).astype(x.dtype)

def rope(x, pos):
    rot = x.shape[-1] // 4
    half = rot // 2
    inv = ROPE_THETA ** (-jnp.arange(half, dtype=jnp.float32) * 2.0 / rot)
    ang = pos.astype(jnp.float32)[:, None] * inv[None, :]
    cos = jnp.cos(ang)[None, :, None, :]
    sin = jnp.sin(ang)[None, :, None, :]
    xr = x[..., :rot].astype(jnp.float32)
    x1, x2 = xr[..., :half], xr[..., half:]
    out = jnp.concatenate([x1 * cos - x2 * sin, x2 * cos + x1 * sin], axis=-1).astype(x.dtype)
    return jnp.concatenate([out, x[..., rot:]], axis=-1)

def causal_dwconv(u, ctx, w, b=None):
    ext = jnp.concatenate([ctx.astype(u.dtype), u], axis=1)
    y = lax.conv_general_dilated(ext, w[:, None, :].astype(u.dtype), window_strides=(1,), padding='VALID',
                                 dimension_numbers=('NWC', 'WIO', 'NWC'), feature_group_count=u.shape[-1])
    if b is not None:
        y = y + b.astype(u.dtype)
    return y, ext[:, ext.shape[1] - (w.shape[0] - 1):]

def select_keys(qi, wi, ki, qpos, topk):
    s = jnp.einsum('bqhd,bsd->bqhs', qi.astype(jnp.float32), ki.astype(jnp.float32)) * IDX_DIM ** -0.5
    score = jnp.einsum('bqhs,bqh->bqs', jax.nn.relu(s), wi.astype(jnp.float32) * N_IDX_HEADS ** -0.5)
    kpos = jnp.arange(ki.shape[1])
    score = jnp.where(kpos[None, None, :] <= qpos[None, :, None], score, -jnp.inf)
    _, idx = lax.top_k(score, topk)
    return idx, idx <= qpos[None, :, None]

def attend(q, kg, vg, valid):
    logits = jnp.einsum('bqhd,bqkhd->bqhk', q.astype(jnp.float32), kg.astype(jnp.float32)) * HEAD_DIM ** -0.5
    logits = jnp.where(valid[:, :, None, :], logits, -jnp.inf)
    p = jax.nn.softmax(logits, axis=-1)
    return jnp.einsum('bqhk,bqkhd->bqhd', p, vg.astype(jnp.float32)).astype(q.dtype)

def dsa_prompt(q, k, v, qi, ki, wi):
    bsz, s_len = q.shape[:2]
    topk = min(TOPK_MAX, s_len // 4)
    nb = s_len // Q_BLOCK
    bidx = jnp.arange(bsz)[:, None, None]

    def block(args):
        i, qb, qib, wib = args
        qpos = i * Q_BLOCK + jnp.arange(Q_BLOCK)
        idx, valid = select_keys(qib, wib, ki, qpos, topk)
        return attend(qb, k[bidx, idx], v[bidx, idx], valid)

    split = lambda t: jnp.swapaxes(t.reshape(bsz, nb, Q_BLOCK, *t.shape[2:]), 0, 1)
    out = lax.map(block, (jnp.arange(nb), split(q), split(qi), split(wi)))
    return jnp.swapaxes(out, 0, 1).reshape(bsz, s_len, A_W)

def dsa_sample(q, k, v, qi, ki, wi, ck, cv, cki, page_table):
    n_dec, t_dec = q.shape[:2]
    past = page_table.shape[1] * PAGE_SIZE
    ki_all = jnp.concatenate([cki[page_table].reshape(n_dec, past, IDX_DIM), ki], axis=1)
    topk = min(TOPK_MAX, (past + t_dec) // 4)
    qpos = past + jnp.arange(t_dec)
    idx, valid = select_keys(qi, wi, ki_all, qpos, topk)
    bidx = jnp.arange(n_dec)[:, None, None]
    pidx = jnp.minimum(idx, past - 1)
    phys = page_table[bidx, pidx // PAGE_SIZE]
    off = pidx % PAGE_SIZE
    nidx = jnp.clip(idx - past, 0, t_dec - 1)
    is_past = (idx < past)[..., None, None]
    kg = jnp.where(is_past, ck[phys, off].astype(k.dtype), k[bidx, nidx])
    vg = jnp.where(is_past, cv[phys, off].astype(v.dtype), v[bidx, nidx])
    return attend(q, kg, vg, valid).reshape(n_dec, t_dec, A_W)

def ssd_chunked(x, dt, a, bm, cm, h0, chunk):
    bsz, s_len, n_h, p_dim = x.shape
    rep = n_h // bm.shape[2]
    bh = jnp.repeat(bm, rep, axis=2)
    ch = jnp.repeat(cm, rep, axis=2)
    nc = s_len // chunk
    blk = lambda t: jnp.moveaxis(t.reshape(bsz, nc, chunk, *t.shape[2:]), 1, 0)
    causal = jnp.tril(jnp.ones((chunk, chunk), bool))[None, :, :, None]

    def step(h, inp):
        xc, dtc, bc, cc = inp
        cs = jnp.cumsum(dtc * a, axis=1)
        seg = cs[:, :, None, :] - cs[:, None, :, :]
        decay = jnp.where(causal, jnp.exp(jnp.where(causal, seg, 0.0)), 0.0)
        cb = jnp.einsum('bthn,bshn->btsh', cc, bc)
        y = jnp.einsum('btsh,bshp->bthp', cb * decay * dtc[:, None], xc)
        y = y + jnp.einsum('bthn,bhpn->bthp', cc, h) * jnp.exp(cs)[..., None]
        w_end = jnp.exp(cs[:, -1:] - cs) * dtc
        h = h * jnp.exp(cs[:, -1])[:, :, None, None] + jnp.einsum('bsh,bshn,bshp->bhpn', w_end, bc, xc)
        return h, y

    h, ys = lax.scan(step, h0.astype(jnp.float32), (blk(x), blk(dt), blk(bh), blk(ch)))
    return jnp.moveaxis(ys, 0, 1).reshape(bsz, s_len, n_h, p_dim), h

def layer(x, pos, attn_fn, ctx_b, ctx_c, ctx_d, h0, p):
    bsz, s_len, _ = x.shape
    f32 = jnp.float32
    u = rms_norm(x, p['g_pre_mix'])
    cuts = [int(c) for c in np.cumsum(IN_SIZES)[:-1]]
    (q, k, v, qi, ki, wi, bx, gb, gc, glu, zg, xbc, dt) = jnp.split(u @ p['w_in'], cuts, axis=-1)
    heads = lambda t, n: t.reshape(bsz, s_len, n, -1)
    q = rope(heads(q, N_HEADS_A), pos)
    k = rope(heads(k, N_KV_HEADS), pos)
    v = heads(v, N_KV_HEADS)
    qi = rope(heads(qi, N_IDX_HEADS), pos)
    ki = rope(ki[:, :, None, :], pos)[:, :, 0]
    y_a = attn_fn(q, k, v, qi, ki, wi)
    conv_b, new_b = causal_dwconv(gc * bx, ctx_b, p['bconv_w'])
    y_b = gb * conv_b
    ga, gg = jnp.split(glu, 2, axis=-1)
    conv_c, new_c = causal_dwconv(ga * jax.nn.sigmoid(gg), ctx_c, p['cconv_w'], p['cconv_b'])
    y_c = jax.nn.silu(layer_norm(conv_c, p['cln_g'], p['cln_b']))
    conv_d, new_d = causal_dwconv(xbc, ctx_d, p['dconv_w'], p['dconv_b'])
    xs, bm, cm = jnp.split(jax.nn.silu(conv_d).astype(f32), [D_W, D_W + D_GROUPS * D_STATE], axis=-1)
    dtv = jax.nn.softplus(dt.astype(f32) + p['dt_bias'].astype(f32))
    a = -jnp.exp(p['a_log'].astype(f32))
    chunk = SSD_CHUNK if s_len % SSD_CHUNK == 0 else s_len
    xs4 = xs.reshape(bsz, s_len, D_HEADS, D_HEAD_DIM)
    ys, h_new = ssd_chunked(xs4, dtv, a, bm.reshape(bsz, s_len, D_GROUPS, D_STATE),
                            cm.reshape(bsz, s_len, D_GROUPS, D_STATE), h0, chunk)
    ys = (ys + p['d_skip'].astype(f32)[:, None] * xs4).reshape(bsz, s_len, D_W)
    yg = ys * jax.nn.silu(zg.astype(f32))
    y_d = (yg * lax.rsqrt(jnp.mean(yg * yg, axis=-1, keepdims=True) + RMS_EPS) * p['d_norm'].astype(f32)).astype(x.dtype)
    mix = jnp.concatenate([y_a, y_b, y_c, y_d], axis=-1) @ p['w_out']
    x = x + rms_norm(mix, p['g_post_mix'])
    hf = rms_norm(x, p['g_pre_ffn'])
    f = (jax.nn.silu(hf @ p['ffn_gate']) * (hf @ p['ffn_up'])) @ p['ffn_down']
    x = x + rms_norm(f, p['g_post_ffn'])
    return x, (k, v, ki, new_b, new_c, new_d, h_new.astype(x.dtype))

def setup_inputs(seed: int = 0) -> dict:
    key = jax.random.key(seed)
    ks = iter(jax.random.split(key, 40))
    nrm = lambda shape, scale: jax.random.normal(next(ks), shape, jnp.float32) * scale
    n_pages = PAST_LEN // PAGE_SIZE
    used = DEC_BATCH * n_pages
    n_phys = used + max(1, used // 4)
    page_table = jax.random.permutation(next(ks), n_phys)[:used].reshape(DEC_BATCH, n_pages).astype(jnp.int32)
    dt0 = jnp.exp(jax.random.uniform(next(ks), (DEPTH, D_HEADS), jnp.float32, math.log(1e-3), math.log(1e-1)))
    a_log = jnp.log(jax.random.uniform(next(ks), (DEPTH, D_HEADS), jnp.float32, 1.0, 16.0))
    return {
        'x_prompt': nrm((BATCH, SEQ, D_MODEL), 1.0),
        'x_sample': nrm((DEC_BATCH, DEC_SEQ, D_MODEL), 1.0),
        'cache_k': nrm((DEPTH, n_phys, PAGE_SIZE, N_KV_HEADS, HEAD_DIM), 1.0),
        'cache_v': nrm((DEPTH, n_phys, PAGE_SIZE, N_KV_HEADS, HEAD_DIM), 1.0),
        'cache_kidx': nrm((DEPTH, n_phys, PAGE_SIZE, IDX_DIM), 1.0),
        'page_table': page_table,
        'state_bconv': nrm((DEPTH, DEC_BATCH, B_CONV - 1, B_W), 1.0),
        'state_cconv': nrm((DEPTH, DEC_BATCH, C_CONV - 1, C_W), 0.5),
        'state_dconv': nrm((DEPTH, DEC_BATCH, D_CONV - 1, D_XBC), 1.0),
        'state_ssm': nrm((DEPTH, DEC_BATCH, D_HEADS, D_HEAD_DIM, D_STATE), 0.1),
        'w_in': nrm((DEPTH, D_MODEL, IN_W), D_MODEL ** -0.5),
        'w_out': nrm((DEPTH, MIX_W, D_MODEL), MIX_W ** -0.5),
        'g_pre_mix': 1.0 + nrm((DEPTH, D_MODEL), 0.02),
        'g_post_mix': 1.0 + nrm((DEPTH, D_MODEL), 0.02),
        'g_pre_ffn': 1.0 + nrm((DEPTH, D_MODEL), 0.02),
        'g_post_ffn': 1.0 + nrm((DEPTH, D_MODEL), 0.02),
        'bconv_w': nrm((DEPTH, B_CONV, B_W), B_CONV ** -0.5),
        'cconv_w': nrm((DEPTH, C_CONV, C_W), C_CONV ** -0.5),
        'cconv_b': nrm((DEPTH, C_W), 0.02),
        'cln_g': 1.0 + nrm((DEPTH, C_W), 0.02),
        'cln_b': nrm((DEPTH, C_W), 0.02),
        'dconv_w': nrm((DEPTH, D_CONV, D_XBC), D_CONV ** -0.5),
        'dconv_b': nrm((DEPTH, D_XBC), 0.02),
        'dt_bias': dt0 + jnp.log(-jnp.expm1(-dt0)),
        'a_log': a_log,
        'd_skip': 1.0 + nrm((DEPTH, D_HEADS), 0.1),
        'd_norm': 1.0 + nrm((DEPTH, D_W), 0.02),
        'ffn_gate': nrm((DEPTH, D_MODEL, D_FF), D_MODEL ** -0.5),
        'ffn_up': nrm((DEPTH, D_MODEL, D_FF), D_MODEL ** -0.5),
        'ffn_down': nrm((DEPTH, D_FF, D_MODEL), D_FF ** -0.5),
    }

def reference(x_prompt, x_sample, cache_k, cache_v, cache_kidx, page_table, state_bconv, state_cconv, state_dconv,
              state_ssm, w_in, w_out, g_pre_mix, g_post_mix, g_pre_ffn, g_post_ffn, bconv_w, cconv_w, cconv_b,
              cln_g, cln_b, dconv_w, dconv_b, dt_bias, a_log, d_skip, d_norm, ffn_gate, ffn_up, ffn_down):
    n_prompt, seq = x_prompt.shape[:2]
    t_dec = x_sample.shape[1]
    past = page_table.shape[1] * PAGE_SIZE
    pos_p = jnp.arange(seq, dtype=jnp.int32)
    pos_s = past + jnp.arange(t_dec, dtype=jnp.int32)
    dtype = x_prompt.dtype
    zb = jnp.zeros((n_prompt, B_CONV - 1, B_W), dtype)
    zc = jnp.zeros((n_prompt, C_CONV - 1, C_W), dtype)
    zd = jnp.zeros((n_prompt, D_CONV - 1, D_XBC), dtype)
    zh = jnp.zeros((n_prompt, D_HEADS, D_HEAD_DIM, D_STATE), jnp.float32)
    hp, hs = x_prompt, x_sample
    outs_p = [[] for _ in range(7)]
    outs_s = [[] for _ in range(7)]
    for l in range(DEPTH):
        p = {'w_in': w_in[l], 'w_out': w_out[l], 'g_pre_mix': g_pre_mix[l], 'g_post_mix': g_post_mix[l],
             'g_pre_ffn': g_pre_ffn[l], 'g_post_ffn': g_post_ffn[l], 'bconv_w': bconv_w[l], 'cconv_w': cconv_w[l],
             'cconv_b': cconv_b[l], 'cln_g': cln_g[l], 'cln_b': cln_b[l], 'dconv_w': dconv_w[l],
             'dconv_b': dconv_b[l], 'dt_bias': dt_bias[l], 'a_log': a_log[l], 'd_skip': d_skip[l],
             'd_norm': d_norm[l], 'ffn_gate': ffn_gate[l], 'ffn_up': ffn_up[l], 'ffn_down': ffn_down[l]}
        hp, st_p = layer(hp, pos_p, dsa_prompt, zb, zc, zd, zh, p)
        attn_s = functools.partial(dsa_sample, ck=cache_k[l], cv=cache_v[l], cki=cache_kidx[l], page_table=page_table)
        hs, st_s = layer(hs, pos_s, attn_s, state_bconv[l], state_cconv[l], state_dconv[l], state_ssm[l], p)
        for lst, arr in zip(outs_p, st_p):
            lst.append(arr)
        for lst, arr in zip(outs_s, st_s):
            lst.append(arr)
    k_p, v_p, kidx_p, bconv_p, cconv_p, dconv_p, ssm_p = [jnp.stack(a) for a in outs_p]
    k_s, v_s, kidx_s, bconv_s, cconv_s, dconv_s, ssm_s = [jnp.stack(a) for a in outs_s]
    return (hp, hs, k_p, v_p, kidx_p, k_s, v_s, kidx_s, bconv_p, bconv_s, cconv_p, cconv_s, dconv_p, dconv_s, ssm_p, ssm_s)


_drawn_inputs = setup_inputs


def setup_inputs(seed=0):
    import zlib

    import numpy as np

    out = dict(_drawn_inputs(seed))
    spreads = {}
    factors = {'g_post_ffn': 2.853, 'cconv_b': 2.714, 'cln_g': 4.345, 'cln_b': 4.471, 'd_norm': 3.316}
    for name, (base, spread) in spreads.items():
        noise = np.random.default_rng([zlib.crc32(name.encode()), seed]).standard_normal(out[name].shape)
        drawn = base * np.exp(spread * noise) if base else spread * noise
        out[name] = __import__('jax').numpy.asarray(drawn.astype(out[name].dtype))
    for name, factor in factors.items():
        out[name] = (out[name] * factor).astype(out[name].dtype)
    return out
```

```python
from contextlib import ExitStack

import numpy as np
import concourse.bass as bass
from concourse import mybir

F32 = mybir.dt.float32
I32 = mybir.dt.int32
ALU = mybir.AluOpType
ACT = mybir.ActivationFunctionType
AX = mybir.AxisListType

P = 128
D_MODEL, SEQ, DEPTH, NS, PAST, PAGE = 1024, 512, 2, 8, 256, 128
HEADS, HD, IH, ID = 4, 64, 8, 32
TOPK_PROMPT, TOPK_SAMPLE = 128, 64
THETA = 500000.0
B_CONV, C_CONV, D_CONV = 3, 31, 4
D_FF = 2816
N_STATE = 128
W = 256
T = SEQ + NS
HALF = T // 2
KC = D_MODEL // P
FFC = D_FF // P
QT = SEQ // P
TOK_W = 4 * W + ID + IH
FEAT0 = TOK_W
DT0 = FEAT0 + 9 * W
RMS_EPS, LN_EPS = 1e-6, 1e-5
MASKED = -1e30
TAKEN = -3e38
SLOTS = 4
SLAB = KC * W

ROWS_A = [("g_pre_mix", 8), ("g_post_mix", 8), ("g_pre_ffn", 8), ("g_post_ffn", 8), ("bconv_w", 6),
          ("cconv_w", 62), ("cconv_b", 2), ("cln_g", 2), ("cln_b", 2), ("d_norm", 2)]
ROWS_B = [("dconv_w", 24), ("dconv_b", 6)]
AT = {}
for _rows, _base in ((ROWS_A, 0), (ROWS_B, sum(n for _, n in ROWS_A))):
    for _name, _n in _rows:
        AT[_name] = _base
        _base += _n
NA_ROWS, NB_ROWS = sum(n for _, n in ROWS_A), sum(n for _, n in ROWS_B)

CONST = {}
_at = 0
for _name, _n in (("ident", 128), ("ones", 128), ("later", 128), ("future", 128), ("head_of_row", 4),
                  ("sample_of_row", 8), ("cos", 64), ("nsin", 32), ("sin", 32), ("cos_i", 32),
                  ("nsin_i", 16), ("sin_i", 16), ("cos_d", 16), ("nsin_d", 8), ("sin_d", 8),
                  ("cos_id", 8), ("nsin_id", 4), ("sin_id", 4), ("eps", 2),
                  ("rows_of_sample", 32), ("state_rows", 256)):
    CONST[_name] = (_at, _n)
    _at += _n
N_CONST = _at


def shape_constants():
    c = np.zeros((P, N_CONST), np.float32)

    def put(name, v):
        a, n = CONST[name]
        c[:, a:a + n] = np.asarray(v, np.float32).reshape(P, n)

    i = np.arange(P)
    put("ident", np.eye(P))
    put("ones", np.ones((P, P)))
    put("later", np.where(i[:, None] > i[None, :], MASKED, 0.0))
    put("future", np.where(i[None, :] > i[:, None], MASKED, 0.0))
    put("head_of_row", i[:, None] % HEADS == np.arange(HEADS)[None])
    put("sample_of_row", i[:, None] // HEADS == np.arange(NS)[None])
    put("rows_of_sample", np.arange(32)[None, :] // HEADS == i[:, None])
    put("state_rows", np.arange(2 * P)[None, :] // HD == i[:, None])
    for rot, tail in ((HD // 4, ""), (ID // 4, "_i")):
        half = rot // 2
        inv = np.float32(THETA) ** (-np.arange(half, dtype=np.float32) * np.float32(2.0) / np.float32(rot))
        for pos, d in ((np.arange(SEQ).reshape(QT, P).T, ""), (np.full((P, 1), PAST), "d")):
            ang = pos.astype(np.float32)[:, :, None] * inv
            name = (tail + d) if tail else ("_" + d if d else "")
            put("cos" + name, np.concatenate([np.cos(ang)] * 2, -1))
            put("nsin" + name, -np.sin(ang))
            put("sin" + name, np.sin(ang))
    a, _ = CONST["eps"]
    c[:, a], c[:, a + 1] = RMS_EPS, LN_EPS
    return c


def hybrid_decoder(nc, d, out):
    (y_prompt, y_sample, k_prompt, v_prompt, kidx_prompt, k_sample, v_sample, kidx_sample, bconv_prompt,
     bconv_sample, cconv_prompt, cconv_sample, dconv_prompt, dconv_sample, ssm_prompt, ssm_sample) = out
    ctx = ExitStack()

    def sb(name, shape, dt=F32):
        return ctx.enter_context(nc.sbuf_tensor(name, shape, dt))

    sems = []

    def sem(name):
        sems.append(ctx.enter_context(nc.semaphore(name)))
        return sems[-1]

    with ctx:
        cst = sb("cst", [P, N_CONST])
        x = sb("x", [P, KC, T])
        u = sb("u", [P, KC, T])
        ring = sb("ring", [P, SLOTS, SLAB])
        hid = sb("hid", [P, FFC * T])
        par = sb("par", [P, NA_ROWS + NB_ROWS])
        small = sb("small", [P, 64])
        pages = sb("pages", [1, 2 * NS], I32)
        tok8 = sb("tok8", [NS, TOK_W])
        ya = sb("ya", [P, 2, T])
        ctx_b = sb("ctx_b", [P, 2, NS, B_CONV])
        ctx_c = sb("ctx_c", [P, 2, NS, C_CONV])
        ctx_d = sb("ctx_d", [P, 6, NS, D_CONV])
        root = sb("root", [P, T])
        rstd = sb("rstd", [P, T])
        csdt = sb("csdt", [64, T])
        arena = sb("arena", [P, 11424])
        side = sb("side", [P, 7200])
        PS = ctx.enter_context(nc.psum_tensor("PS", [P, 8, 512], F32))

        def view(t, at, *dims):
            n = int(np.prod(dims))
            v = t[:, at:at + n]
            names = "abcd"[:len(dims)]
            if len(dims) == 1:
                return v
            return v.rearrange(f"p ({' '.join(names)}) -> p {' '.join(names)}",
                               **{k: m for k, m in zip(names[:-1], dims[:-1])})

        def const(name):
            a, n = CONST[name]
            return cst[:, a:a + n]

        def pcol(name, i):
            return par[:, AT[name] + i:AT[name] + i + 1]

        ident, ones = const("ident"), const("ones")
        feat = view(hid, 0, 18, T)
        BX, GB, GC, GA, GG, ZG, XBC = 0, 2, 4, 6, 8, 10, 12
        v_cache = view(hid, 0, 2 * NS, W)
        ssm = view(hid, 18 * T, 2 * NS, N_STATE)
        hidden = view(hid, 0, FFC, T)

        tok_k, tok_v, tok_q = view(arena, 0, QT, W), view(arena, 1024, QT, W), view(arena, 2048, QT, W)
        kiw = view(arena, 3072, QT, ID + IH)
        ki_four = view(arena, 3232, QT, 4, ID)
        turned = view(arena, 3744, 7, SEQ)
        score = view(arena, 7328, 3, SEQ)
        tok_qi = view(arena, 8864, QT, W)
        rect = view(arena, 8864, 2, SEQ)
        prob_t = view(arena, 9888, 2, SEQ)
        rope_a, rope_b = view(arena, 10912, 256), view(arena, 11168, 256)
        squares = view(arena, 3744, KC, T)
        rows_a, rows_b = view(arena, 7904, P), view(arena, 8032, P)
        rows_cc, rows_cb, rows_cd = view(arena, 8160, 2, W), view(arena, 8672, W), view(arena, 8928, 3 * W)
        h_t = view(arena, 2048, HEADS, HD)
        read_c = view(arena, 0, HEADS, SEQ)
        decay = view(arena, 3744, 4 * QT, P)
        ecs = view(arena, 5792, HEADS, SEQ)
        xb_tok = view(arena, 7840, QT, 2 * W)
        xw = view(arena, 9888, QT, W)
        hid_gate = view(arena, 0, 2, T)

        k_cache = view(side, 0, 2 * NS, W)
        dc = view(side, 0, 6, T)
        t4 = side[:, 3120:3120 + T]
        temp = view(side, 4096, 4, T)
        ki_cache = view(side, 6176, 2 * NS, ID)
        prod_i = view(side, 6688, 512)
        tails = u[:, 5:8, :].rearrange("p k t -> p (k t)")
        tail_b, tail_c, tail_d = tails[:, 0:256], tails[:, 256:512], tails[:, 512:1280]
        ssm_rows = view(arena, 2304, 2, N_STATE)
        out_rows = view(arena, 0, 8, 1024)
        past_s = view(side, 4096, 2, NS)
        past_l = view(side, 4112, 2, NS, HEADS)
        s_row = side[:, 4176:4176 + 257]
        m_row = side[:, 4433:4433 + 261]
        l_row = side[:, 4694:4694 + 257]
        p_row = side[:, 4951:4951 + 257]
        p_col = view(side, 5208, 2, 32)
        self_p, self_pt = side[:, 5272:5280], side[:, 5280:5312]
        sc64, prod8 = side[:, 5312:5376], side[:, 5376:5632]
        best8 = side[:, 5632:5640]
        stat8 = side[:, 5640:5656]
        chunk_best = view(side, 3900, 3, 8)
        pool_tmp = [arena[:, 10912:11424], sb("pool_tmp", [P, SEQ])[:, :]]
        cst_tok = small[:, 0:16]
        dt_tok = small[:, 16:32]
        w_end = small[:, 32:48]
        neg_max, denom, rden, top_max = small[:, 48:50], small[:, 50:52], small[:, 52:54], small[:, 54:56]
        dsk = small[:, 56:58]
        a_neg, dt_bias, d_skip4, a_log4 = small[0:36, 58:59], small[0:36, 59:60], small[0:36, 60:61], small[0:36, 61:62]
        edt = view(side, 3640, 2, 2, NS)
        dtx = view(side, 3680, 2, NS)
        y_dec = view(side, 3700, 2, NS)
        bc_rows = side[0:NS, 6176:6176 + 512]
        prod_n = side[:, 6688:6688 + 128]
        prod_n2 = side[:, 6816:6816 + 128]

        def pair(i):
            return PS[:, 2 * i:2 * i + 2, 0:HALF]

        def bank(i):
            return PS[:, i, :]

        def halves(ap):
            return ap.rearrange("p (h n) -> p h n", h=2)

        def row(t, l):
            return t[bass.ds(l, 1)]

        const_in, rows_in, sample_in = sem("const_in"), sem("rows_in"), sem("sample_in")
        x_turned, x_copied, x8_turned = sem("x_turned"), sem("x_copied"), sem("x8_turned")
        x_rows = view(arena, 0, QT, D_MODEL)
        x8 = side[0:NS, 0:D_MODEL]
        with nc.Block() as block:
            @block.sync
            def _(sp):
                sp.dma_start(cst[:, :], d["constants"]).then_inc(const_in, 16)
                for t in range(QT):
                    sp.dma_start(x_rows[:, t, :], d["x_prompt"][0, t * P:(t + 1) * P, :]).then_inc(rows_in, 16)
                sp.dma_start(x8, d["x_sample"].rearrange("b s f -> (b s) f")).then_inc(sample_in, 16)
                sp.dma_start(pages[:, :], d["page_table"].rearrange("(o b) g -> o (b g)", o=1)).then_inc(sample_in, 16)
                sp.wait_ge(sample_in, 32)

            @block.tensor
            def _(pe):
                pe.wait_ge(const_in, 16)
                pe.wait_ge(rows_in, 16 * QT)
                for c in range(KC):
                    for t in range(QT):
                        last = pe.transpose(bank(c)[:, t * P:(t + 1) * P], x_rows[:, t, c * P:(c + 1) * P], ident)
                    last.then_inc(x_turned, 1)
                pe.wait_ge(sample_in, 32)
                pe.wait_ge(x_copied, 1)
                for c in range(KC):
                    last = pe.transpose(bank(0)[:, c * NS:(c + 1) * NS], x8[:, c * P:(c + 1) * P], ident[0:NS, 0:NS])
                last.then_inc(x8_turned, 1)

            @block.vector
            def _(dve):
                for c in range(KC):
                    dve.wait_ge(x_turned, c + 1)
                    dve.tensor_copy(x[:, c, 0:SEQ], bank(c)).then_inc(x_copied, 1)
                dve.wait_ge(x8_turned, 1)
                dve.tensor_copy(x[:, :, SEQ:T], view(PS[:, 0, :], 0, KC, NS)).then_inc(x_copied, 1)
                dve.wait_ge(x_copied, KC + 1)

        nc.all_engine_barrier()

        kv_stored, stored, state_copied = sem("kv_stored"), sem("stored"), sem("state_copied")
        tails_stored, ssm_in = sem("tails_stored"), sem("ssm_in")
        N_KV, N_STATES, N_TAILS, N_SSM = 6, 3, 6, 2

        first_layer_sem = len(sems)
        params_in, scalars_in, states_in = sem("params_in"), sem("scalars_in"), sem("states_in")
        k_cache_in, v_cache_in, ki_cache_in = sem("k_cache_in"), sem("v_cache_in"), sem("ki_cache_in")
        slab_in = [sem(f"slab_in{i}") for i in range(SLOTS)]
        params_turned, params_ready = sem("params_turned"), sem("params_ready")
        states_turned, states_ready = sem("states_turned"), sem("states_ready")
        squares_ready, sums_ready, root_ready = sem("squares_ready"), sem("sums_ready"), sem("root_ready")
        normed, x_updated = sem("normed"), sem("x_updated")
        tok_summed, tok_ready = sem("tok_summed"), sem("tok_ready")
        rope_done, turn_done, turned_ready = sem("rope_done"), sem("turn_done"), sem("turned_ready")
        rows_spread, rows_used = sem("rows_spread"), sem("rows_used")
        feat_summed, feat_ready = sem("feat_summed"), sem("feat_ready")
        dec_pe, dec_dve, dec_max, dec_exp, dec_out = (sem("dec_pe"), sem("dec_dve"), sem("dec_max"), sem("dec_exp"),
                                                      sem("dec_out"))
        idx_summed, idx_rect, idx_added, chosen = sem("idx_summed"), sem("idx_rect"), sem("idx_added"), sem("chosen")
        logits_summed, logits_masked, exp_done, prob_ready = (sem("logits_summed"), sem("logits_masked"),
                                                              sem("exp_done"), sem("prob_ready"))
        prob_turned, prob_t_ready, mixed, mixed_out = (sem("prob_turned"), sem("prob_t_ready"), sem("mixed"),
                                                       sem("mixed_out"))
        vec, pool_step, conv_c_done, conv_c_started = sem("vec"), sem("pool_step"), sem("conv_c_done"), sem("conv_c_started")
        conv_d_done, conv_d_act, segments, dec_rows = (sem("conv_d_done"), sem("conv_d_act"), sem("segments"),
                                                       sem("dec_rows"))
        dt_pe, dt_exp, dt_low, dt_dve = sem("dt_pe"), sem("dt_exp"), sem("dt_low"), sem("dt_dve")
        ssd_pe, ssd_act, ssd_dve = sem("ssd_pe"), sem("ssd_act"), sem("ssd_dve")
        state_pe, state_dve = sem("state_pe"), sem("state_dve")
        decd_pe, decd_dve, decd_act = sem("decd_pe"), sem("decd_dve"), sem("decd_act")
        glu_act, gate_in, tails_turned, tails_ready = (sem("glu_act"), sem("gate_in"), sem("tails_turned"),
                                                       sem("tails_ready"))
        ssm_done = sem("ssm_done")
        cln_pe, cln_act, cln_dve = sem("cln_pe"), sem("cln_act"), sem("cln_dve")
        dn_pe, dn_act, dn_dve = sem("dn_pe"), sem("dn_act"), sem("dn_dve")
        b_done = sem("b_done")
        out_summed, out_ready = sem("out_summed"), sem("out_ready")
        gate_summed, up_summed, gate_ready, hidden_ready = (sem("gate_summed"), sem("up_summed"),
                                                            sem("gate_ready"), sem("hidden_ready"))
        down_summed, down_ready = sem("down_summed"), sem("down_ready")
        last_layer_sem = len(sems)

        FEAT_SLABS = [6, 7, 8, "dt", 4, 5, 3, 2, 0, 1]
        N_TOK, N_FEAT = 5, len(FEAT_SLABS)
        OUT0 = N_TOK + N_FEAT
        GU0 = OUT0 + 4
        DN0 = GU0 + 22
        GU_TURNS, DN_TURNS = 5, 4
        feat_tiles = []
        for n, s in enumerate(FEAT_SLABS):
            for c in ([None] if s == "dt" else [0, 1]):
                feat_tiles.append((n, s, c))
        FEAT_AT = {(s, c): i for i, (n, s, c) in enumerate(feat_tiles)}

        def feat_count(*chunks):
            return 1 + max(FEAT_AT[(c // 2, c % 2)] for c in chunks)

        DT_COUNT = 1 + FEAT_AT[("dt", None)]
        STEPS = [(blk, h) for blk in range(QT) for h in range(HEADS)]
        IDX = [(blk, h) for blk in range(1, QT) for h in range(IH)]

        with nc.Fori(0, DEPTH) as layer:
            with nc.Block() as block:

                @block.sync
                def _(sp):
                    l = layer

                    def used_up(n):
                        if n < N_TOK:
                            return tok_summed, (QT + 1) * (n + 1)
                        if n < OUT0:
                            return feat_summed, sum(1 for m, _, _ in feat_tiles if m <= n - N_TOK)
                        if n < GU0:
                            return out_summed, 2 * (n - OUT0 + 1)
                        return up_summed, 2 * ((n - GU0) // 2 + 1)

                    def slab(n, dst_w, src):
                        if n >= SLOTS:
                            sp.wait_ge(*used_up(n - SLOTS))
                        sp.dma_start(view(ring[:, n % SLOTS, :], 0, KC, W)[:, :, 0:dst_w], src)\
                          .then_inc(slab_in[n % SLOTS], 16)

                    def cols(name, a, w):
                        return row(d[name], l).rearrange("o (k p) n -> p (o k) n", p=P)[:, :, a:a + w]

                    for rows, tile in ((ROWS_A, rows_a), (ROWS_B, rows_b)):
                        at = 0
                        for name, n in rows:
                            src = row(d[name], l)
                            src = src.rearrange("o (c p) -> (o c) p", p=P) if src.ndim == 2 else \
                                src.rearrange("o t (c p) -> (o t c) p", p=P)
                            sp.dma_start(tile[at:at + n, :], src).then_inc(params_in, 16)
                            at += n
                    for n in range(2):
                        slab(n, W, cols("w_in", n * W, W))
                    per = 4 * (C_CONV - 1)
                    for half in range(2):
                        sp.dma_start(rows_cc[0:per, half, :], row(d["state_cconv"], l)[:, 4 * half:4 * half + 4]
                                     .rearrange("o b t c -> (o b t) c")).then_inc(states_in, 16)
                    sp.dma_start(rows_cb[0:2 * NS, :], row(d["state_bconv"], l)
                                 .rearrange("o b t c -> (o b t) c")).then_inc(states_in, 16)
                    sp.dma_start(rows_cd[0:3 * NS, :], row(d["state_dconv"], l)
                                 .rearrange("o b t c -> (o b t) c")).then_inc(states_in, 16)
                    for name, dst in (("dt_bias", dt_bias), ("d_skip", d_skip4), ("a_log", a_log4)):
                        sp.dma_start(dst[0:HEADS, :], row(d[name], l).rearrange("o h -> h o")).then_inc(scalars_in, 16)
                    for n in range(2, 4):
                        slab(n, W, cols("w_in", n * W, W))
                    for i in range(2 * NS):
                        page = sp.value_load(pages[0:1, i:i + 1], min_val=0, max_val=d["cache_k"].shape[1] - 1)
                        for name, dst, s in (("cache_kidx", ki_cache, ki_cache_in), ("cache_k", k_cache, k_cache_in),
                                             ("cache_v", v_cache, v_cache_in)):
                            src = row(d[name], l)[:, bass.ds(page, 1)]
                            src = src.rearrange("o g r c -> r (o g c)") if src.ndim == 4 else \
                                src.rearrange("o g r h c -> r (o g h c)")
                            sp.dma_start(dst[:, i, :], src).then_inc(s, 16)
                    slab(4, ID + IH, cols("w_in", 4 * W, ID + IH))
                    for i, s in enumerate(FEAT_SLABS):
                        if s == "dt":
                            slab(N_TOK + i, HEADS, cols("w_in", DT0, HEADS))
                        else:
                            slab(N_TOK + i, W, cols("w_in", FEAT0 + s * W, W))
                    for n in range(4):
                        slab(OUT0 + n, W, cols("w_out", n * W, W))

                    def ring_slot(n0, j):
                        return (n0 + j) % SLOTS

                    def gate_up(j, col):
                        src = row(d["ffn_up" if j % 2 else "ffn_gate"], l)\
                            .rearrange("o (k p) n -> p (o k) n", p=P)[:, :, bass.ds(col, W)]
                        slot = ring_slot(GU0, j)
                        sp.dma_start(view(ring[:, slot, :], 0, KC, W), src).then_inc(slab_in[slot], 16)

                    for j in range(4):
                        sp.wait_ge(*used_up(GU0 + j - SLOTS))
                        gate_up(j, (j // 2) * W)
                    with sp.Fori(1, GU_TURNS) as i:
                        for j in range(4):
                            sp.wait_ge(up_summed, i * 4 + (2 * (j // 2) - 2))
                            gate_up(j, i * (2 * W) + (j // 2) * W)
                    for j in range(2):
                        sp.wait_ge(*used_up(GU0 + 4 * GU_TURNS + j - SLOTS))
                        gate_up(j, GU_TURNS * 2 * W)

                    def down(j, col):
                        src = row(d["ffn_down"], l).rearrange("o (k p) n -> p (o k) n", p=P)[
                            :, (j % 2) * 11:(j % 2) * 11 + 11, bass.ds(col, P)]
                        slot = ring_slot(DN0, j)
                        sp.dma_start(view(ring[:, slot, :], 0, 11, P), src).then_inc(slab_in[slot], 16)

                    for j in range(4):
                        sp.wait_ge(*used_up(DN0 + j - SLOTS))
                        down(j, (j // 2) * P)
                    with sp.Fori(1, DN_TURNS) as i:
                        for j in range(4):
                            sp.wait_ge(down_summed, i * 2 + (j // 2 - 1))
                            down(j, i * (2 * P) + (j // 2) * P)

                @block.tensor
                def _(pe):
                    def slab_here(n):
                        pe.wait_ge(slab_in[n % SLOTS], 16 * (n // SLOTS + 1))
                        return view(ring[:, n % SLOTS, :], 0, KC, W)

                    pe.wait_ge(params_in, 16 * (len(ROWS_A) + len(ROWS_B)))
                    pe.transpose(bank(7)[:, 0:NA_ROWS], rows_a[0:NA_ROWS, :], ident[0:NA_ROWS, 0:NA_ROWS])
                    pe.transpose(bank(7)[:, NA_ROWS:NA_ROWS + NB_ROWS], rows_b[0:NB_ROWS, :],
                                 ident[0:NB_ROWS, 0:NB_ROWS]).then_inc(params_turned, 1)

                    def sum_squares(to, ready, first, each):
                        for k in range(KC):
                            pe.wait_ge(ready, first + each * (k + 1))
                            for h in range(2):
                                last = pe.matmul(to[:, h, :], ones, squares[:, k, h * HALF:(h + 1) * HALF],
                                                 start=(k == 0), stop=(k == KC - 1))
                        last.then_inc(sums_ready, 1)

                    sum_squares(pair(0), squares_ready, 0, 1)
                    pe.wait_ge(states_in, 64)
                    per = 4 * (C_CONV - 1)
                    for c in range(2):
                        for half in range(2):
                            at = (2 * c + half) * per
                            pe.transpose(bank(6)[:, at:at + per], rows_cc[0:per, half, c * P:(c + 1) * P],
                                         ident[0:per, 0:per])
                        pe.transpose(bank(5)[:, c * 16:(c + 1) * 16], rows_cb[0:16, c * P:(c + 1) * P], ident[0:16, 0:16])
                    for c in range(6):
                        last = pe.transpose(bank(5)[:, 32 + c * 24:32 + (c + 1) * 24], rows_cd[0:24, c * P:(c + 1) * P],
                                            ident[0:24, 0:24])
                    last.then_inc(states_turned, 1)

                    g = 0
                    pe.wait_ge(states_ready, 3)
                    pe.wait_ge(params_ready, 1)
                    for s in range(N_TOK):
                        w = W if s < 4 else ID + IH
                        wt = slab_here(s)
                        for t in range(QT + 1):
                            m = P if t < QT else NS
                            to = bank(2 + g % 6)[0:m, 0:w]
                            if g >= 6:
                                pe.wait_ge(tok_ready, g - 5)
                            for k in range(KC):
                                if s == 0 and t == 0:
                                    pe.wait_ge(normed, k + 1)
                                last = pe.matmul(to, u[:, k, t * P:t * P + m], wt[:, k, 0:w], start=(k == 0), stop=(k == KC - 1))
                            last.then_inc(tok_summed, 1)
                            g += 1

                    pe.wait_ge(tok_ready, g)
                    for j, (src, c, need) in enumerate(((tok_q, 0, 1), (tok_q, 1, 1), (tok_k, 0, 2), (tok_k, 1, 2),
                                                        (tok_qi, 0, 3), (tok_qi, 1, 3), (ki_four, 0, 4))):
                        pe.wait_ge(rope_done, need)
                        if j == 0:
                            pe.wait_ge(root_ready, 1)
                        flat = src.rearrange("p t a b -> p t (a b)") if src.ndim == 4 else src
                        for t in range(QT):
                            last = pe.transpose(bank(j)[:, t * P:(t + 1) * P], flat[:, t, c * P:(c + 1) * P], ident)
                        last.then_inc(turn_done, 1)

                    feat_i = [0]

                    def feature_tile():
                        i = feat_i[0]
                        n, s, c = feat_tiles[i]
                        wt = slab_here(N_TOK + n)
                        m, a = (HEADS, 0) if s == "dt" else (P, c * P)
                        if i >= 2:
                            pe.wait_ge(feat_ready, i - 1)
                        for k in range(KC):
                            for h in range(2):
                                last = pe.matmul(pair(i % 2)[0:m, h, :], wt[:, k, a:a + m],
                                                 u[:, k, h * HALF:(h + 1) * HALF], start=(k == 0), stop=(k == KC - 1))
                        last.then_inc(feat_summed, 1)
                        feat_i[0] += 1

                    def spread(b):
                        if b >= 2:
                            pe.wait_ge(rows_used, b - 1)
                        pick = ident[0:NS, b:b + 1].broadcast_to([NS, P])
                        pe.matmul(bank(4 + 2 * (b % 2))[:, 0:W], pick, tok8[:, 0:W], start=True, stop=True)
                        pe.matmul(bank(5 + 2 * (b % 2))[:, 0:TOK_W - 3 * W], pick, tok8[:, 3 * W:TOK_W],
                                  start=True, stop=True).then_inc(rows_spread, 1)

                    pe.wait_ge(turned_ready, 7)
                    pe.wait_ge(rope_done, 5)
                    for b in range(0, NS, 2):
                        spread(b)
                        spread(b + 1)
                        feature_tile()
                    pe.wait_ge(dec_dve, 1)
                    for pg in range(2):
                        pe.transpose(bank(4)[0:NS, pg * P:(pg + 1) * P], past_s[:, pg, :], ident)
                        last = pe.transpose(bank(5)[0:32, pg * P:(pg + 1) * P],
                                            past_l.rearrange("p g b h -> p g (b h)")[:, pg, :], ident)
                    last.then_inc(dec_pe, 1)
                    feature_tile()
                    feature_tile()
                    pe.wait_ge(dec_dve, 2)
                    pe.matmul(bank(6)[0:32, 0:261],
                              const("rows_of_sample")[0:NS, :],
                              m_row[0:NS, :], start=True, stop=True).then_inc(dec_pe, 1)
                    feature_tile()
                    pe.wait_ge(dec_dve, 3)
                    for pg in range(2):
                        pe.transpose(bank(7)[:, pg * 32:(pg + 1) * 32], p_row[0:32, pg * P:(pg + 1) * P], ident[0:32, 0:32])
                    pe.transpose(bank(7)[0:NS, 64:96], self_p[0:32, :], ident[0:32, 0:32]).then_inc(dec_pe, 1)
                    feature_tile()
                    pe.wait_ge(dec_dve, 4)
                    pe.wait_ge(v_cache_in, 16 * 2 * NS)
                    for hp in range(2):
                        pe.matmul(bank(4 + hp)[:, 0:32], tok8[:, 2 * W + hp * P:2 * W + (hp + 1) * P], self_pt[0:NS, :],
                                  start=True, stop=False, skip_group_check=True)
                        for b in range(NS):
                            for pg in range(2):
                                last = pe.matmul(bank(4 + hp)[:, 4 * b:4 * b + 4], v_cache[:, 2 * b + pg, hp * P:(hp + 1) * P],
                                                 p_col[:, pg, 4 * b:4 * b + 4], start=False,
                                                 stop=(b == NS - 1 and pg == 1), skip_group_check=True)
                    last.then_inc(dec_pe, 1)

                    pe.wait_ge(dec_out, 4)
                    for n, (blk, h) in enumerate(IDX):
                        keys = (blk + 1) * P
                        r = 32 * (h % 4)
                        if n >= 4:
                            pe.wait_ge(idx_rect, n - 3)
                        pe.matmul(bank(4 + n % 4)[:, 0:keys], turned[r:r + 32, 4 + h // 4, blk * P:(blk + 1) * P],
                                  turned[r:r + 32, 6, 0:keys], start=True, stop=True).then_inc(idx_summed, 1)
                    while feat_i[0] < len(feat_tiles):
                        feature_tile()

                    pe.wait_ge(idx_rect, len(IDX))
                    for j in range(len(STEPS) + 2):
                        if j < len(STEPS):
                            blk, h = STEPS[j]
                            r = HD * (h % 2)
                            if j >= 2:
                                pe.wait_ge(logits_masked, j - 1)
                            pe.matmul(bank(4 + j % 2)[:, 0:(blk + 1) * P],
                                      turned[r:r + HD, h // 2, blk * P:(blk + 1) * P],
                                      turned[r:r + HD, 2 + h // 2, 0:(blk + 1) * P],
                                      start=True, stop=True).then_inc(logits_summed, 1)
                        if 1 <= j <= len(STEPS):
                            i = j - 1
                            blk, h = STEPS[i]
                            pe.wait_ge(prob_ready, i + 1)
                            if i >= 1:
                                pe.wait_ge(prob_t_ready, i)
                            for kb in range(blk + 1):
                                last = pe.transpose(bank(6)[:, kb * P:(kb + 1) * P], rect[:, i % 2, kb * P:(kb + 1) * P], ident)
                            last.then_inc(prob_turned, 1)
                        if j >= 2:
                            i = j - 2
                            blk, h = STEPS[i]
                            r = HD * (h % 2)
                            pe.wait_ge(prob_t_ready, i + 1)
                            if h == 0 and blk >= 2:
                                pe.wait_ge(mixed_out, blk - 1)
                            at = (blk % 2) * W + (h // 2) * P
                            for kb in range(blk + 1):
                                last = pe.matmul(bank(7)[r:r + HD, at:at + P], tok_v[:, kb, h * HD:(h + 1) * HD],
                                                 prob_t[:, i % 2, kb * P:(kb + 1) * P], start=(kb == 0), stop=(kb == blk))
                            last.then_inc(mixed, 1)

                    pe.wait_ge(feat_ready, len(feat_tiles))
                    pe.wait_ge(mixed_out, QT)
                    pe.wait_ge(dt_dve, 1)
                    for c in range(QT):
                        last = pe.transpose(bank(6)[:, c * 64:c * 64 + 36], csdt[0:36, c * P:(c + 1) * P], ident[0:36, 0:36])
                    last.then_inc(dt_pe, 1)
                    for h in range(HEADS):
                        pe.matmul(bank(h), ident[0:HEADS, h:h + 1].broadcast_to([HEADS, P]), csdt[0:HEADS, 0:SEQ],
                                  start=True, stop=True).then_inc(dt_pe, 1)
                    for c in range(2):
                        pick = const("state_rows")[0:HEADS, c * P:(c + 1) * P]
                        for q, src in ((0, csdt), (1, t4)):
                            pe.matmul(bank(7)[:, 16 * q + 8 * c:16 * q + 8 * c + 8], pick, src[0:HEADS, SEQ:T],
                                      start=True, stop=True)
                        last = pe.matmul(bank(7)[:, 32 + c:33 + c],
                                         pick,
                                         d_skip4[0:HEADS, :], start=True, stop=True)
                    last.then_inc(dt_pe, 1)
                    pe.wait_ge(conv_d_act, 6)
                    for gr in range(2):
                        for c in range(QT):
                            last = pe.matmul(bank(4 + gr)[:, c * P:(c + 1) * P], dc[:, 2 + gr, c * P:(c + 1) * P],
                                             dc[:, 4 + gr, c * P:(c + 1) * P], start=True, stop=True)
                    last.then_inc(ssd_pe, 1)
                    pe.wait_ge(dt_dve, 2)
                    for c in range(QT):
                        to = bank(6 + c % 2)
                        if c >= 2:
                            pe.wait_ge(ssd_act, c - 1 + HEADS)
                        for q in range(4):
                            last = pe.transpose(to[:, q * P:(q + 1) * P], dc[:, q, c * P:(c + 1) * P], ident)
                        last.then_inc(ssd_pe, 1)
                    pe.wait_ge(ssd_act, HEADS + QT)
                    for c in range(QT):
                        pe.wait_ge(ssd_dve, c + 1)
                        if c >= 2:
                            pe.wait_ge(state_dve, c - 1)
                        for h in range(HEADS):
                            gr = h // 2
                            last = pe.matmul(bank(6 + c % 2)[:, h * HD:(h + 1) * HD],
                                             xb_tok[:, c, W + gr * P:W + (gr + 1) * P],
                                             xw[:, c, h * HD:(h + 1) * HD], start=True, stop=True)
                        last.then_inc(state_pe, 1)
                        if c == 0:
                            pe.wait_ge(ssd_dve, QT + 1)
                        if c >= 1:
                            pe.wait_ge(state_dve, c)
                        for h in range(HEADS):
                            r = HD * (h % 2)
                            to = bank(2 + h // 2)[r:r + HD, c * P:(c + 1) * P]
                            last = pe.matmul(to, xb_tok[:, c, h * HD:(h + 1) * HD], decay[:, h * QT + c, :],
                                             start=True, stop=(c == 0))
                            if c >= 1:
                                last = pe.matmul(to, h_t[:, h, :], read_c[:, h, c * P:(c + 1) * P], start=False, stop=True)
                        last.then_inc(state_pe, 1)
                    pe.wait_ge(state_dve, QT)
                    for c in range(2):
                        last = pe.transpose(bank(6)[:, c * P:(c + 1) * P],
                                            h_t.rearrange("p h c -> p (h c)")[:, c * P:(c + 1) * P], ident)
                    last.then_inc(state_pe, 1)
                    for q in range(4):
                        last = pe.transpose(bank(4)[0:NS, q * P:(q + 1) * P], dc[:, 2 + q, SEQ:T], ident)
                    last.then_inc(decd_pe, 1)
                    pe.wait_ge(decd_dve, 1)
                    for b in range(NS):
                        if b >= 2:
                            pe.wait_ge(decd_dve, b)
                        pe.matmul(bank(4 + b % 2), ident[0:NS, b:b + 1].broadcast_to([NS, P]), bc_rows,
                                  start=True, stop=True).then_inc(decd_pe, 1)
                    pe.wait_ge(gate_in, 4)
                    pe.wait_ge(state_dve, QT + 1)
                    for c in range(2):
                        pe.transpose(bank(6)[0:10, c * P:(c + 1) * P], feat[:, GC + c, T - 10:T], ident)
                        pe.transpose(bank(6)[0:38, W + c * P:W + (c + 1) * P], feat[:, GA + c, T - 38:T], ident)
                    for c in range(6):
                        to = bank(7)[0:11, c * P:(c + 1) * P] if c < 4 else bank(0)[0:11, (c - 4) * P:(c - 3) * P]
                        last = pe.transpose(to, feat[:, XBC + c, T - 11:T], ident)
                    last.then_inc(tails_turned, 1)
                    pe.wait_ge(cln_dve, 1)
                    pe.wait_ge(conv_c_done, 1)
                    pe.wait_ge(tails_ready, 4)
                    for c in range(2):
                        for h in range(2):
                            last = pe.matmul(pair(3)[:, h, :], ones, feat[:, GG + c, h * HALF:(h + 1) * HALF],
                                             start=(c == 0), stop=(c == 1))
                    last.then_inc(cln_pe, 1)
                    pe.wait_ge(cln_act, 2)
                    for c in range(2):
                        for h in range(2):
                            last = pe.matmul(pair(0)[:, h, :], ones, temp[:, c, h * HALF:(h + 1) * HALF],
                                             start=(c == 0), stop=(c == 1))
                    last.then_inc(cln_pe, 1)
                    pe.wait_ge(dn_act, 2)
                    for c in range(2):
                        for h in range(2):
                            last = pe.matmul(pair(1)[:, h, :], ones, temp[:, 2 + c, h * HALF:(h + 1) * HALF],
                                             start=(c == 0), stop=(c == 1))
                    last.then_inc(dn_pe, 1)

                    pe.wait_ge(b_done, 2)
                    pe.wait_ge(cln_act, 5)
                    pe.wait_ge(dn_dve, 3)
                    mixer_out = [ya[:, 0, :], ya[:, 1, :], feat[:, BX, :], feat[:, BX + 1, :], feat[:, GG, :],
                                 feat[:, GG + 1, :], feat[:, ZG, :], feat[:, ZG + 1, :]]
                    for m in range(KC):
                        wt = slab_here(OUT0 + m // 2)
                        if m >= 4:
                            pe.wait_ge(out_ready, 2 * (m - 3))
                        for k in range(KC):
                            for h in range(2):
                                last = pe.matmul(pair(m % 4)[:, h, :], wt[:, k, (m % 2) * P:(m % 2 + 1) * P],
                                                 mixer_out[k][:, h * HALF:(h + 1) * HALF],
                                                 start=(k == 0), stop=(k == KC - 1))
                        last.then_inc(out_summed, 1)
                    pe.wait_ge(out_ready, 2 * 5)
                    sum_squares(pair(0), out_ready, 0, 2)
                    pe.wait_ge(out_ready, 2 * 6)
                    sum_squares(pair(1), squares_ready, KC, 1)

                    pe.wait_ge(out_ready, 2 * KC)
                    pe.wait_ge(root_ready, 3)
                    pe.wait_ge(normed, 2 * KC)

                    def gate_up(i, turn, n0, first_free):
                        for c in range(2):
                            for part, summed in ((0, gate_summed), (1, up_summed)):
                                slot = (GU0 + n0 + part) % SLOTS
                                wt = view(ring[:, slot, :], 0, KC, W)
                                if c == 0:
                                    pe.wait_ge(slab_in[slot], turn * 16 + 16 * ((GU0 + n0 + part) // SLOTS + 1))
                                if part == 0 and first_free is not None:
                                    pe.wait_ge(hidden_ready, first_free + c)
                                for k in range(KC):
                                    for h in range(2):
                                        last = pe.matmul(pair(2 * c + part)[:, h, :], wt[:, k, c * P:(c + 1) * P],
                                                         u[:, k, h * HALF:(h + 1) * HALF], start=(k == 0), stop=(k == KC - 1))
                                last.then_inc(summed, 1)

                    with pe.Fori(0, GU_TURNS) as i:
                        for j in range(2):
                            gate_up(j, i, 2 * j, i * 4 + (2 * j + 1))
                    gate_up(0, GU_TURNS, 0, GU_TURNS * 4 + 1)

                    pe.wait_ge(hidden_ready, FFC + 2)
                    with pe.Fori(0, DN_TURNS) as i:
                        for c in range(2):
                            for half in range(2):
                                slot = (DN0 + 2 * c + half) % SLOTS
                                pe.wait_ge(slab_in[slot], i * 16 + 16 * ((DN0 + 2 * c + half) // SLOTS + 1))
                                wt = view(ring[:, slot, :], 0, 11, P)
                                if half == 0:
                                    pe.wait_ge(down_ready, i * 4 + (2 * c + 2))
                                for k in range(11):
                                    for h in range(2):
                                        last = pe.matmul(pair(c)[:, h, :], wt[:, k, :],
                                                         hidden[:, 11 * half + k, h * HALF:(h + 1) * HALF],
                                                         start=(half == 0 and k == 0), stop=(half == 1 and k == 10))
                            last.then_inc(down_summed, 1)
                    sum_squares(pair(2), down_ready, 4, 2)

                @block.scalar
                def _(act):
                    def root_of(n, sums, scale, eps):
                        act.wait_ge(sums_ready, n + 1)
                        act.activation(halves(root[:, :]), sums, ACT.Sqrt, bias=const("eps")[:, eps:eps + 1], scale=scale)\
                           .then_inc(root_ready, 1)

                    for k in range(KC):
                        act.activation(squares[:, k, :], x[:, k, :], ACT.Square).then_inc(squares_ready, 1)
                    root_of(0, pair(0), 1.0 / D_MODEL, 0)

                    g = 0
                    for s in range(N_TOK):
                        w = W if s < 4 else ID + IH
                        for t in range(QT + 1):
                            act.wait_ge(tok_summed, g + 1)
                            if t < QT:
                                to = (tok_q, tok_k, tok_v, tok_qi, kiw)[s][:, t, :]
                            else:
                                to = tok8[:, s * W:s * W + w]
                            act.copy(to, bank(2 + g % 6)[0:to.shape[0], 0:w]).then_inc(tok_ready, 1)
                            g += 1
                    for j in range(7):
                        act.wait_ge(turn_done, j + 1)
                        act.copy(turned[:, j, :], bank(j)).then_inc(turned_ready, 1)

                    feat_i = [0]

                    def feature_out(upto):
                        while feat_i[0] < upto:
                            i = feat_i[0]
                            n, s, c = feat_tiles[i]
                            act.wait_ge(feat_summed, i + 1)
                            if s == "dt":
                                act.copy(halves(temp[0:HEADS, 3, :]), pair(i % 2)[0:HEADS]).then_inc(feat_ready, 1)
                            else:
                                func = {GG // 2: ACT.Sigmoid, ZG // 2: ACT.Silu}.get(s, ACT.Copy)
                                act.activation(halves(feat[:, 2 * s + c, :]), pair(i % 2), func).then_inc(feat_ready, 1)
                            feat_i[0] += 1

                    feature_out(6)
                    act.wait_ge(dec_max, 1)
                    act.activation(p_row[0:32, :], l_row[0:32, :], ACT.Exp, bias=stat8[0:32, 1:2], scale=HD ** -0.5,
                                   accum_out=stat8[0:32, 2:3]).then_inc(dec_exp, 1)
                    feature_out(8)
                    act.wait_ge(dec_pe, 4)
                    for hp in range(2):
                        o = bank(4 + hp)[:, 0:32].rearrange("p (b h) -> p b h", h=HEADS)
                        for q in range(2):
                            act.copy(ya[HD * q:HD * (q + 1), hp, SEQ:T], o[HD * q:HD * (q + 1), :, 2 * hp + q])\
                               .then_inc(dec_out, 1)
                    for n, (blk, h) in enumerate(IDX):
                        keys = (blk + 1) * P
                        act.wait_ge(idx_summed, n + 1)
                        if n >= 2:
                            act.wait_ge(idx_added, n - 1)
                        act.activation(rect[:, n % 2, 0:keys], bank(4 + n % 4)[:, 0:keys], ACT.Relu,
                                       scale=(ID * IH) ** -0.5).then_inc(idx_rect, 1)
                    feature_out(len(feat_tiles))
                    act.wait_ge(conv_d_done, 1)
                    for c in range(6):
                        act.activation(dc[:, c, :], dc[:, c, :], ACT.Silu).then_inc(conv_d_act, 1)
                    act.wait_ge(dt_low, 1)
                    act.activation(temp[0:HEADS, 0, :], temp[0:HEADS, 0, :], ACT.Exp).then_inc(dt_exp, 1)
                    act.wait_ge(scalars_in, 48)
                    act.activation(a_neg[0:HEADS, :], a_log4[0:HEADS, :], ACT.Exp).then_inc(dt_exp, 1)
                    for j in range(len(STEPS) + 1):
                        if j < len(STEPS):
                            blk, h = STEPS[j]
                            keys = (blk + 1) * P
                            act.wait_ge(logits_masked, j + 1)
                            act.activation(rect[:, j % 2, 0:keys], rect[:, j % 2, 0:keys], ACT.Exp,
                                           bias=neg_max[:, j % 2:j % 2 + 1], scale=HD ** -0.5,
                                           accum_out=denom[:, j % 2:j % 2 + 1]).then_inc(exp_done, 1)
                        if j >= 1:
                            i = j - 1
                            blk, h = STEPS[i]
                            keys = (blk + 1) * P
                            act.wait_ge(prob_turned, i + 1)
                            if i >= 2:
                                act.wait_ge(mixed, i - 1)
                            act.copy(prob_t[:, i % 2, 0:keys], bank(6)[:, 0:keys]).then_inc(prob_t_ready, 1)
                            if h == HEADS - 1:
                                act.wait_ge(mixed, i + 1)
                                act.copy(ya[:, :, blk * P:(blk + 1) * P],
                                         view(PS[:, 7, :], (blk % 2) * W, 2, P)).then_inc(mixed_out, 1)
                    for h in range(HEADS):
                        act.wait_ge(dt_pe, 2 + h)
                        act.activation(ecs[:, h, :], bank(h), ACT.Exp).then_inc(ssd_act, 1)
                    act.wait_ge(dt_dve, 2)
                    act.activation(edt[:, 0], edt[:, 0], ACT.Exp).then_inc(dt_exp, 1)
                    act.wait_ge(dt_dve, 3)
                    act.activation(w_end, w_end, ACT.Exp).then_inc(dt_exp, 1)
                    for c in range(QT):
                        act.wait_ge(ssd_pe, 2 + c)
                        act.copy(xb_tok[:, c, :], bank(6 + c % 2)).then_inc(ssd_act, 1)
                    for h in range(HEADS):
                        act.wait_ge(segments, h + 1)
                        act.activation(decay[:, QT * h:QT * (h + 1), :], decay[:, QT * h:QT * (h + 1), :], ACT.Exp)\
                           .then_inc(ssd_act, 1)
                    act.wait_ge(tails_turned, 1)
                    act.copy(tail_b[0:10, :], bank(6)[0:10, 0:W]).then_inc(tails_ready, 1)
                    act.copy(tail_c[0:38, :], bank(6)[0:38, W:2 * W]).then_inc(tails_ready, 1)
                    act.copy(tail_d[0:11, 0:512], bank(7)[0:11, :]).then_inc(tails_ready, 1)
                    act.copy(tail_d[0:11, 512:768], bank(0)[0:11, 0:W]).then_inc(tails_ready, 1)
                    act.wait_ge(cln_dve, 2)
                    for c in range(2):
                        act.activation(temp[:, c, :], feat[:, GG + c, :], ACT.Square).then_inc(cln_act, 1)
                    act.wait_ge(dn_dve, 1)
                    for c in range(2):
                        act.activation(temp[:, 2 + c, :], feat[:, ZG + c, :], ACT.Square).then_inc(dn_act, 1)
                    act.wait_ge(cln_pe, 2)
                    act.activation(halves(root[:, :]), pair(0), ACT.Sqrt, bias=const("eps")[:, 1:2], scale=1.0 / W)\
                       .then_inc(cln_act, 1)
                    act.wait_ge(dn_pe, 1)
                    act.wait_ge(cln_dve, 3)
                    act.activation(halves(root[:, :]), pair(1), ACT.Sqrt, bias=const("eps")[:, 0:1], scale=1.0 / W)\
                       .then_inc(dn_act, 1)
                    act.wait_ge(cln_dve, 5)
                    for c in range(2):
                        act.activation(feat[:, GG + c, :], feat[:, GG + c, :], ACT.Silu, bias=pcol("cln_b", c))\
                           .then_inc(cln_act, 1)
                    for m in range(KC):
                        act.wait_ge(out_summed, m + 1)
                        if m == 5:
                            act.wait_ge(tails_stored, layer * (16 * N_TAILS) + 16 * N_TAILS)
                        act.copy(halves(u[:, m, :]), pair(m % 4)).then_inc(out_ready, 1)
                        act.activation(halves(squares[:, m, :]), pair(m % 4), ACT.Square).then_inc(out_ready, 1)
                    root_of(1, pair(0), 1.0 / D_MODEL, 0)
                    for k in range(KC):
                        act.wait_ge(x_updated, k + 1)
                        act.activation(squares[:, k, :], x[:, k, :], ACT.Square).then_inc(squares_ready, 1)
                    root_of(2, pair(1), 1.0 / D_MODEL, 0)

                    with act.Fori(0, FFC // 2) as i:
                        for c in range(2):
                            act.wait_ge(gate_summed, i * 2 + (c + 1))
                            act.wait_ge(hidden_ready, i * 2 + (c + 1))
                            act.activation(halves(hid_gate[:, c, :]), pair(2 * c), ACT.Silu).then_inc(gate_ready, 1)
                    act.sem_inc(down_ready, 4)
                    with act.Fori(0, DN_TURNS) as i:
                        for c in range(2):
                            act.wait_ge(down_summed, i * 2 + (c + 1))
                            act.copy(u[:, bass.ds(i * 2 + c, 1), :].rearrange("p o (h n) -> p (o h) n", h=2), pair(c))\
                               .then_inc(down_ready, 1)
                            act.activation(squares[:, bass.ds(i * 2 + c, 1), :].rearrange("p o (h n) -> p (o h) n", h=2),
                                           pair(c), ACT.Square).then_inc(down_ready, 1)
                    root_of(3, pair(2), 1.0 / D_MODEL, 0)

                @block.vector
                def _(dve):
                    made = [0]

                    def step(ins):
                        ins.then_inc(vec, 1)
                        made[0] += 1

                    def settle():
                        dve.wait_ge(vec, made[0])

                    def normalise(n, source, gain, to):
                        dve.wait_ge(root_ready, n + 1)
                        step(dve.reciprocal(rstd[:, :], root[:, :]))
                        settle()
                        for k in range(KC):
                            dve.scalar_tensor_tensor(to[:, k, :], source[:, k, :], pcol(gain, k), rstd[:, :], ALU.mult, ALU.mult)\
                               .then_inc(normed, 1)

                    dve.wait_ge(params_turned, 1)
                    dve.tensor_copy(par[:, :], bank(7)[:, 0:NA_ROWS + NB_ROWS]).then_inc(params_ready, 1)
                    dve.wait_ge(params_ready, 1)
                    normalise(0, x, "g_pre_mix", u)
                    dve.wait_ge(states_turned, 1)
                    dve.tensor_copy(ctx_c[:, :, :, 0:C_CONV - 1].rearrange("p c b t -> p (c b) t"),
                                    view(PS[:, 6, :], 0, 2 * NS, C_CONV - 1)).then_inc(states_ready, 1)
                    dve.tensor_copy(ctx_b[:, :, :, 0:2].rearrange("p c b t -> p (c b) t"),
                                    view(PS[:, 5, :], 0, 2 * NS, 2)).then_inc(states_ready, 1)
                    dve.tensor_copy(ctx_d[:, :, :, 0:3].rearrange("p c b t -> p (c b) t"),
                                    view(PS[:, 5, :], 32, 6 * NS, 3)).then_inc(states_ready, 1)

                    def rope(v, heads, rot, tables, p, blocks):
                        half = rot // 2
                        n = blocks * heads
                        a = rope_a[0:p, 0:n * rot].rearrange("p (t h r) -> p t h r", h=heads, r=rot)
                        b = rope_b[0:p, 0:n * rot].rearrange("p (t h r) -> p t h r", h=heads, r=rot)
                        tabs = [const(x)[0:p].rearrange("p (t r) -> p t r", t=blocks).unsqueeze(2) for x in tables]
                        full, part = [p, blocks, heads, rot], [p, blocks, heads, half]
                        for t in range(blocks):
                            step(dve.tensor_tensor(a[:, t], v[:, t], tabs[0][:, t].broadcast_to([p, heads, rot]), ALU.mult))
                            step(dve.tensor_tensor(b[:, t, :, 0:half], v[:, t, :, half:rot],
                                                   tabs[1][:, t].broadcast_to([p, heads, half]), ALU.mult))
                            step(dve.tensor_tensor(b[:, t, :, half:rot], v[:, t, :, 0:half],
                                                   tabs[2][:, t].broadcast_to([p, heads, half]), ALU.mult))
                        settle()
                        for t in range(blocks):
                            last = dve.tensor_tensor(v[:, t], a[:, t], b[:, t], ALU.add)
                            if t < blocks - 1:
                                step(last)
                        return last

                    tab, tab_i = ("cos", "nsin", "sin"), ("cos_i", "nsin_i", "sin_i")
                    for s, (t, heads, width, rot, tb) in ((0, (tok_q, HEADS, HD, 16, tab)), (1, (tok_k, HEADS, HD, 16, tab)),
                                                          (3, (tok_qi, IH, ID, 8, tab_i)), (4, (kiw, 1, ID, 8, tab_i))):
                        dve.wait_ge(tok_ready, 5 * s + 4)
                        v = t[:, :, 0:heads * width].rearrange("p t (h c) -> p t h c", c=width)[:, :, :, 0:rot]
                        ins = rope(v, heads, rot, tb, P, QT)
                        if s < 4:
                            ins.then_inc(rope_done, 1)
                            dve.wait_ge(rope_done, 1 + (0, 1, None, 2)[s])
                        else:
                            step(ins)
                            settle()
                            dve.tensor_copy(ki_four, kiw[:, :, 0:ID].unsqueeze(2).broadcast_to([P, QT, 4, ID]))\
                               .then_inc(rope_done, 1)
                    dve.wait_ge(tok_ready, 25)
                    for at, heads, width, rot, tb in ((0, 2 * HEADS, HD, 16, ("cos_d", "nsin_d", "sin_d")),
                                                      (3 * W, IH + 1, ID, 8, ("cos_id", "nsin_id", "sin_id"))):
                        v = tok8[:, at:at + heads * width].rearrange("p (t h c) -> p t h c", t=1, c=width)[:, :, :, 0:rot]
                        step(rope(v, heads, rot, tb, NS, 1))
                        settle()
                    dve.tensor_scalar(tok8[:, TOK_W - IH:TOK_W], tok8[:, TOK_W - IH:TOK_W], (ID * IH) ** -0.5, None, ALU.mult)\
                       .then_inc(rope_done, 1)
                    dve.wait_ge(rope_done, 5)

                    dve.wait_ge(k_cache_in, 16 * 2 * NS)
                    dve.wait_ge(ki_cache_in, 16 * 2 * NS)
                    for b in range(NS):
                        qb, ib = bank(4 + 2 * (b % 2)), bank(5 + 2 * (b % 2))
                        dve.wait_ge(rows_spread, b + 1)
                        kb = k_cache[:, 2 * b:2 * b + 2, :]
                        step(dve.tensor_tensor(kb, kb, qb[:, 0:W].unsqueeze(1).broadcast_to([P, 2, W]), ALU.mult))
                        pi = prod_i.rearrange("p (g h c) -> p g h c", g=2, c=ID)
                        for pg in range(2):
                            step(dve.tensor_tensor(pi[:, pg], ki_cache[:, 2 * b + pg, :].unsqueeze(1).broadcast_to([P, IH, ID]),
                                                   ib[:, 0:W].rearrange("p (h c) -> p h c", c=ID), ALU.mult))
                        settle()
                        step(dve.tensor_reduce(past_l[:, :, b, :], kb.rearrange("p g (h c) -> p g h c", c=HD), AX.X, ALU.add))
                        s16 = sc64[:, 0:16].rearrange("p (g h) -> p g h", g=2)
                        step(dve.tensor_reduce(s16, pi, AX.X, ALU.add))
                        settle()
                        dve.scalar_tensor_tensor(s16, s16, 0.0, ib[:, W + ID:W + ID + IH].unsqueeze(1).broadcast_to([P, 2, IH]),
                                                 ALU.max, ALU.mult).then_inc(rows_used, 1)
                        dve.wait_ge(rows_used, b + 1)
                        step(dve.tensor_reduce(past_s[:, :, b], s16, AX.X, ALU.add))
                    q8, k8 = tok8[:, 0:W], tok8[:, W:2 * W]
                    settle()
                    step(dve.tensor_tensor(prod8[0:NS, :], q8, k8, ALU.mult))
                    settle()
                    step(dve.tensor_reduce(m_row[0:NS, 257:261], prod8[0:NS, :].rearrange("p (h c) -> p h c", c=HD), AX.X, ALU.add))
                    settle()
                    step(dve.tensor_tensor(prod8[0:NS, :].rearrange("p (h c) -> p h c", c=ID),
                                           tok8[:, 3 * W:4 * W].rearrange("p (h c) -> p h c", c=ID),
                                           tok8[:, 4 * W:4 * W + ID].unsqueeze(1).broadcast_to([NS, IH, ID]), ALU.mult))
                    settle()
                    step(dve.tensor_reduce(sc64[0:NS, 16:24], prod8[0:NS, :].rearrange("p (h c) -> p h c", c=ID), AX.X, ALU.add))
                    settle()
                    step(dve.scalar_tensor_tensor(sc64[0:NS, 24:32], sc64[0:NS, 16:24], 0.0, tok8[:, TOK_W - IH:TOK_W],
                                                  ALU.max, ALU.mult))
                    settle()
                    dve.tensor_reduce(s_row[0:NS, 256:257], sc64[0:NS, 24:32], AX.X, ALU.add).then_inc(dec_dve, 1)
                    dve.wait_ge(dec_pe, 1)
                    step(dve.tensor_copy(s_row[0:NS, 0:256], bank(4)[0:NS, 0:256]))
                    step(dve.tensor_copy(l_row[0:32, 0:256], bank(5)[0:32, 0:256]))
                    dve.wait_ge(dec_dve, 1)
                    for r in range(TOPK_SAMPLE // 8):
                        settle()
                        step(dve.max(best8[0:NS, :], s_row[0:NS, :]))
                        settle()
                        step(dve.match_replace(s_row[0:NS, :], best8[0:NS, :], s_row[0:NS, :], TAKEN))
                    settle()
                    dve.tensor_scalar(m_row[0:NS, 0:257], s_row[0:NS, :], TAKEN, MASKED, ALU.not_equal, ALU.mult)\
                       .then_inc(dec_dve, 1)
                    dve.wait_ge(dec_pe, 2)
                    step(dve.tensor_tensor(sc64[0:32, 32:36], bank(6)[0:32, 257:261], const("head_of_row")[0:32, :], ALU.mult))
                    settle()
                    step(dve.tensor_reduce(l_row[0:32, 256:257], sc64[0:32, 32:36], AX.X, ALU.add))
                    settle()
                    step(dve.tensor_tensor(l_row[0:32, :], l_row[0:32, :], bank(6)[0:32, 0:257], ALU.add))
                    settle()
                    step(dve.tensor_reduce(stat8[0:32, 0:1], l_row[0:32, :], AX.X, ALU.max))
                    settle()
                    dve.tensor_scalar(stat8[0:32, 1:2], stat8[0:32, 0:1], -HD ** -0.5, None, ALU.mult).then_inc(dec_max, 1)
                    dve.wait_ge(dec_exp, 1)
                    step(dve.reciprocal(stat8[0:32, 3:4], stat8[0:32, 2:3]))
                    settle()
                    step(dve.tensor_scalar(p_row[0:32, :], p_row[0:32, :], stat8[0:32, 3:4], None, ALU.mult))
                    settle()
                    dve.tensor_scalar(self_p[0:32, :], const("sample_of_row")[0:32, :], p_row[0:32, 256:257], None, ALU.mult)\
                       .then_inc(dec_dve, 1)
                    dve.wait_ge(dec_pe, 3)
                    step(dve.tensor_copy(p_col.rearrange("p g m -> p (g m)"), bank(7)[:, 0:64]))
                    dve.tensor_copy(self_pt[0:NS, :], bank(7)[0:NS, 64:96]).then_inc(dec_dve, 1)

                    for n, (blk, h) in enumerate(IDX):
                        keys = (blk + 1) * P
                        w = kiw[:, blk, ID + h:ID + h + 1]
                        s = score[:, blk - 1, 0:keys]
                        dve.wait_ge(idx_rect, n + 1)
                        if h == 0:
                            dve.tensor_scalar(s, rect[:, n % 2, 0:keys], w, None, ALU.mult).then_inc(idx_added, 1)
                        else:
                            dve.wait_ge(idx_added, n)
                            dve.scalar_tensor_tensor(s, rect[:, n % 2, 0:keys], w, s, ALU.mult, ALU.add).then_inc(idx_added, 1)
                    dve.wait_ge(idx_added, len(IDX))
                    for blk in range(1, QT):
                        own = score[:, blk - 1, blk * P:(blk + 1) * P]
                        step(dve.tensor_tensor(own, own, const("future"), ALU.add))
                    for r in range(TOPK_PROMPT // 8):
                        settle()
                        for blk in range(1, QT):
                            step(dve.max(chunk_best[:, blk - 1, :], score[:, blk - 1, 0:(blk + 1) * P]))
                        settle()
                        for blk in range(1, QT):
                            s = score[:, blk - 1, 0:(blk + 1) * P]
                            step(dve.match_replace(s, chunk_best[:, blk - 1, :], s, TAKEN))
                    settle()
                    for blk in range(1, QT):
                        s = score[:, blk - 1, 0:(blk + 1) * P]
                        step(dve.tensor_scalar(s, s, TAKEN, MASKED, ALU.not_equal, ALU.mult))
                    settle()

                    def conv(to, source, name, chunk, taps, bias, chunks):
                        w = lambda tap: pcol(name, tap * chunks + chunk)
                        if bias is None:
                            step(dve.tensor_scalar(to[:, 0:SEQ], source[:, 0:SEQ], w(taps - 1), None, ALU.mult))
                        else:
                            step(dve.tensor_scalar(to[:, 0:SEQ], source[:, 0:SEQ], w(taps - 1), bias, ALU.mult, ALU.add))
                        for back in range(1, taps):
                            settle()
                            step(dve.scalar_tensor_tensor(to[:, back:SEQ], source[:, 0:SEQ - back], w(taps - 1 - back),
                                                          to[:, back:SEQ], ALU.mult, ALU.add))

                    def conv8(to, window, name, taps, chunks, scratch, bias):
                        w = par[:, AT[name]:AT[name] + taps * chunks].rearrange("p (t c) -> p c t", c=chunks)
                        pr = scratch[:, 0:chunks * NS * taps].rearrange("p (c b t) -> p c b t", b=NS, t=taps)
                        for c in range(chunks):
                            step(dve.tensor_tensor(pr[:, c], window[:, c], w[:, c].unsqueeze(1).broadcast_to([P, NS, taps]), ALU.mult))
                        settle()
                        for c in range(chunks):
                            step(dve.tensor_reduce(to[:, c, SEQ:T], pr[:, c], AX.X, ALU.add))
                        settle()
                        if bias is not None:
                            for c in range(chunks):
                                step(dve.tensor_scalar(to[:, c, SEQ:T], to[:, c, SEQ:T], pcol(bias, c), None, ALU.add))
                            settle()

                    dve.wait_ge(feat_ready, DT_COUNT)
                    for c in range(6):
                        step(dve.tensor_copy(ctx_d[:, c, :, D_CONV - 1], feat[:, XBC + c, SEQ:T]))
                    settle()
                    conv8(dc, ctx_d, "dconv_w", D_CONV, 6, prod_i, "dconv_b")
                    for c in range(6):
                        conv(dc[:, c, :], feat[:, XBC + c, :], "dconv_w", c, D_CONV, pcol("dconv_b", c), 6)
                    settle()
                    dve.sem_inc(conv_d_done, 1)

                    dve.wait_ge(scalars_in, 16 * 3)
                    dve.wait_ge(dec_pe, 4)
                    v, e, s, z, q = temp[0:HEADS, 3, :], temp[0:HEADS, 0, :], temp[0:HEADS, 1, :], temp[0:HEADS, 2, :], t4[0:HEADS, :]
                    step(dve.memset(csdt[:, :], 0.0))
                    step(dve.tensor_scalar(v, v, dt_bias[0:HEADS, :], None, ALU.add))
                    settle()
                    dve.scalar_tensor_tensor(e, v, -1.0, v, ALU.mult, ALU.min).then_inc(dt_low, 1)

                    dve.wait_ge(feat_ready, feat_count(GA, GA + 1, GG, GG + 1))
                    for c in range(2):
                        dve.tensor_tensor(feat[:, GA + c, :], feat[:, GA + c, :], feat[:, GG + c, :], ALU.mult).then_inc(gate_in, 1)
                    dve.wait_ge(gate_in, 2)
                    for c in range(2):
                        step(dve.tensor_copy(ctx_c[:, c, :, C_CONV - 1], feat[:, GA + c, SEQ:T]))
                    settle()
                    conv8(feat[:, GG:GG + 2, :], ctx_c, "cconv_w", C_CONV, 2, prod_i, "cconv_b")
                    dve.sem_inc(cln_dve, 1)
                    dve.wait_ge(feat_ready, feat_count(GC, GC + 1, BX, BX + 1, GB, GB + 1))
                    for c in range(2):
                        dve.tensor_tensor(feat[:, GC + c, :], feat[:, GC + c, :], feat[:, BX + c, :], ALU.mult).then_inc(gate_in, 1)
                    dve.wait_ge(gate_in, 4)
                    for c in range(2):
                        step(dve.tensor_copy(ctx_b[:, c, :, B_CONV - 1], feat[:, GC + c, SEQ:T]))
                    settle()
                    conv8(feat[:, BX:BX + 2, :], ctx_b, "bconv_w", B_CONV, 2, prod_i, None)
                    for c in range(2):
                        conv(feat[:, BX + c, :], feat[:, GC + c, :], "bconv_w", c, B_CONV, None, 2)
                    settle()
                    for c in range(2):
                        dve.tensor_tensor(feat[:, BX + c, :], feat[:, BX + c, :], feat[:, GB + c, :], ALU.mult).then_inc(b_done, 1)

                    dve.wait_ge(dt_exp, 1)
                    step(dve.tensor_scalar(s, e, 2.0, None, ALU.add))
                    settle()
                    step(dve.reciprocal(s, s))
                    settle()
                    step(dve.tensor_tensor(s, s, e, ALU.mult))
                    settle()
                    step(dve.tensor_tensor(z, s, s, ALU.mult))
                    settle()
                    step(dve.tensor_scalar(q, z, 1.0 / 15.0, None, ALU.mult))
                    for n in (13, 11, 9, 7, 5, 3):
                        settle()
                        step(dve.scalar_tensor_tensor(q, q, 1.0 / n, z, ALU.add, ALU.mult))
                    settle()
                    step(dve.scalar_tensor_tensor(q, q, 1.0, s, ALU.add, ALU.mult))
                    step(dve.tensor_scalar(v, v, 0.0, None, ALU.max))
                    settle()
                    step(dve.scalar_tensor_tensor(q, q, 2.0, v, ALU.mult, ALU.add))
                    settle()
                    step(dve.tensor_copy(csdt[32:32 + HEADS, :], q))
                    dve.wait_ge(dt_exp, 2)
                    step(dve.tensor_scalar(e, q, a_neg[0:HEADS, :], -1.0, ALU.mult, ALU.mult))
                    settle()
                    for c in range(QT):
                        cols = slice(c * P, (c + 1) * P)
                        step(dve.tensor_tensor_scan(csdt[0:HEADS, cols], ones[0:HEADS, :], e[:, cols], 0.0, ALU.mult, ALU.add))
                    dve.tensor_copy(csdt[0:HEADS, SEQ:T], e[:, SEQ:T]).then_inc(dt_dve, 1)

                    for j in range(len(STEPS) + 1):
                        if j < len(STEPS):
                            blk, h = STEPS[j]
                            keys = (blk + 1) * P
                            dve.wait_ge(logits_summed, j + 1)
                            if j >= 2:
                                dve.wait_ge(prob_turned, j - 1)
                            mask = const("future") if blk == 0 else score[:, blk - 1, 0:keys]
                            step(dve.tensor_tensor_reduce(rect[:, j % 2, 0:keys], bank(4 + j % 2)[:, 0:keys], mask, 1.0, MASKED,
                                                          ALU.add, ALU.max, top_max[:, j % 2:j % 2 + 1]))
                            settle()
                            dve.tensor_scalar(neg_max[:, j % 2:j % 2 + 1], top_max[:, j % 2:j % 2 + 1], -HD ** -0.5, None,
                                              ALU.mult).then_inc(logits_masked, 1)
                        if j >= 1:
                            i = j - 1
                            blk, h = STEPS[i]
                            keys = (blk + 1) * P
                            b2 = slice(i % 2, i % 2 + 1)
                            dve.wait_ge(exp_done, i + 1)
                            step(dve.reciprocal(rden[:, b2], denom[:, b2]))
                            settle()
                            dve.tensor_scalar(rect[:, i % 2, 0:keys], rect[:, i % 2, 0:keys], rden[:, b2], None, ALU.mult)\
                               .then_inc(prob_ready, 1)

                    dve.wait_ge(dt_pe, 1)
                    cs_dt = view(PS[:, 6, :], 0, QT, 64)
                    cs4, dt4, we4 = (t.rearrange("p (c h) -> p c h", h=HEADS) for t in (cst_tok, dt_tok, w_end))
                    step(dve.tensor_copy(cs4, cs_dt[:, :, 0:HEADS]))
                    step(dve.tensor_copy(dt4, cs_dt[:, :, 32:32 + HEADS]))
                    dve.wait_ge(dt_pe, 6)
                    step(dve.tensor_copy(edt.rearrange("p q c b -> p (q c b)"), bank(7)[:, 0:32]))
                    dve.tensor_copy(dsk, bank(7)[:, 32:34]).then_inc(dt_dve, 1)
                    dve.wait_ge(dt_dve, 2)
                    settle()
                    dve.wait_ge(ssd_act, HEADS)
                    for h in range(HEADS):
                        ends = bank(h)[:, P - 1:SEQ:P]
                        step(dve.tensor_tensor(we4[:, :, h], ends, cs4[:, :, h], ALU.subtract))
                    settle()
                    dve.sem_inc(dt_dve, 1)
                    for h in range(HEADS):
                        for c in range(QT):
                            step(dve.scalar_tensor_tensor(decay[:, h * QT + c, :], bank(h)[:, c * P:(c + 1) * P],
                                                          cs4[:, c, h:h + 1], const("later"), ALU.subtract, ALU.add))
                        settle()
                        dve.sem_inc(segments, 1)
                    dve.wait_ge(dt_exp, 4)
                    step(dve.tensor_tensor(w_end, w_end, dt_tok, ALU.mult))
                    settle()
                    dve.wait_ge(mixed, len(STEPS))
                    dve.wait_ge(kv_stored, layer * (16 * N_KV) + 16 * N_KV)
                    for c in range(QT):
                        dve.wait_ge(ssd_act, HEADS + 1 + c)
                        dve.tensor_tensor(xw[:, c, :].rearrange("p (h c) -> p h c", c=HD),
                                          xb_tok[:, c, 0:W].rearrange("p (h c) -> p h c", c=HD),
                                          we4[:, c, :].unsqueeze(2).broadcast_to([P, HEADS, HD]), ALU.mult).then_inc(ssd_dve, 1)
                    dve.wait_ge(ssd_pe, 1)
                    for h in range(HEADS):
                        step(dve.tensor_tensor(read_c[:, h, :], dc[:, 4 + h // 2, 0:SEQ], ecs[:, h, :], ALU.mult))
                    for h in range(HEADS):
                        dve.wait_ge(ssd_act, HEADS + QT + 1 + h)
                        for c in range(QT):
                            m = decay[:, h * QT + c, :]
                            step(dve.scalar_tensor_tensor(m, m, dt4[:, c, h:h + 1], bank(4 + h // 2)[:, c * P:(c + 1) * P],
                                                          ALU.mult, ALU.mult))
                    settle()
                    dve.sem_inc(ssd_dve, 1)
                    flat_h = h_t.rearrange("p h c -> p (h c)")
                    for c in range(QT):
                        dve.wait_ge(state_pe, 2 * c + 2)
                        new = bank(6 + c % 2)[:, 0:W]
                        if c == 0:
                            dve.tensor_copy(flat_h, new).then_inc(state_dve, 1)
                        else:
                            end = ecs[:, :, (c + 1) * P - 1].unsqueeze(2).broadcast_to([P, HEADS, HD])
                            step(dve.tensor_tensor(h_t, h_t, end, ALU.mult))
                            settle()
                            dve.tensor_tensor(flat_h, flat_h, new, ALU.add).then_inc(state_dve, 1)
                        dve.wait_ge(state_dve, c + 1)
                    for c in range(2):
                        step(dve.scalar_tensor_tensor(dc[:, c, 0:SEQ], dc[:, c, 0:SEQ], dsk[:, c:c + 1], bank(2 + c), ALU.mult, ALU.add))
                    dve.wait_ge(state_pe, 2 * QT + 1)
                    dve.tensor_copy(ssm_rows.rearrange("p c n -> p (c n)"), bank(6)[:, 0:W]).then_inc(state_dve, 1)
                    dve.wait_ge(decd_pe, 1)
                    dve.tensor_copy(bc_rows, bank(4)[0:NS, :]).then_inc(decd_dve, 1)
                    step(dve.tensor_tensor(dtx, edt[:, 1], dc[:, 0:2, SEQ:T], ALU.mult))
                    settle()
                    dve.wait_ge(ssm_in, layer * 16 + 16)
                    for b in range(NS):
                        dve.wait_ge(decd_pe, b + 2)
                        bc = bank(4 + b % 2)
                        pr = (prod_n, prod_n2)
                        for c in range(2):
                            step(dve.tensor_scalar(pr[c], bc[:, c * P:(c + 1) * P], dtx[:, c, b:b + 1], None, ALU.mult))
                        settle()
                        for c in range(2):
                            hs = ssm[:, 2 * b + c, :]
                            step(dve.scalar_tensor_tensor(hs, hs, edt[:, 0, c, b:b + 1], pr[c], ALU.mult, ALU.add))
                        settle()
                        for c in range(2):
                            last = dve.tensor_tensor_reduce(pr[c], ssm[:, 2 * b + c, :], bc[:, W + c * P:W + (c + 1) * P], 1.0, 0.0,
                                                            ALU.mult, ALU.add, y_dec[:, c, b:b + 1])
                            if c == 0:
                                step(last)
                        last.then_inc(decd_dve, 1)
                        dve.wait_ge(decd_dve, b + 2)
                    dve.sem_inc(ssm_done, 1)
                    for c in range(2):
                        step(dve.scalar_tensor_tensor(dc[:, c, SEQ:T], dc[:, c, SEQ:T], dsk[:, c:c + 1], y_dec[:, c, :], ALU.mult, ALU.add))
                    settle()
                    for c in range(2):
                        step(dve.tensor_tensor(feat[:, ZG + c, :], feat[:, ZG + c, :], dc[:, c, :], ALU.mult))
                    settle()
                    dve.sem_inc(dn_dve, 1)
                    dve.wait_ge(cln_pe, 1)
                    for c in range(2):
                        f = halves(feat[:, GG + c, :])
                        step(dve.scalar_tensor_tensor(f, pair(3), -1.0 / W, f, ALU.mult, ALU.add))
                    settle()
                    dve.sem_inc(cln_dve, 1)
                    dve.wait_ge(cln_act, 3)
                    dve.reciprocal(rstd[:, :], root[:, :]).then_inc(cln_dve, 1)
                    dve.wait_ge(cln_dve, 3)
                    for c in range(2):
                        f = feat[:, GG + c, :]
                        dve.scalar_tensor_tensor(f, f, pcol("cln_g", c), rstd[:, :], ALU.mult, ALU.mult).then_inc(cln_dve, 1)
                    dve.wait_ge(dn_act, 3)
                    dve.wait_ge(cln_dve, 5)
                    step(dve.reciprocal(rstd[:, :], root[:, :]))
                    settle()
                    for c in range(2):
                        f = feat[:, ZG + c, :]
                        dve.scalar_tensor_tensor(f, f, pcol("d_norm", c), rstd[:, :], ALU.mult, ALU.mult).then_inc(dn_dve, 1)

                    def add_normed(n, gain):
                        dve.wait_ge(root_ready, n + 1)
                        step(dve.reciprocal(rstd[:, :], root[:, :]))
                        settle()
                        for k in range(KC):
                            step(dve.scalar_tensor_tensor(u[:, k, :], u[:, k, :], pcol(gain, k), rstd[:, :], ALU.mult, ALU.mult))
                            settle()
                            dve.tensor_tensor(x[:, k, :], x[:, k, :], u[:, k, :], ALU.add).then_inc(x_updated, 1)

                    add_normed(1, "g_post_mix")
                    dve.wait_ge(stored, layer * (16 * N_SSM) + 16 * N_SSM)
                    dve.sem_inc(hidden_ready, 2)
                    normalise(2, x, "g_pre_ffn", u)
                    with dve.Fori(0, FFC // 2) as i:
                        for c in range(2):
                            dve.wait_ge(gate_ready, i * 2 + (c + 1))
                            dve.wait_ge(up_summed, i * 2 + (c + 1))
                            dve.tensor_tensor(hidden[:, bass.ds(i * 2 + c, 1), :].rearrange("p o (h n) -> p (o h) n", h=2),
                                              halves(hid_gate[:, c, :]), pair(2 * c + 1), ALU.mult).then_inc(hidden_ready, 1)
                    add_normed(3, "g_post_ffn")
                    dve.wait_ge(x_updated, 2 * KC)

                @block.gpsimd
                def _(pool):
                    l = layer

                    def tokens(t):
                        return row(t, l)[0:1, 0].rearrange("o (t p) h c -> p (o t) (h c)", p=P) if t.ndim == 5 else \
                            row(t, l)[0:1, 0].rearrange("o (t p) c -> p (o t) c", p=P)

                    pool.dma_start(ssm, row(d["state_ssm"], l).rearrange("o b (c h) p n -> (h p) (o b c) n", c=2))\
                        .then_inc(ssm_in, 16)
                    pool.wait_ge(rope_done, 2)
                    pool.dma_start(tokens(k_prompt), tok_k).then_inc(kv_stored, 16)
                    pool.wait_ge(tok_ready, 14)
                    pool.dma_start(tokens(v_prompt), tok_v).then_inc(kv_stored, 16)
                    pool.wait_ge(rope_done, 5)
                    pool.dma_start(tokens(kidx_prompt), kiw[:, :, 0:ID]).then_inc(kv_stored, 16)
                    for t, at in ((k_sample, W), (v_sample, 2 * W)):
                        pool.dma_start(row(t, l).rearrange("o b s h c -> (o b s) (h c)"), tok8[:, at:at + W]).then_inc(kv_stored, 16)
                    pool.dma_start(row(kidx_sample, l).rearrange("o b s c -> (o b s) c"), tok8[:, 4 * W:4 * W + ID])\
                        .then_inc(kv_stored, 16)
                    for t, name in ((bconv_sample, "state_bconv"), (cconv_sample, "state_cconv"), (dconv_sample, "state_dconv")):
                        n = t.shape[2]
                        pool.dma_start(row(t, l)[:, :, 0:n - 1].rearrange("o b t c -> (o b) t c"),
                                       row(d[name], l)[:, :, 1:n].rearrange("o b t c -> (o b) t c")).then_inc(state_copied, 16)
                    pool.wait_ge(gate_in, 2)
                    pool.wait_ge(cln_dve, 1)
                    made = 0
                    w = lambda tap, c: pcol("cconv_w", 2 * tap + c)
                    for c in range(2):
                        pool.tensor_scalar(feat[:, GG + c, 0:SEQ], feat[:, GA + c, 0:SEQ], w(C_CONV - 1, c), pcol("cconv_b", c),
                                           ALU.mult, ALU.add).then_inc(pool_step, 1)
                        made += 1
                    for back in range(1, C_CONV):
                        for c in range(2):
                            pool.tensor_scalar(pool_tmp[c][:, back:SEQ], feat[:, GA + c, 0:SEQ - back], w(C_CONV - 1 - back, c),
                                               None, ALU.mult).then_inc(pool_step, 1)
                            made += 1
                        pool.wait_ge(pool_step, made)
                        for c in range(2):
                            acc = feat[:, GG + c, back:SEQ]
                            pool.tensor_tensor(acc, acc, pool_tmp[c][:, back:SEQ], ALU.add).then_inc(pool_step, 1)
                            made += 1
                        pool.wait_ge(pool_step, made)
                    pool.sem_inc(conv_c_done, 1)
                    pool.wait_ge(tails_ready, 4)
                    for src, lo, t_p, t_s in ((tail_b, 2, bconv_prompt, bconv_sample), (tail_c, 30, cconv_prompt, cconv_sample),
                                              (tail_d, 3, dconv_prompt, dconv_sample)):
                        pool.dma_start(row(t_p, l).rearrange("o b t c -> (o b t) c"), src[0:lo, :]).then_inc(tails_stored, 16)
                        pool.dma_start(row(t_s, l)[:, :, lo - 1].rearrange("o b c -> (o b) c"), src[lo:lo + NS, :])\
                            .then_inc(tails_stored, 16)
                    pool.wait_ge(state_dve, QT + 1)
                    pool.dma_start(row(ssm_prompt, l)[0:1, 0].rearrange("o (c h) p n -> (h p) (o c) n", c=2), ssm_rows)\
                        .then_inc(stored, 16)
                    pool.wait_ge(ssm_done, 1)
                    pool.dma_start(row(ssm_sample, l).rearrange("o b (c h) p n -> (h p) (o b c) n", c=2), ssm).then_inc(stored, 16)
                    pool.wait_ge(kv_stored, layer * (16 * N_KV) + 16 * N_KV)
                    pool.wait_ge(state_copied, layer * (16 * N_STATES) + 16 * N_STATES)
                    pool.wait_ge(tails_stored, layer * (16 * N_TAILS) + 16 * N_TAILS)
                    pool.wait_ge(stored, layer * (16 * N_SSM) + 16 * N_SSM)

            nc.all_engine_barrier()
            nc.gpsimd.sem_clear(range(sems[first_layer_sem].num, sems[last_layer_sem - 1].num + 1))
            nc.all_engine_barrier()

        y_turned, y_copied, y_stored = sem("y_turned"), sem("y_copied"), sem("y_stored")
        y_rows = view(arena, 0, QT + 1, D_MODEL)
        with nc.Block() as block:
            @block.tensor
            def _(pe):
                for t in range(QT + 1):
                    m = P if t < QT else NS
                    for q in range(2):
                        n = 2 * t + q
                        if n >= 8:
                            pe.wait_ge(y_copied, n - 7)
                        for c in range(4):
                            last = pe.transpose(bank(n % 8)[0:m, c * P:(c + 1) * P], x[:, 4 * q + c, t * P:t * P + m], ident)
                        last.then_inc(y_turned, 1)

            @block.vector
            def _(dve):
                for t in range(QT + 1):
                    m = P if t < QT else NS
                    for q in range(2):
                        dve.wait_ge(y_turned, 2 * t + q + 1)
                        dve.tensor_copy(y_rows[0:m, t, 512 * q:512 * (q + 1)], bank((2 * t + q) % 8)[0:m, :]).then_inc(y_copied, 1)

            @block.sync
            def _(sp):
                for t in range(QT + 1):
                    sp.wait_ge(y_copied, 2 * t + 2)
                    to = y_prompt[0, t * P:(t + 1) * P, :] if t < QT else y_sample.rearrange("b s f -> (b s) f")
                    sp.dma_start(to, y_rows[0:P if t < QT else NS, t, :]).then_inc(y_stored, 16)
                sp.wait_ge(y_stored, 16 * (QT + 1))
    return nc


_INS = ["x_prompt", "x_sample", "cache_k", "cache_v", "cache_kidx", "page_table", "state_bconv", "state_cconv",
        "state_dconv", "state_ssm", "w_in", "w_out", "g_pre_mix", "g_post_mix", "g_pre_ffn", "g_post_ffn", "bconv_w",
        "cconv_w", "cconv_b", "cln_g", "cln_b", "dconv_w", "dconv_b", "dt_bias", "a_log", "d_skip", "d_norm",
        "ffn_gate", "ffn_up", "ffn_down"]
_XBC = W + 4 * N_STATE
_OUTS = [(1, SEQ, D_MODEL), (NS, 1, D_MODEL), (DEPTH, 1, SEQ, HEADS, HD), (DEPTH, 1, SEQ, HEADS, HD),
         (DEPTH, 1, SEQ, ID), (DEPTH, NS, 1, HEADS, HD), (DEPTH, NS, 1, HEADS, HD), (DEPTH, NS, 1, ID),
         (DEPTH, 1, 2, W), (DEPTH, NS, 2, W), (DEPTH, 1, 30, W), (DEPTH, NS, 30, W), (DEPTH, 1, 3, _XBC),
         (DEPTH, NS, 3, _XBC), (DEPTH, 1, HEADS, HD, N_STATE), (DEPTH, NS, HEADS, HD, N_STATE)]


def kernel(**inputs):
    import concourse.bacc as _bacc
    from concourse.bass_utils import run_bass_kernel_spmd as _run

    nc = _bacc.Bacc("TRN2", target_bir_lowering=False, num_devices=1)
    arrays, dram = {}, {}
    for name in _INS:
        a = np.ascontiguousarray(inputs[name])
        arrays[f"in_{name}"] = a
        dram[name] = nc.dram_tensor(f"in_{name}", a.shape, mybir.dt.from_np(a.dtype), kind="ExternalInput").ap()
    arrays["constants"] = shape_constants()
    dram["constants"] = nc.dram_tensor("constants", arrays["constants"].shape, F32, kind="ExternalInput").ap()
    outs = [nc.dram_tensor(f"out_{i}", shape, F32, kind="ExternalOutput").ap() for i, shape in enumerate(_OUTS)]
    hybrid_decoder(nc, dram, outs)
    r = _run(nc, [arrays], core_ids=[0])
    return tuple(r.results[0][f"out_{i}"] for i in range(len(_OUTS)))
```

```python
from contextlib import ExitStack

import numpy as np
import concourse.bass as bass
from concourse import mybir

F32 = mybir.dt.float32
F32R = mybir.dt.float32r
I32 = mybir.dt.int32
ALU = mybir.AluOpType
ACT = mybir.ActivationFunctionType
AX = mybir.AxisListType

P = 128
D_MODEL, SEQ, DEPTH, NS, PAST, PAGE = 1024, 512, 2, 8, 256, 128
HEADS, HD, IH, ID = 4, 64, 8, 32
TOPK_PROMPT, TOPK_SAMPLE = 128, 64
THETA = 500000.0
B_CONV, C_CONV, D_CONV = 3, 31, 4
D_FF = 2816
N_STATE = 128
W = 256
T = SEQ + NS
HALF = T // 2
KC = D_MODEL // P
FFC = D_FF // P
QT = SEQ // P
TOK_W = 4 * W + ID + IH
FEAT0 = TOK_W
DT0 = FEAT0 + 9 * W
RMS_EPS, LN_EPS = 1e-6, 1e-5
MASKED = -1e30
TAKEN = -3e38
SLOTS = 4
SLAB = KC * W

ROWS_A = [("g_pre_mix", 8), ("g_post_mix", 8), ("g_pre_ffn", 8), ("g_post_ffn", 8), ("bconv_w", 6),
          ("cconv_w", 62), ("cconv_b", 2), ("cln_g", 2), ("cln_b", 2), ("d_norm", 2)]
ROWS_B = [("dconv_w", 24), ("dconv_b", 6)]
AT = {}
for _rows, _base in ((ROWS_A, 0), (ROWS_B, sum(n for _, n in ROWS_A))):
    for _name, _n in _rows:
        AT[_name] = _base
        _base += _n
NA_ROWS, NB_ROWS = sum(n for _, n in ROWS_A), sum(n for _, n in ROWS_B)

CONST = {}
_at = 0
for _name, _n in (("ident", 128), ("ones", 128), ("later", 128), ("future", 128), ("upto", 128), ("head_of_row", 4),
                  ("sample_of_row", 8), ("cos", 64), ("nsin", 32), ("sin", 32), ("cos_i", 32),
                  ("nsin_i", 16), ("sin_i", 16), ("cos_d", 16), ("nsin_d", 8), ("sin_d", 8),
                  ("cos_id", 8), ("nsin_id", 4), ("sin_id", 4), ("eps", 2),
                  ("rows_of_sample", 32), ("state_rows", 256)):
    CONST[_name] = (_at, _n)
    _at += _n
N_CONST = _at


def shape_constants():
    c = np.zeros((P, N_CONST), np.float32)

    def put(name, v):
        a, n = CONST[name]
        c[:, a:a + n] = np.asarray(v, np.float32).reshape(P, n)

    i = np.arange(P)
    put("ident", np.eye(P))
    put("ones", np.ones((P, P)))
    put("later", np.where(i[:, None] > i[None, :], MASKED, 0.0))
    put("future", np.where(i[None, :] > i[:, None], MASKED, 0.0))
    put("upto", i[:, None] <= i[None, :])
    put("head_of_row", i[:, None] % HEADS == np.arange(HEADS)[None])
    put("sample_of_row", i[:, None] // HEADS == np.arange(NS)[None])
    put("rows_of_sample", np.arange(32)[None, :] // HEADS == i[:, None])
    put("state_rows", np.arange(2 * P)[None, :] // HD == i[:, None])
    for rot, tail in ((HD // 4, ""), (ID // 4, "_i")):
        half = rot // 2
        inv = np.float32(THETA) ** (-np.arange(half, dtype=np.float32) * np.float32(2.0) / np.float32(rot))
        for pos, d in ((np.arange(SEQ).reshape(QT, P).T, ""), (np.full((P, 1), PAST), "d")):
            ang = pos.astype(np.float32)[:, :, None] * inv
            name = (tail + d) if tail else ("_" + d if d else "")
            put("cos" + name, np.concatenate([np.cos(ang)] * 2, -1))
            put("nsin" + name, -np.sin(ang))
            put("sin" + name, np.sin(ang))
    a, _ = CONST["eps"]
    c[:, a], c[:, a + 1] = RMS_EPS, LN_EPS
    return c


def hybrid_decoder(nc, d, out):
    (y_prompt, y_sample, k_prompt, v_prompt, kidx_prompt, k_sample, v_sample, kidx_sample, bconv_prompt,
     bconv_sample, cconv_prompt, cconv_sample, dconv_prompt, dconv_sample, ssm_prompt, ssm_sample) = out
    ctx = ExitStack()

    address = {}

    def sb(name, shape, dt=F32):
        t = ctx.enter_context(nc.sbuf_tensor(name, shape, dt))
        address[name] = nc.sbuf_base - 4 * int(np.prod(shape[1:]))
        return t

    def over(name, under, at, shape, dt=F32R):
        return nc.alloc_sbuf_tensor_at(name, shape, dt, offset=address[under] + 4 * at)

    sems = []

    def sem(name):
        sems.append(ctx.enter_context(nc.semaphore(name)))
        return sems[-1]

    with ctx:
        cst = sb("cst", [P, N_CONST])
        x = sb("x", [P, KC, T])
        u = sb("u", [P, KC, T])
        ring = sb("ring", [P, SLOTS, SLAB])
        hid = sb("hid", [P, FFC * T])
        all_par = sb("all_par", [P, DEPTH, NA_ROWS + NB_ROWS])
        par = sb("par", [P, 1, NA_ROWS + NB_ROWS])
        small = sb("small", [P, 64])
        pages = sb("pages", [1, 2 * NS], I32)
        tok8 = sb("tok8", [NS, TOK_W])
        ya = sb("ya", [P, 2, T])
        ctx_b = sb("ctx_b", [P, 2, NS, B_CONV])
        ctx_c = sb("ctx_c", [P, 2, NS, C_CONV])
        ctx_d = sb("ctx_d", [P, 6, NS, D_CONV])
        root = sb("root", [P, T])
        rstd = sb("rstd", [P, T])
        dt_tiles = sb("dt_tiles", [P, 6, (QT + 1) * HEADS])
        head_row = sb("head_row", [1, 2 * HEADS])
        head_all = sb("head_all", [P, 2, HEADS])
        arena = sb("arena", [P, FFC * T])
        side = sb("side", [P, 7200])
        u_hi, u_lo = over("u_hi", "u", 0, [P, KC, T]), over("u_lo", "side", 0, [P, KC, T])
        hid_hi, hid_lo = over("hid_hi", "hid", 0, [P, FFC, T]), over("hid_lo", "arena", 0, [P, FFC, T])
        y_lo = [over(f"y_lo{k}", *(("hid", (12 + k) * T) if k < 6 else ("ya", (k - 6) * T)), [P, 1, T]) for k in range(KC)]
        w_hi = [over(f"w_hi{i}", "ring", (4 + 2 * i) * KC * P, [P, KC, P]) for i in range(2)]
        w_lo = [over(f"w_lo{i}", "ring", (5 + 2 * i) * KC * P, [P, KC, P]) for i in range(2)]
        PS = ctx.enter_context(nc.psum_tensor("PS", [P, 8, 512], F32))

        def view(t, at, *dims):
            n = int(np.prod(dims))
            v = t[:, at:at + n]
            names = "abcd"[:len(dims)]
            if len(dims) == 1:
                return v
            return v.rearrange(f"p ({' '.join(names)}) -> p {' '.join(names)}",
                               **{k: m for k, m in zip(names[:-1], dims[:-1])})

        def const(name):
            a, n = CONST[name]
            return cst[:, a:a + n]

        def pcol(name, i):
            return par[:, 0, AT[name] + i:AT[name] + i + 1]

        ident, ones = const("ident"), const("ones")
        feat = view(hid, 0, 18, T)
        BX, GB, GC, GA, GG, ZG, XBC = 0, 2, 4, 6, 8, 10, 12
        v_cache = view(hid, 0, 2 * NS, W)
        ssm = view(hid, 18 * T, 2 * NS, N_STATE)
        raw = [view(ring[:, i // 2, :], (i % 2) * KC * P, KC, P) for i in range(4)]

        tok_k, tok_v, tok_q = view(arena, 0, QT, W), view(arena, 1024, QT, W), view(arena, 2048, QT, W)
        kiw = view(arena, 3072, QT, ID + IH)
        ki_four = view(arena, 3232, QT, 4, ID)
        turned = view(arena, 3744, 7, SEQ)
        score = view(arena, 7328, 3, SEQ)
        tok_qi = view(arena, 8864, QT, W)
        rect = view(arena, 8864, 2, SEQ)
        prob_t = view(arena, 9888, 2, SEQ)
        rope_a, rope_b = view(arena, 10912, 256), view(arena, 11168, 256)
        squares = view(arena, 3744, KC, T)
        rows_of = [[view(arena, 4096 + (2 * l + q) * P, P) for q in range(2)] for l in range(DEPTH)]
        rows_cc, rows_cb, rows_cd = view(arena, 8160, 2, W), view(arena, 8672, W), view(arena, 8928, 3 * W)
        h_t = view(arena, 2048, HEADS, HD)
        read_c = view(arena, 0, HEADS, SEQ)
        decay = view(arena, 3744, 4 * QT, P)
        ecs = view(arena, 5792, HEADS, SEQ)
        xb_tok = view(arena, 7840, QT, 2 * W)
        xw = view(arena, 9888, QT, W)
        scaled = view(arena, 0, KC, T)
        hid_gate, hid_f = ya, view(side, KC * T, 2, T)
        ffn_squares = view(side, 0, KC, T)
        mix = view(hid, 0, KC, T)

        k_cache = view(side, 0, 2 * NS, W)
        dc = view(side, 0, 6, T)
        dt_rows = view(side, 3120, 2, HEADS, HD)[0:NS]
        temp = view(side, 4096, 4, T)
        ki_cache = view(side, 6176, 2 * NS, ID)
        prod_i = view(side, 6688, 512)
        tails = u[:, 5:8, :].rearrange("p k t -> p (k t)")
        tail_b, tail_c, tail_d = tails[:, 0:256], tails[:, 256:512], tails[:, 512:1280]
        ssm_rows = view(arena, 2304, 2, N_STATE)
        out_rows = view(arena, 0, 8, 1024)
        past_s = view(side, 4096, 2, NS)
        past_l = view(side, 4112, 2, NS, HEADS)
        s_row = side[:, 4176:4176 + 257]
        m_row = side[:, 4433:4433 + 261]
        l_row = side[:, 4694:4694 + 257]
        p_row = side[:, 4951:4951 + 257]
        p_col = view(side, 5208, 2, 32)
        self_p, self_pt = side[:, 5272:5280], side[:, 5280:5312]
        sc64, prod8 = side[:, 5312:5376], side[:, 5376:5632]
        best8 = side[:, 5632:5640]
        stat8 = side[:, 5640:5656]
        chunk_best = view(side, 3900, 3, 8)
        pool_tmp = [arena[:, 10912:11424], sb("pool_tmp", [P, SEQ])[:, :]]
        cst_tok = small[:, 0:16]
        dt_v, dt_e, dt_s, dt_z, dt_q, dt_a = (dt_tiles[:, i, :] for i in range(6))
        dt_tok = dt_q[:, 0:QT * HEADS]
        w_end = small[:, 32:48]
        neg_max, denom, rden, top_max = small[:, 48:50], small[:, 50:52], small[:, 52:54], small[:, 54:56]
        dsk = small[:, 56:58]
        d_skip4 = small[0:36, 60:61]
        edt = view(side, 3640, 2, 2, NS)
        dtx = view(side, 3680, 2, NS)
        y_dec = view(side, 3700, 2, NS)
        bc_rows = side[0:NS, 6176:6176 + 512]
        prod_n = side[:, 6688:6688 + 128]
        prod_n2 = side[:, 6816:6816 + 128]

        def pair(i):
            return PS[:, 2 * i:2 * i + 2, 0:HALF]

        def bank(i):
            return PS[:, i, :]

        def halves(ap):
            return ap.rearrange("p (h n) -> p h n", h=2)

        def row(t, l):
            return t[bass.ds(l, 1)]

        const_in, rows_in, sample_in = sem("const_in"), sem("rows_in"), sem("sample_in")
        params_in, params_turned = sem("params_in"), sem("params_turned")
        x_turned, x_copied, x8_turned = sem("x_turned"), sem("x_copied"), sem("x8_turned")
        x_rows = view(arena, 0, QT, D_MODEL)
        x8 = side[0:NS, 0:D_MODEL]
        with nc.Block() as block:
            @block.sync
            def _(sp):
                sp.dma_start(cst[:, :], d["constants"]).then_inc(const_in, 16)
                for t in range(QT):
                    sp.dma_start(x_rows[:, t, :], d["x_prompt"][0, t * P:(t + 1) * P, :]).then_inc(rows_in, 16)
                sp.dma_start(x8, d["x_sample"].rearrange("b s f -> (b s) f")).then_inc(sample_in, 16)
                sp.dma_start(pages[:, :], d["page_table"].rearrange("(o b) g -> o (b g)", o=1)).then_inc(sample_in, 16)
                for l in range(DEPTH):
                    for rows, tile in zip((ROWS_A, ROWS_B), rows_of[l]):
                        at = 0
                        for name, n in rows:
                            src = d[name][l:l + 1]
                            src = src.rearrange("o (c p) -> (o c) p", p=P) if src.ndim == 2 else \
                                src.rearrange("o t (c p) -> (o t c) p", p=P)
                            sp.dma_start(tile[at:at + n, :], src).then_inc(params_in, 16)
                            at += n
                sp.wait_ge(sample_in, 32)

            @block.tensor
            def _(pe):
                pe.wait_ge(const_in, 16)
                pe.wait_ge(rows_in, 16 * QT)
                for c in range(KC):
                    for t in range(QT):
                        last = pe.transpose(bank(c)[:, t * P:(t + 1) * P], x_rows[:, t, c * P:(c + 1) * P], ident)
                    last.then_inc(x_turned, 1)
                pe.wait_ge(sample_in, 32)
                pe.wait_ge(x_copied, 1)
                for c in range(KC):
                    last = pe.transpose(bank(0)[:, c * NS:(c + 1) * NS], x8[:, c * P:(c + 1) * P], ident[0:NS, 0:NS])
                last.then_inc(x8_turned, 1)
                pe.wait_ge(params_in, 16 * DEPTH * (len(ROWS_A) + len(ROWS_B)))
                pe.wait_ge(x_copied, DEPTH + 1)
                for l in range(DEPTH):
                    pe.transpose(bank(1 + l)[:, 0:NA_ROWS], rows_of[l][0][0:NA_ROWS, :], ident[0:NA_ROWS, 0:NA_ROWS])
                    pe.transpose(bank(1 + l)[:, NA_ROWS:NA_ROWS + NB_ROWS], rows_of[l][1][0:NB_ROWS, :],
                                 ident[0:NB_ROWS, 0:NB_ROWS]).then_inc(params_turned, 1)

            @block.vector
            def _(dve):
                for c in range(KC):
                    dve.wait_ge(x_turned, c + 1)
                    dve.tensor_copy(x[:, c, 0:SEQ], bank(c)).then_inc(x_copied, 1)
                dve.wait_ge(x8_turned, 1)
                dve.tensor_copy(x[:, :, SEQ:T], view(PS[:, 0, :], 0, KC, NS)).then_inc(x_copied, 1)
                for l in range(DEPTH):
                    dve.wait_ge(params_turned, l + 1)
                    dve.tensor_copy(all_par[:, l, :], bank(1 + l)[:, 0:NA_ROWS + NB_ROWS]).then_inc(x_copied, 1)
                dve.wait_ge(x_copied, KC + 1 + DEPTH)

        nc.all_engine_barrier()

        kv_stored, stored, state_copied = sem("kv_stored"), sem("stored"), sem("state_copied")
        tails_stored, ssm_in = sem("tails_stored"), sem("ssm_in")
        N_KV, N_STATES, N_TAILS, N_SSM = 6, 3, 6, 2

        first_layer_sem = len(sems)
        scalars_in, states_in = sem("scalars_in"), sem("states_in")
        k_cache_in, v_cache_in, ki_cache_in = sem("k_cache_in"), sem("v_cache_in"), sem("ki_cache_in")
        slab_in = [sem(f"slab_in{i}") for i in range(SLOTS)]
        params_ready = sem("params_ready")
        states_turned, states_ready = sem("states_turned"), sem("states_ready")
        squares_ready, sums_ready, root_ready = sem("squares_ready"), sem("sums_ready"), sem("root_ready")
        normed, x_updated = sem("normed"), sem("x_updated")
        tok_summed, tok_ready = sem("tok_summed"), sem("tok_ready")
        rope_done, turn_done, turned_ready = sem("rope_done"), sem("turn_done"), sem("turned_ready")
        rows_spread, rows_used = sem("rows_spread"), sem("rows_used")
        feat_summed, feat_ready = sem("feat_summed"), sem("feat_ready")
        dec_pe, dec_dve, dec_max, dec_exp, dec_out = (sem("dec_pe"), sem("dec_dve"), sem("dec_max"), sem("dec_exp"),
                                                      sem("dec_out"))
        idx_summed, idx_rect, idx_added, chosen = sem("idx_summed"), sem("idx_rect"), sem("idx_added"), sem("chosen")
        logits_summed, logits_masked, exp_done, prob_ready = (sem("logits_summed"), sem("logits_masked"),
                                                              sem("exp_done"), sem("prob_ready"))
        prob_turned, prob_t_ready, mixed, mixed_out = (sem("prob_turned"), sem("prob_t_ready"), sem("mixed"),
                                                       sem("mixed_out"))
        vec, pool_step, conv_c_done, conv_c_started = sem("vec"), sem("pool_step"), sem("conv_c_done"), sem("conv_c_started")
        conv_d_done, conv_d_act, segments, dec_rows = (sem("conv_d_done"), sem("conv_d_act"), sem("segments"),
                                                       sem("dec_rows"))
        dt_pe, dt_exp, dt_low, dt_dve = sem("dt_pe"), sem("dt_exp"), sem("dt_low"), sem("dt_dve")
        dt_w_in = sem("dt_w_in")
        ssd_pe, ssd_act, ssd_dve = sem("ssd_pe"), sem("ssd_act"), sem("ssd_dve")
        state_pe, state_dve = sem("state_pe"), sem("state_dve")
        decd_pe, decd_dve, decd_act = sem("decd_pe"), sem("decd_dve"), sem("decd_act")
        glu_act, gate_in, tails_turned, tails_ready = (sem("glu_act"), sem("gate_in"), sem("tails_turned"),
                                                       sem("tails_ready"))
        ssm_done = sem("ssm_done")
        cln_pe, cln_act, cln_dve = sem("cln_pe"), sem("cln_act"), sem("cln_dve")
        dn_pe, dn_act, dn_dve = sem("dn_pe"), sem("dn_act"), sem("dn_dve")
        b_done = sem("b_done")
        out_summed, out_ready = sem("out_summed"), sem("out_ready")
        raw_in = [sem(f"raw_in{i}") for i in range(4)]
        part_hi, part_lo = sem("part_hi"), sem("part_lo")
        u_scaled, u_hi_ready, u_lo_ready = sem("u_scaled"), sem("u_hi_ready"), sem("u_lo_ready")
        gate_summed, up_summed, gate_ready = sem("gate_summed"), sem("up_summed"), sem("gate_ready")
        hidden_made, hidden_hi, hidden_lo = sem("hidden_made"), sem("hidden_hi"), sem("hidden_lo")
        y_hi_ready, y_lo_ready = sem("y_hi_ready"), sem("y_lo_ready")
        down_part, down_ready = sem("down_part"), sem("down_ready")
        last_layer_sem = len(sems)

        FEAT_SLABS = [6, 7, 8, 4, 3, 5, 2, 0, 1]
        N_TOK, N_FEAT = 5, len(FEAT_SLABS)
        GU0 = KC
        DN0 = GU0 + 2 * FFC
        DOWN_PARTS = [(0, 6), (6, 6), (12, 5), (17, 5)]
        feat_tiles = []
        for n, s in enumerate(FEAT_SLABS):
            for c in range(2):
                feat_tiles.append((n, s, c))
        FEAT_AT = {(s, c): i for i, (n, s, c) in enumerate(feat_tiles)}

        def feat_count(*chunks):
            return 1 + max(FEAT_AT[(c // 2, c % 2)] for c in chunks)

        STEPS = [(blk, h) for blk in range(QT) for h in range(HEADS)]
        IDX = [(blk, h) for blk in range(1, QT) for h in range(IH)]

        with nc.Fori(0, DEPTH) as layer:
            with nc.Block() as block:

                @block.sync
                def _(sp):
                    l = layer

                    def used_up(n):
                        if n < N_TOK:
                            return tok_summed, (QT + 1) * (n + 1)
                        return feat_summed, sum(1 for m, _, _ in feat_tiles if m <= n - N_TOK)

                    def slab(n, dst_w, src):
                        if n >= SLOTS:
                            sp.wait_ge(*used_up(n - SLOTS))
                        sp.dma_start(view(ring[:, n % SLOTS, :], 0, KC, W)[:, :, 0:dst_w], src)\
                          .then_inc(slab_in[n % SLOTS], 16)

                    def cols(name, a, w):
                        return row(d[name], l).rearrange("o (k p) n -> p (o k) n", p=P)[:, :, a:a + w]

                    for n in range(2):
                        slab(n, W, cols("w_in", n * W, W))
                    per = 4 * (C_CONV - 1)
                    for half in range(2):
                        sp.dma_start(rows_cc[0:per, half, :], row(d["state_cconv"], l)[:, 4 * half:4 * half + 4]
                                     .rearrange("o b t c -> (o b t) c")).then_inc(states_in, 16)
                    sp.dma_start(rows_cb[0:2 * NS, :], row(d["state_bconv"], l)
                                 .rearrange("o b t c -> (o b t) c")).then_inc(states_in, 16)
                    sp.dma_start(rows_cd[0:3 * NS, :], row(d["state_dconv"], l)
                                 .rearrange("o b t c -> (o b t) c")).then_inc(states_in, 16)
                    sp.dma_start(d_skip4[0:HEADS, :], row(d["d_skip"], l).rearrange("o h -> h o")).then_inc(scalars_in, 16)
                    for name, at in (("dt_bias", 0), ("a_log", HEADS)):
                        sp.dma_start(head_row[:, at:at + HEADS], row(d[name], l)).then_inc(scalars_in, 16)
                    for n in range(2, 4):
                        slab(n, W, cols("w_in", n * W, W))
                    for i in range(2 * NS):
                        page = sp.value_load(pages[0:1, i:i + 1], min_val=0, max_val=d["cache_k"].shape[1] - 1)
                        for name, dst, s in (("cache_kidx", ki_cache, ki_cache_in), ("cache_k", k_cache, k_cache_in),
                                             ("cache_v", v_cache, v_cache_in)):
                            src = row(d[name], l)[:, bass.ds(page, 1)]
                            src = src.rearrange("o g r c -> r (o g c)") if src.ndim == 4 else \
                                src.rearrange("o g r h c -> r (o g h c)")
                            sp.dma_start(dst[:, i, :], src).then_inc(s, 16)
                    slab(4, ID + IH, cols("w_in", 4 * W, ID + IH))
                    sp.dma_start(view(ring[:, 4 % SLOTS, :], 0, KC, W)[:, :, ID + IH:ID + IH + HEADS], cols("w_in", DT0, HEADS))\
                      .then_inc(dt_w_in, 16)
                    for i, s in enumerate(FEAT_SLABS):
                        slab(N_TOK + i, W, cols("w_in", FEAT0 + s * W, W))
                    for j in range(KC):
                        if j < 4:
                            sp.wait_ge(*used_up(max(n for n in range(N_TOK + N_FEAT) if n % SLOTS == j // 2)))
                        else:
                            sp.wait_ge(part_lo, j - 3)
                        sp.dma_start(raw[j % 4], cols("w_out", j * P, P)).then_inc(raw_in[j % 4], 16)

                    def gate_up(j, col):
                        src = row(d["ffn_up" if j % 2 else "ffn_gate"], l)\
                            .rearrange("o (k p) n -> p (o k) n", p=P)[:, :, bass.ds(col, P)]
                        sp.dma_start(raw[j], src).then_inc(raw_in[j], 16)

                    with sp.Fori(0, FFC // 2) as i:
                        for j in range(4):
                            sp.wait_ge(part_lo, i * 4 + (GU0 + j - 3))
                            gate_up(j, i * (2 * P) + (j // 2) * P)

                    def down(q, col):
                        k, n = DOWN_PARTS[q]
                        src = row(d["ffn_down"], l).rearrange("o (k p) n -> p (o k) n", p=P)[:, k:k + n, bass.ds(col, P)]
                        sp.dma_start(raw[q][:, 0:n, :], src).then_inc(raw_in[q], 16)

                    with sp.Fori(0, KC) as m:
                        for q in range(4):
                            sp.wait_ge(part_lo, m * 4 + (DN0 + q - 3))
                            down(q, m * P)

                @block.tensor
                def _(pe):
                    def slab_here(n):
                        pe.wait_ge(slab_in[n % SLOTS], 16 * (n // SLOTS + 1))
                        return view(ring[:, n % SLOTS, :], 0, KC, W)

                    def sum_squares(to, ready, first, each, squares=squares):
                        for k in range(KC):
                            pe.wait_ge(ready, first + each * (k + 1))
                            for h in range(2):
                                last = pe.matmul(to[:, h, :], ones, squares[:, k, h * HALF:(h + 1) * HALF],
                                                 start=(k == 0), stop=(k == KC - 1))
                        last.then_inc(sums_ready, 1)

                    sum_squares(pair(0), squares_ready, 0, 1)
                    g = 0
                    for s in range(N_TOK):
                        w = W if s < 4 else ID + IH
                        if s == 2:
                            pe.wait_ge(root_ready, 1)
                            pe.wait_ge(states_in, 64)
                            per = 4 * (C_CONV - 1)
                            for c in range(2):
                                for half in range(2):
                                    at = (2 * c + half) * per
                                    pe.transpose(bank(0)[:, at:at + per], rows_cc[0:per, half, c * P:(c + 1) * P],
                                                 ident[0:per, 0:per])
                                pe.transpose(bank(1)[:, c * 16:(c + 1) * 16], rows_cb[0:16, c * P:(c + 1) * P], ident[0:16, 0:16])
                            for c in range(6):
                                last = pe.transpose(bank(1)[:, 32 + c * 24:32 + (c + 1) * 24], rows_cd[0:24, c * P:(c + 1) * P],
                                                    ident[0:24, 0:24])
                            pe.wait_ge(scalars_in, 48)
                            pe.matmul(bank(1)[:, 256:256 + 2 * HEADS], ones[0:1, :], head_row[:, :], start=True, stop=True)\
                              .then_inc(states_turned, 1)
                        wt = slab_here(s)
                        if s == 4:
                            w += HEADS
                            pe.wait_ge(dt_w_in, 16)
                        for t in range(QT + 1):
                            m = P if t < QT else NS
                            to = bank(2 + g % 6)[0:m, 0:w]
                            if g >= 6:
                                pe.wait_ge(tok_ready, g - 5)
                            for k in range(KC):
                                if s == 0 and t == 0:
                                    pe.wait_ge(normed, k + 1)
                                last = pe.matmul(to, u[:, k, t * P:t * P + m], wt[:, k, 0:w], start=(k == 0), stop=(k == KC - 1))
                            last.then_inc(tok_summed, 1)
                            g += 1

                    pe.wait_ge(tok_ready, g)
                    pe.wait_ge(states_ready, 4)
                    for j, (src, c, need) in enumerate(((tok_q, 0, 1), (tok_q, 1, 1), (tok_k, 0, 2), (tok_k, 1, 2),
                                                        (tok_qi, 0, 3), (tok_qi, 1, 3), (ki_four, 0, 4))):
                        pe.wait_ge(rope_done, need)
                        if j == 0:
                            pe.wait_ge(root_ready, 1)
                        flat = src.rearrange("p t a b -> p t (a b)") if src.ndim == 4 else src
                        for t in range(QT):
                            last = pe.transpose(bank(j)[:, t * P:(t + 1) * P], flat[:, t, c * P:(c + 1) * P], ident)
                        last.then_inc(turn_done, 1)

                    feat_i = [0]

                    def feature_tile():
                        i = feat_i[0]
                        n, s, c = feat_tiles[i]
                        wt = slab_here(N_TOK + n)
                        m, a = P, c * P
                        if i >= 2:
                            pe.wait_ge(feat_ready, i - 1)
                        for k in range(KC):
                            for h in range(2):
                                last = pe.matmul(pair(i % 2)[0:m, h, :], wt[:, k, a:a + m],
                                                 u[:, k, h * HALF:(h + 1) * HALF], start=(k == 0), stop=(k == KC - 1))
                        last.then_inc(feat_summed, 1)
                        feat_i[0] += 1

                    def spread(b):
                        if b >= 2:
                            pe.wait_ge(rows_used, b - 1)
                        pick = ident[0:NS, b:b + 1].broadcast_to([NS, P])
                        pe.matmul(bank(4 + 2 * (b % 2))[:, 0:W], pick, tok8[:, 0:W], start=True, stop=True)
                        pe.matmul(bank(5 + 2 * (b % 2))[:, 0:TOK_W - 3 * W], pick, tok8[:, 3 * W:TOK_W],
                                  start=True, stop=True).then_inc(rows_spread, 1)

                    pe.wait_ge(turned_ready, 7)
                    pe.wait_ge(rope_done, 5)
                    for b in range(0, NS, 2):
                        spread(b)
                        spread(b + 1)
                        feature_tile()
                    pe.wait_ge(dec_dve, 1)
                    for pg in range(2):
                        pe.transpose(bank(4)[0:NS, pg * P:(pg + 1) * P], past_s[:, pg, :], ident)
                        last = pe.transpose(bank(5)[0:32, pg * P:(pg + 1) * P],
                                            past_l.rearrange("p g b h -> p g (b h)")[:, pg, :], ident)
                    last.then_inc(dec_pe, 1)
                    feature_tile()
                    feature_tile()
                    pe.wait_ge(dec_dve, 2)
                    pe.matmul(bank(6)[0:32, 0:261],
                              const("rows_of_sample")[0:NS, :],
                              m_row[0:NS, :], start=True, stop=True).then_inc(dec_pe, 1)
                    feature_tile()
                    pe.wait_ge(dec_dve, 3)
                    for pg in range(2):
                        pe.transpose(bank(7)[:, pg * 32:(pg + 1) * 32], p_row[0:32, pg * P:(pg + 1) * P], ident[0:32, 0:32])
                    pe.transpose(bank(7)[0:NS, 64:96], self_p[0:32, :], ident[0:32, 0:32]).then_inc(dec_pe, 1)
                    feature_tile()
                    pe.wait_ge(dec_dve, 4)
                    pe.wait_ge(v_cache_in, 16 * 2 * NS)
                    for hp in range(2):
                        pe.matmul(bank(4 + hp)[:, 0:32], tok8[:, 2 * W + hp * P:2 * W + (hp + 1) * P], self_pt[0:NS, :],
                                  start=True, stop=False, skip_group_check=True)
                        for b in range(NS):
                            for pg in range(2):
                                last = pe.matmul(bank(4 + hp)[:, 4 * b:4 * b + 4], v_cache[:, 2 * b + pg, hp * P:(hp + 1) * P],
                                                 p_col[:, pg, 4 * b:4 * b + 4], start=False,
                                                 stop=(b == NS - 1 and pg == 1), skip_group_check=True)
                    last.then_inc(dec_pe, 1)

                    pe.wait_ge(dec_out, 4)
                    for n, (blk, h) in enumerate(IDX):
                        keys = (blk + 1) * P
                        r = 32 * (h % 4)
                        if n >= 4:
                            pe.wait_ge(idx_rect, n - 3)
                        pe.matmul(bank(4 + n % 4)[:, 0:keys], turned[r:r + 32, 4 + h // 4, blk * P:(blk + 1) * P],
                                  turned[r:r + 32, 6, 0:keys], start=True, stop=True).then_inc(idx_summed, 1)
                    while feat_i[0] < len(feat_tiles):
                        feature_tile()

                    pe.wait_ge(gate_in, 4)
                    pe.wait_ge(feat_ready, len(feat_tiles))
                    for c in range(2):
                        pe.transpose(bank(0)[0:10, c * P:(c + 1) * P], feat[:, GC + c, T - 10:T], ident)
                        pe.transpose(bank(0)[0:38, W + c * P:W + (c + 1) * P], feat[:, GA + c, T - 38:T], ident)
                    for c in range(6):
                        to = bank(1)[0:11, c * P:(c + 1) * P] if c < 4 else bank(2)[0:11, (c - 4) * P:(c - 3) * P]
                        last = pe.transpose(to, feat[:, XBC + c, T - 11:T], ident)
                    last.then_inc(tails_turned, 1)

                    pe.wait_ge(idx_rect, len(IDX))
                    for j in range(-1, len(STEPS) + 2):
                        if j + 1 < len(STEPS):
                            blk, h = STEPS[j + 1]
                            r = HD * (h % 2)
                            if j >= 2:
                                pe.wait_ge(logits_masked, j - 1)
                            pe.matmul(bank(3 + (j + 1) % 3)[:, 0:(blk + 1) * P],
                                      turned[r:r + HD, h // 2, blk * P:(blk + 1) * P],
                                      turned[r:r + HD, 2 + h // 2, 0:(blk + 1) * P],
                                      start=True, stop=True).then_inc(logits_summed, 1)
                        if 1 <= j <= len(STEPS):
                            i = j - 1
                            blk, h = STEPS[i]
                            pe.wait_ge(prob_ready, i + 1)
                            if i >= 1:
                                pe.wait_ge(prob_t_ready, i)
                            for kb in range(blk + 1):
                                last = pe.transpose(bank(6)[:, kb * P:(kb + 1) * P], rect[:, i % 2, kb * P:(kb + 1) * P], ident)
                            last.then_inc(prob_turned, 1)
                        if j >= 2:
                            i = j - 2
                            blk, h = STEPS[i]
                            r = HD * (h % 2)
                            pe.wait_ge(prob_t_ready, i + 1)
                            if h == 0 and blk >= 2:
                                pe.wait_ge(mixed_out, blk - 1)
                            at = (blk % 2) * W + (h // 2) * P
                            for kb in range(blk + 1):
                                last = pe.matmul(bank(7)[r:r + HD, at:at + P], tok_v[:, kb, h * HD:(h + 1) * HD],
                                                 prob_t[:, i % 2, kb * P:(kb + 1) * P], start=(kb == 0), stop=(kb == blk))
                            last.then_inc(mixed, 1)

                    pe.wait_ge(tails_ready, 4)
                    pe.wait_ge(mixed_out, QT)
                    pe.wait_ge(dt_dve, 2)
                    upto = const("upto")
                    pe.matmul(bank(6)[:, 0:QT * HEADS], upto, dt_a[:, 0:QT * HEADS], start=True, stop=True)\
                      .then_inc(dt_pe, 1)
                    for h in range(HEADS):
                        for c in range(QT):
                            last = pe.matmul(bank(h)[:, c * P:(c + 1) * P],
                                             dt_a[:, c * HEADS + h:c * HEADS + h + 1].broadcast_to([P, P]), upto,
                                             start=True, stop=True)
                        last.then_inc(dt_pe, 1)
                    for c in range(2):
                        pick = const("state_rows")[0:HEADS, c * P:(c + 1) * P]
                        for q in range(2):
                            pe.transpose(bank(7)[:, 16 * q + 8 * c:16 * q + 8 * c + 8],
                                         dt_rows[:, q, 2 * c:2 * c + 2, :].rearrange("p h c -> p (h c)"), ident[0:NS, 0:NS])
                        last = pe.matmul(bank(7)[:, 32 + c:33 + c],
                                         pick,
                                         d_skip4[0:HEADS, :], start=True, stop=True)
                    last.then_inc(dt_pe, 1)
                    pe.wait_ge(conv_d_act, 6)
                    for gr in range(2):
                        for c in range(QT):
                            last = pe.matmul(bank(4 + gr)[:, c * P:(c + 1) * P], dc[:, 2 + gr, c * P:(c + 1) * P],
                                             dc[:, 4 + gr, c * P:(c + 1) * P], start=True, stop=True)
                    last.then_inc(ssd_pe, 1)
                    pe.wait_ge(dt_dve, 3)
                    for c in range(QT):
                        to = bank(6 + c % 2)
                        if c >= 2:
                            pe.wait_ge(ssd_act, c - 1 + HEADS)
                        for q in range(4):
                            last = pe.transpose(to[:, q * P:(q + 1) * P], dc[:, q, c * P:(c + 1) * P], ident)
                        last.then_inc(ssd_pe, 1)
                    pe.wait_ge(ssd_act, HEADS + QT)
                    for c in range(QT):
                        pe.wait_ge(ssd_dve, c + 1)
                        if c >= 2:
                            pe.wait_ge(state_dve, c - 1)
                        for h in range(HEADS):
                            gr = h // 2
                            last = pe.matmul(bank(6 + c % 2)[:, h * HD:(h + 1) * HD],
                                             xb_tok[:, c, W + gr * P:W + (gr + 1) * P],
                                             xw[:, c, h * HD:(h + 1) * HD], start=True, stop=True)
                        last.then_inc(state_pe, 1)
                        if c == 0:
                            pe.wait_ge(ssd_dve, QT + 1)
                        if c >= 1:
                            pe.wait_ge(state_dve, c)
                        for h in range(HEADS):
                            r = HD * (h % 2)
                            to = bank(2 + h // 2)[r:r + HD, c * P:(c + 1) * P]
                            last = pe.matmul(to, xb_tok[:, c, h * HD:(h + 1) * HD], decay[:, h * QT + c, :],
                                             start=True, stop=(c == 0))
                            if c >= 1:
                                last = pe.matmul(to, h_t[:, h, :], read_c[:, h, c * P:(c + 1) * P], start=False, stop=True)
                        last.then_inc(state_pe, 1)
                        if c == 1:
                            pe.wait_ge(cln_dve, 1)
                            pe.wait_ge(conv_c_done, 2)
                            for k in range(2):
                                for h in range(2):
                                    last = pe.matmul(pair(0)[:, h, :], ones, feat[:, GG + k, h * HALF:(h + 1) * HALF],
                                                     start=(k == 0), stop=(k == 1))
                            last.then_inc(cln_pe, 1)
                    pe.wait_ge(cln_act, 2)
                    for k in range(2):
                        for h in range(2):
                            last = pe.matmul(pair(0)[:, h, :], ones, temp[:, k, h * HALF:(h + 1) * HALF],
                                             start=(k == 0), stop=(k == 1))
                    last.then_inc(cln_pe, 1)
                    pe.wait_ge(state_dve, QT)
                    for c in range(2):
                        last = pe.transpose(bank(6)[:, c * P:(c + 1) * P],
                                            h_t.rearrange("p h c -> p (h c)")[:, c * P:(c + 1) * P], ident)
                    last.then_inc(state_pe, 1)
                    for q in range(4):
                        last = pe.transpose(bank(4)[0:NS, q * P:(q + 1) * P], dc[:, 2 + q, SEQ:T], ident)
                    last.then_inc(decd_pe, 1)
                    pe.wait_ge(decd_dve, 1)
                    for b in range(NS):
                        if b >= 2:
                            pe.wait_ge(decd_dve, b)
                        pe.matmul(bank(4 + b % 2), ident[0:NS, b:b + 1].broadcast_to([NS, P]), bc_rows,
                                  start=True, stop=True).then_inc(decd_pe, 1)
                    pe.wait_ge(dn_act, 2)
                    for c in range(2):
                        for h in range(2):
                            last = pe.matmul(pair(1)[:, h, :], ones, temp[:, 2 + c, h * HALF:(h + 1) * HALF],
                                             start=(c == 0), stop=(c == 1))
                    last.then_inc(dn_pe, 1)

                    def split_product(to, part, a_hi, a_lo, ks, first, last):
                        whi, wlo = w_hi[part % 2], w_lo[part % 2]
                        for n, k in enumerate(ks):
                            begin, end = first and n == 0, last and n == len(ks) - 1
                            for w, a in ((whi, a_hi), (whi, a_lo), (wlo, a_hi)):
                                for h in range(2):
                                    ins = pe.matmul(to[:, h, :], w[:, n, :], a[k][:, h * HALF:(h + 1) * HALF],
                                                    start=(begin and w is whi and a is a_hi), stop=(end and w is wlo))
                        return ins

                    pe.wait_ge(cln_act, 3)
                    pe.wait_ge(dn_act, 3)
                    pe.wait_ge(y_lo_ready, KC)
                    chunks = lambda t, n=KC: [t[:, k, :] for k in range(n)]
                    for m in range(KC):
                        if m >= 4:
                            pe.wait_ge(out_ready, 2 * (m - 3))
                        pe.wait_ge(part_lo, m + 1)
                        split_product(pair(m % 4), m, chunks(u_hi), [t[:, 0, :] for t in y_lo], range(KC), True, True)\
                            .then_inc(out_summed, 1)
                    pe.wait_ge(out_ready, 2 * 5)
                    sum_squares(pair(0), out_ready, 0, 2)
                    pe.wait_ge(out_ready, 2 * 6)
                    sum_squares(pair(1), squares_ready, KC, 1)

                    pe.wait_ge(out_ready, 2 * KC)
                    pe.wait_ge(root_ready, 3)
                    pe.wait_ge(u_lo_ready, KC)
                    with pe.Fori(0, FFC // 2) as i:
                        for c in range(2):
                            for q, summed in ((0, gate_summed), (1, up_summed)):
                                pe.wait_ge(part_lo, i * 4 + (GU0 + 2 * c + q + 1))
                                split_product(pair(2 * c + q), q, chunks(u_hi), chunks(u_lo), range(KC), True, True).then_inc(summed, 1)

                    pe.wait_ge(hidden_lo, FFC)
                    with pe.Fori(0, KC // 2) as i:
                        for c in range(2):
                            pe.wait_ge(down_ready, i * 4 + (2 * c + 2))
                            for q, (k, n) in enumerate(DOWN_PARTS):
                                pe.wait_ge(part_lo, i * 8 + (DN0 + 4 * c + q + 1))
                                split_product(pair(c), q, chunks(hid_hi, FFC), chunks(hid_lo, FFC), range(k, k + n), q == 0, q == 3)\
                                    .then_inc(down_part, 1)
                    sum_squares(pair(2), down_ready, 4, 2, ffn_squares)

                @block.scalar
                def _(act):
                    def root_of(n, sums, scale, eps):
                        act.wait_ge(sums_ready, n + 1)
                        act.activation(halves(root[:, :]), sums, ACT.Sqrt, bias=const("eps")[:, eps:eps + 1], scale=scale)\
                           .then_inc(root_ready, 1)

                    for k in range(KC):
                        act.activation(squares[:, k, :], x[:, k, :], ACT.Square).then_inc(squares_ready, 1)
                    root_of(0, pair(0), 1.0 / D_MODEL, 0)

                    g = 0
                    act.wait_ge(dt_dve, 1)
                    for s in range(N_TOK):
                        w = W if s < 4 else ID + IH
                        for t in range(QT + 1):
                            act.wait_ge(tok_summed, g + 1)
                            if t < QT:
                                to = (tok_q, tok_k, tok_v, tok_qi, kiw)[s][:, t, :]
                            else:
                                to = tok8[:, s * W:s * W + w]
                            if s == 4:
                                m = to.shape[0]
                                act.copy(dt_v[0:m, t * HEADS:(t + 1) * HEADS], bank(2 + g % 6)[0:m, w:w + HEADS])
                            act.copy(to, bank(2 + g % 6)[0:to.shape[0], 0:w]).then_inc(tok_ready, 1)
                            g += 1
                    for j in range(7):
                        act.wait_ge(turn_done, j + 1)
                        act.copy(turned[:, j, :], bank(j)).then_inc(turned_ready, 1)

                    feat_i = [0]

                    def feature_out(upto):
                        while feat_i[0] < upto:
                            i = feat_i[0]
                            n, s, c = feat_tiles[i]
                            act.wait_ge(feat_summed, i + 1)
                            func = {GG // 2: ACT.Sigmoid, ZG // 2: ACT.Silu}.get(s, ACT.Copy)
                            act.activation(halves(feat[:, 2 * s + c, :]), pair(i % 2), func).then_inc(feat_ready, 1)
                            feat_i[0] += 1

                    act.wait_ge(dt_low, 1)
                    act.activation(dt_e, dt_e, ACT.Exp).then_inc(dt_exp, 1)
                    act.activation(head_all[:, 1, :], head_all[:, 1, :], ACT.Exp).then_inc(dt_exp, 1)
                    feature_out(6)
                    act.wait_ge(dec_max, 1)
                    act.activation(p_row[0:32, :], l_row[0:32, :], ACT.Exp, bias=stat8[0:32, 1:2], scale=HD ** -0.5,
                                   accum_out=stat8[0:32, 2:3]).then_inc(dec_exp, 1)
                    feature_out(8)
                    act.wait_ge(dec_pe, 4)
                    for hp in range(2):
                        o = bank(4 + hp)[:, 0:32].rearrange("p (b h) -> p b h", h=HEADS)
                        for q in range(2):
                            act.copy(ya[HD * q:HD * (q + 1), hp, SEQ:T], o[HD * q:HD * (q + 1), :, 2 * hp + q])\
                               .then_inc(dec_out, 1)
                    for n, (blk, h) in enumerate(IDX):
                        keys = (blk + 1) * P
                        act.wait_ge(idx_summed, n + 1)
                        if n >= 2:
                            act.wait_ge(idx_added, n - 1)
                        act.activation(rect[:, n % 2, 0:keys], bank(4 + n % 4)[:, 0:keys], ACT.Relu,
                                       scale=(ID * IH) ** -0.5).then_inc(idx_rect, 1)
                    feature_out(len(feat_tiles))
                    act.wait_ge(conv_d_done, 1)
                    for c in range(6):
                        act.activation(dc[:, c, :], dc[:, c, :], ACT.Silu).then_inc(conv_d_act, 1)
                    act.wait_ge(tails_turned, 1)
                    act.copy(tail_b[0:10, :], bank(0)[0:10, 0:W]).then_inc(tails_ready, 1)
                    act.copy(tail_c[0:38, :], bank(0)[0:38, W:2 * W]).then_inc(tails_ready, 1)
                    act.copy(tail_d[0:11, 0:512], bank(1)[0:11, :]).then_inc(tails_ready, 1)
                    act.copy(tail_d[0:11, 512:768], bank(2)[0:11, 0:W]).then_inc(tails_ready, 1)
                    def upper(part, free, value, turn, n=KC):
                        act.wait_ge(raw_in[part % 4], turn)
                        act.wait_ge(free, value)
                        act.copy(w_hi[part % 2][:, 0:n, :], raw[part % 4][:, 0:n, :]).then_inc(part_hi, 1)

                    for n in range(2):
                        upper(n, feat_summed, len(feat_tiles), 16)

                    def y_upper(k, source):
                        act.copy(u_hi[:, k:k + 2, :], source).then_inc(y_hi_ready, 1)

                    for j in range(len(STEPS) + 1):
                        if j < len(STEPS):
                            blk, h = STEPS[j]
                            keys = (blk + 1) * P
                            act.wait_ge(logits_masked, j + 1)
                            act.activation(rect[:, j % 2, 0:keys], rect[:, j % 2, 0:keys], ACT.Exp,
                                           bias=neg_max[:, j % 2:j % 2 + 1], scale=HD ** -0.5,
                                           accum_out=denom[:, j % 2:j % 2 + 1]).then_inc(exp_done, 1)
                        if j >= 1:
                            i = j - 1
                            blk, h = STEPS[i]
                            keys = (blk + 1) * P
                            act.wait_ge(prob_turned, i + 1)
                            if i >= 2:
                                act.wait_ge(mixed, i - 1)
                            act.copy(prob_t[:, i % 2, 0:keys], bank(6)[:, 0:keys]).then_inc(prob_t_ready, 1)
                            if h == HEADS - 1:
                                act.wait_ge(mixed, i + 1)
                                act.copy(ya[:, :, blk * P:(blk + 1) * P],
                                         view(PS[:, 7, :], (blk % 2) * W, 2, P)).then_inc(mixed_out, 1)
                    for h in range(HEADS):
                        act.wait_ge(dt_pe, 2 + h)
                        act.activation(ecs[:, h, :], bank(h), ACT.Exp).then_inc(ssd_act, 1)
                    act.wait_ge(dt_dve, 3)
                    act.activation(edt[:, 0], edt[:, 0], ACT.Exp).then_inc(dt_exp, 1)
                    act.wait_ge(dt_dve, 4)
                    act.activation(w_end, w_end, ACT.Exp).then_inc(dt_exp, 1)
                    for c in range(QT):
                        act.wait_ge(ssd_pe, 2 + c)
                        act.copy(xb_tok[:, c, :], bank(6 + c % 2)).then_inc(ssd_act, 1)
                    for h in range(HEADS):
                        act.wait_ge(segments, h + 1)
                        act.activation(decay[:, QT * h:QT * (h + 1), :], decay[:, QT * h:QT * (h + 1), :], ACT.Exp)\
                           .then_inc(ssd_act, 1)
                    act.wait_ge(mixed_out, QT)
                    y_upper(0, ya[:, :, :])
                    act.wait_ge(b_done, 2)
                    y_upper(2, feat[:, BX:BX + 2, :])
                    act.wait_ge(cln_dve, 2)
                    for c in range(2):
                        act.activation(temp[:, c, :], feat[:, GG + c, :], ACT.Square).then_inc(cln_act, 1)
                    act.wait_ge(cln_pe, 2)
                    act.activation(halves(root[:, :]), pair(0), ACT.Sqrt, bias=const("eps")[:, 1:2], scale=1.0 / W)\
                       .then_inc(cln_act, 1)
                    act.wait_ge(cln_dve, 5)
                    for c in range(2):
                        act.activation(feat[:, GG + c, :], feat[:, GG + c, :], ACT.Silu, bias=pcol("cln_b", c))\
                           .then_inc(cln_act, 1)
                    act.wait_ge(tails_stored, layer * (16 * N_TAILS) + 16 * N_TAILS)
                    act.wait_ge(cln_act, 5)
                    y_upper(4, feat[:, GG:GG + 2, :])
                    act.wait_ge(dn_dve, 1)
                    for c in range(2):
                        act.activation(temp[:, 2 + c, :], feat[:, ZG + c, :], ACT.Square).then_inc(dn_act, 1)
                    act.wait_ge(dn_pe, 1)
                    act.activation(halves(root[:, :]), pair(1), ACT.Sqrt, bias=const("eps")[:, 0:1], scale=1.0 / W)\
                       .then_inc(dn_act, 1)
                    act.wait_ge(dn_dve, 3)
                    y_upper(6, feat[:, ZG:ZG + 2, :])
                    for m in range(KC):
                        act.wait_ge(out_summed, m + 1)
                        upper(m + 2, out_summed, m + 1, 16 * ((m + 2) // 4 + 1))
                        act.copy(halves(mix[:, m, :]), pair(m % 4)).then_inc(out_ready, 1)
                        act.activation(halves(squares[:, m, :]), pair(m % 4), ACT.Square).then_inc(out_ready, 1)
                    root_of(1, pair(0), 1.0 / D_MODEL, 0)

                    for k in range(KC):
                        act.wait_ge(x_updated, k + 1)
                        act.activation(squares[:, k, :], x[:, k, :], ACT.Square).then_inc(squares_ready, 1)
                    root_of(2, pair(1), 1.0 / D_MODEL, 0)
                    for k in range(KC):
                        act.wait_ge(u_scaled, k + 1)
                        act.copy(u_hi[:, k, :], scaled[:, k, :]).then_inc(u_hi_ready, 1)
                    act.wait_ge(stored, layer * (16 * N_SSM) + 16 * N_SSM)

                    def hidden_tile(i, c, next_n):
                        for q, summed in ((0, gate_summed), (1, up_summed)):
                            part = GU0 + 2 * c + q + 2
                            upper(part, summed, i * 2 + (c + 1), i * 16 + 16 * (part // 4 + 1), next_n)
                            if q == 0:
                                act.activation(halves(hid_gate[:, c, :]), pair(2 * c), ACT.Silu).then_inc(gate_ready, 1)
                        act.wait_ge(hidden_made, i * 2 + (c + 1))
                        act.copy(hid_hi[:, bass.ds(i * 2 + c, 1), :], hid_f[:, c:c + 1, :]).then_inc(hidden_hi, 1)

                    with act.Fori(0, FFC // 2 - 1) as i:
                        for c in range(2):
                            hidden_tile(i, c, KC)
                    hidden_tile(FFC // 2 - 1, 0, KC)
                    hidden_tile(FFC // 2 - 1, 1, DOWN_PARTS[0][1])
                    act.sem_inc(down_ready, 4)

                    def down_tile(i, c, parts):
                        for q in parts:
                            part = DN0 + 4 * c + q + 2
                            upper(part, down_part, i * 8 + (4 * c + q + 1), i * 32 + 16 * (part // 4 + 1),
                                  DOWN_PARTS[part % 4][1])
                        act.wait_ge(down_part, i * 8 + (4 * c + 4))
                        act.copy(u[:, bass.ds(i * 2 + c, 1), :].rearrange("p o (h n) -> p (o h) n", h=2), pair(c))\
                           .then_inc(down_ready, 1)
                        act.activation(ffn_squares[:, bass.ds(i * 2 + c, 1), :].rearrange("p o (h n) -> p (o h) n", h=2),
                                       pair(c), ACT.Square).then_inc(down_ready, 1)

                    with act.Fori(0, KC // 2 - 1) as i:
                        down_tile(i, 0, range(4))
                        down_tile(i, 1, range(4))
                    down_tile(KC // 2 - 1, 0, range(4))
                    down_tile(KC // 2 - 1, 1, range(2))
                    root_of(3, pair(2), 1.0 / D_MODEL, 0)

                @block.vector
                def _(dve):
                    made = [0]

                    def step(ins):
                        ins.then_inc(vec, 1)
                        made[0] += 1

                    def settle():
                        dve.wait_ge(vec, made[0])

                    def normalise(n, source, gain, to):
                        dve.wait_ge(root_ready, n + 1)
                        step(dve.reciprocal(rstd[:, :], root[:, :]))
                        settle()
                        for k in range(KC):
                            dve.scalar_tensor_tensor(to[:, k, :], source[:, k, :], pcol(gain, k), rstd[:, :], ALU.mult, ALU.mult)\
                               .then_inc(normed, 1)

                    dve.tensor_copy(par[:, :, :], all_par[:, bass.ds(layer, 1), :]).then_inc(params_ready, 1)
                    dve.wait_ge(params_ready, 1)
                    dve.memset(dt_v[:, QT * HEADS:], 0.0).then_inc(dt_dve, 1)
                    normalise(0, x, "g_pre_mix", u)
                    def rope(v, heads, rot, tables, p, blocks):
                        half = rot // 2
                        n = blocks * heads
                        a = rope_a[0:p, 0:n * rot].rearrange("p (t h r) -> p t h r", h=heads, r=rot)
                        b = rope_b[0:p, 0:n * rot].rearrange("p (t h r) -> p t h r", h=heads, r=rot)
                        tabs = [const(x)[0:p].rearrange("p (t r) -> p t r", t=blocks).unsqueeze(2) for x in tables]
                        full, part = [p, blocks, heads, rot], [p, blocks, heads, half]
                        for t in range(blocks):
                            step(dve.tensor_tensor(a[:, t], v[:, t], tabs[0][:, t].broadcast_to([p, heads, rot]), ALU.mult))
                            step(dve.tensor_tensor(b[:, t, :, 0:half], v[:, t, :, half:rot],
                                                   tabs[1][:, t].broadcast_to([p, heads, half]), ALU.mult))
                            step(dve.tensor_tensor(b[:, t, :, half:rot], v[:, t, :, 0:half],
                                                   tabs[2][:, t].broadcast_to([p, heads, half]), ALU.mult))
                        settle()
                        for t in range(blocks):
                            last = dve.tensor_tensor(v[:, t], a[:, t], b[:, t], ALU.add)
                            if t < blocks - 1:
                                step(last)
                        return last

                    def take_states():
                        dve.wait_ge(states_turned, 1)
                        dve.tensor_copy(ctx_c[:, :, :, 0:C_CONV - 1].rearrange("p c b t -> p (c b) t"),
                                        view(PS[:, 0, :], 0, 2 * NS, C_CONV - 1)).then_inc(states_ready, 1)
                        dve.tensor_copy(ctx_b[:, :, :, 0:2].rearrange("p c b t -> p (c b) t"),
                                        view(PS[:, 1, :], 0, 2 * NS, 2)).then_inc(states_ready, 1)
                        dve.tensor_copy(ctx_d[:, :, :, 0:3].rearrange("p c b t -> p (c b) t"),
                                        view(PS[:, 1, :], 32, 6 * NS, 3)).then_inc(states_ready, 1)
                        dve.tensor_copy(head_all.rearrange("p q h -> p (q h)"), PS[:, 1, 256:256 + 2 * HEADS]).then_inc(states_ready, 1)

                    tab, tab_i = ("cos", "nsin", "sin"), ("cos_i", "nsin_i", "sin_i")
                    for s, (t, heads, width, rot, tb) in ((0, (tok_q, HEADS, HD, 16, tab)), (1, (tok_k, HEADS, HD, 16, tab)),
                                                          (3, (tok_qi, IH, ID, 8, tab_i)), (4, (kiw, 1, ID, 8, tab_i))):
                        if s == 3:
                            take_states()
                        dve.wait_ge(tok_ready, 5 * s + 4)
                        v = t[:, :, 0:heads * width].rearrange("p t (h c) -> p t h c", c=width)[:, :, :, 0:rot]
                        ins = rope(v, heads, rot, tb, P, QT)
                        if s < 4:
                            ins.then_inc(rope_done, 1)
                            dve.wait_ge(rope_done, 1 + (0, 1, None, 2)[s])
                        else:
                            step(ins)
                            settle()
                            dve.tensor_copy(ki_four, kiw[:, :, 0:ID].unsqueeze(2).broadcast_to([P, QT, 4, ID]))\
                               .then_inc(rope_done, 1)
                    dve.wait_ge(tok_ready, 25)
                    for at, heads, width, rot, tb in ((0, 2 * HEADS, HD, 16, ("cos_d", "nsin_d", "sin_d")),
                                                      (3 * W, IH + 1, ID, 8, ("cos_id", "nsin_id", "sin_id"))):
                        v = tok8[:, at:at + heads * width].rearrange("p (t h c) -> p t h c", t=1, c=width)[:, :, :, 0:rot]
                        step(rope(v, heads, rot, tb, NS, 1))
                        settle()
                    dve.tensor_scalar(tok8[:, TOK_W - IH:TOK_W], tok8[:, TOK_W - IH:TOK_W], (ID * IH) ** -0.5, None, ALU.mult)\
                       .then_inc(rope_done, 1)
                    dve.wait_ge(rope_done, 5)
                    def per_head(t):
                        return t.rearrange("p (b h) -> p b h", h=HEADS)

                    blocks = [P, QT + 1, HEADS]
                    dve.wait_ge(states_ready, 4)
                    step(dve.tensor_tensor(per_head(dt_v), per_head(dt_v), head_all[:, 0:1, :].broadcast_to(blocks), ALU.add))
                    settle()
                    dve.scalar_tensor_tensor(dt_e, dt_v, -1.0, dt_v, ALU.mult, ALU.min).then_inc(dt_low, 1)

                    dve.wait_ge(k_cache_in, 16 * 2 * NS)
                    dve.wait_ge(ki_cache_in, 16 * 2 * NS)
                    for b in range(NS):
                        qb, ib = bank(4 + 2 * (b % 2)), bank(5 + 2 * (b % 2))
                        dve.wait_ge(rows_spread, b + 1)
                        kb = k_cache[:, 2 * b:2 * b + 2, :]
                        step(dve.tensor_tensor(kb, kb, qb[:, 0:W].unsqueeze(1).broadcast_to([P, 2, W]), ALU.mult))
                        pi = prod_i.rearrange("p (g h c) -> p g h c", g=2, c=ID)
                        for pg in range(2):
                            step(dve.tensor_tensor(pi[:, pg], ki_cache[:, 2 * b + pg, :].unsqueeze(1).broadcast_to([P, IH, ID]),
                                                   ib[:, 0:W].rearrange("p (h c) -> p h c", c=ID), ALU.mult))
                        settle()
                        step(dve.tensor_reduce(past_l[:, :, b, :], kb.rearrange("p g (h c) -> p g h c", c=HD), AX.X, ALU.add))
                        s16 = sc64[:, 0:16].rearrange("p (g h) -> p g h", g=2)
                        step(dve.tensor_reduce(s16, pi, AX.X, ALU.add))
                        settle()
                        dve.scalar_tensor_tensor(s16, s16, 0.0, ib[:, W + ID:W + ID + IH].unsqueeze(1).broadcast_to([P, 2, IH]),
                                                 ALU.max, ALU.mult).then_inc(rows_used, 1)
                        dve.wait_ge(rows_used, b + 1)
                        step(dve.tensor_reduce(past_s[:, :, b], s16, AX.X, ALU.add))
                    q8, k8 = tok8[:, 0:W], tok8[:, W:2 * W]
                    settle()
                    step(dve.tensor_tensor(prod8[0:NS, :], q8, k8, ALU.mult))
                    settle()
                    step(dve.tensor_reduce(m_row[0:NS, 257:261], prod8[0:NS, :].rearrange("p (h c) -> p h c", c=HD), AX.X, ALU.add))
                    settle()
                    step(dve.tensor_tensor(prod8[0:NS, :].rearrange("p (h c) -> p h c", c=ID),
                                           tok8[:, 3 * W:4 * W].rearrange("p (h c) -> p h c", c=ID),
                                           tok8[:, 4 * W:4 * W + ID].unsqueeze(1).broadcast_to([NS, IH, ID]), ALU.mult))
                    settle()
                    step(dve.tensor_reduce(sc64[0:NS, 16:24], prod8[0:NS, :].rearrange("p (h c) -> p h c", c=ID), AX.X, ALU.add))
                    settle()
                    step(dve.scalar_tensor_tensor(sc64[0:NS, 24:32], sc64[0:NS, 16:24], 0.0, tok8[:, TOK_W - IH:TOK_W],
                                                  ALU.max, ALU.mult))
                    settle()
                    dve.tensor_reduce(s_row[0:NS, 256:257], sc64[0:NS, 24:32], AX.X, ALU.add).then_inc(dec_dve, 1)
                    dve.wait_ge(dt_exp, 1)
                    step(dve.tensor_scalar(dt_s, dt_e, 2.0, None, ALU.add))
                    settle()
                    step(dve.reciprocal(dt_s, dt_s))
                    settle()
                    step(dve.tensor_tensor(dt_s, dt_s, dt_e, ALU.mult))
                    settle()
                    step(dve.tensor_tensor(dt_z, dt_s, dt_s, ALU.mult))
                    settle()
                    step(dve.tensor_scalar(dt_q, dt_z, 1.0 / 15.0, None, ALU.mult))
                    for n in (13, 11, 9, 7, 5, 3):
                        settle()
                        step(dve.scalar_tensor_tensor(dt_q, dt_q, 1.0 / n, dt_z, ALU.add, ALU.mult))
                    settle()
                    step(dve.scalar_tensor_tensor(dt_q, dt_q, 1.0, dt_s, ALU.add, ALU.mult))
                    step(dve.tensor_scalar(dt_v, dt_v, 0.0, None, ALU.max))
                    settle()
                    step(dve.scalar_tensor_tensor(dt_q, dt_q, 2.0, dt_v, ALU.mult, ALU.add))
                    settle()
                    dve.wait_ge(dt_exp, 2)
                    step(dve.scalar_tensor_tensor(per_head(dt_a), per_head(dt_q), -1.0, head_all[:, 1:2, :].broadcast_to(blocks),
                                                  ALU.mult, ALU.mult))
                    settle()
                    for q, t in ((0, dt_a), (1, dt_q)):
                        last = dve.tensor_copy(dt_rows[:, q], t[0:NS, QT * HEADS:].unsqueeze(2).broadcast_to([NS, HEADS, HD]))
                        if q == 0:
                            step(last)
                    last.then_inc(dt_dve, 1)
                    dve.wait_ge(dec_pe, 1)
                    step(dve.tensor_copy(s_row[0:NS, 0:256], bank(4)[0:NS, 0:256]))
                    step(dve.tensor_copy(l_row[0:32, 0:256], bank(5)[0:32, 0:256]))
                    dve.wait_ge(dec_dve, 1)
                    for r in range(TOPK_SAMPLE // 8):
                        settle()
                        step(dve.max(best8[0:NS, :], s_row[0:NS, :]))
                        settle()
                        step(dve.match_replace(s_row[0:NS, :], best8[0:NS, :], s_row[0:NS, :], TAKEN))
                    settle()
                    dve.tensor_scalar(m_row[0:NS, 0:257], s_row[0:NS, :], TAKEN, MASKED, ALU.not_equal, ALU.mult)\
                       .then_inc(dec_dve, 1)
                    dve.wait_ge(dec_pe, 2)
                    step(dve.tensor_tensor(sc64[0:32, 32:36], bank(6)[0:32, 257:261], const("head_of_row")[0:32, :], ALU.mult))
                    settle()
                    step(dve.tensor_reduce(l_row[0:32, 256:257], sc64[0:32, 32:36], AX.X, ALU.add))
                    settle()
                    step(dve.tensor_tensor(l_row[0:32, :], l_row[0:32, :], bank(6)[0:32, 0:257], ALU.add))
                    settle()
                    step(dve.tensor_reduce(stat8[0:32, 0:1], l_row[0:32, :], AX.X, ALU.max))
                    settle()
                    dve.tensor_scalar(stat8[0:32, 1:2], stat8[0:32, 0:1], -HD ** -0.5, None, ALU.mult).then_inc(dec_max, 1)
                    dve.wait_ge(dec_exp, 1)
                    step(dve.reciprocal(stat8[0:32, 3:4], stat8[0:32, 2:3]))
                    settle()
                    step(dve.tensor_scalar(p_row[0:32, :], p_row[0:32, :], stat8[0:32, 3:4], None, ALU.mult))
                    settle()
                    dve.tensor_scalar(self_p[0:32, :], const("sample_of_row")[0:32, :], p_row[0:32, 256:257], None, ALU.mult)\
                       .then_inc(dec_dve, 1)
                    dve.wait_ge(dec_pe, 3)
                    step(dve.tensor_copy(p_col.rearrange("p g m -> p (g m)"), bank(7)[:, 0:64]))
                    dve.tensor_copy(self_pt[0:NS, :], bank(7)[0:NS, 64:96]).then_inc(dec_dve, 1)

                    for n, (blk, h) in enumerate(IDX):
                        keys = (blk + 1) * P
                        w = kiw[:, blk, ID + h:ID + h + 1]
                        s = score[:, blk - 1, 0:keys]
                        dve.wait_ge(idx_rect, n + 1)
                        if h == 0:
                            dve.tensor_scalar(s, rect[:, n % 2, 0:keys], w, None, ALU.mult).then_inc(idx_added, 1)
                        else:
                            dve.wait_ge(idx_added, n)
                            dve.scalar_tensor_tensor(s, rect[:, n % 2, 0:keys], w, s, ALU.mult, ALU.add).then_inc(idx_added, 1)
                    dve.wait_ge(idx_added, len(IDX))
                    for blk in range(1, QT):
                        own = score[:, blk - 1, blk * P:(blk + 1) * P]
                        step(dve.tensor_tensor(own, own, const("future"), ALU.add))
                    def conv8(to, window, name, taps, chunks, scratch, bias):
                        w = par[:, 0, AT[name]:AT[name] + taps * chunks].rearrange("p (t c) -> p c t", c=chunks)
                        pr = scratch[:, 0:chunks * NS * taps].rearrange("p (c b t) -> p c b t", b=NS, t=taps)
                        for c in range(chunks):
                            step(dve.tensor_tensor(pr[:, c], window[:, c], w[:, c].unsqueeze(1).broadcast_to([P, NS, taps]), ALU.mult))
                        settle()
                        for c in range(chunks):
                            step(dve.tensor_reduce(to[:, c, SEQ:T], pr[:, c], AX.X, ALU.add))
                        settle()
                        if bias is not None:
                            for c in range(chunks):
                                step(dve.tensor_scalar(to[:, c, SEQ:T], to[:, c, SEQ:T], pcol(bias, c), None, ALU.add))
                            settle()

                    def gate_c():
                        dve.wait_ge(feat_ready, feat_count(GA, GA + 1, GG, GG + 1))
                        for c in range(2):
                            dve.tensor_tensor(feat[:, GA + c, :], feat[:, GA + c, :], feat[:, GG + c, :], ALU.mult).then_inc(gate_in, 1)
                        dve.wait_ge(gate_in, 2)
                        for c in range(2):
                            step(dve.tensor_copy(ctx_c[:, c, :, C_CONV - 1], feat[:, GA + c, SEQ:T]))
                        settle()
                        conv8(feat[:, GG:GG + 2, :], ctx_c, "cconv_w", C_CONV, 2, prod_i, "cconv_b")
                        dve.sem_inc(cln_dve, 1)

                    for r in range(TOPK_PROMPT // 8):
                        if r == 6:
                            gate_c()
                        settle()
                        for blk in range(1, QT):
                            step(dve.max(chunk_best[:, blk - 1, :], score[:, blk - 1, 0:(blk + 1) * P]))
                        settle()
                        for blk in range(1, QT):
                            s = score[:, blk - 1, 0:(blk + 1) * P]
                            step(dve.match_replace(s, chunk_best[:, blk - 1, :], s, TAKEN))
                    settle()
                    for blk in range(1, QT):
                        s = score[:, blk - 1, 0:(blk + 1) * P]
                        step(dve.tensor_scalar(s, s, TAKEN, MASKED, ALU.not_equal, ALU.mult))
                    settle()

                    def conv(to, source, name, chunk, taps, bias, chunks):
                        w = lambda tap: pcol(name, tap * chunks + chunk)
                        if bias is None:
                            step(dve.tensor_scalar(to[:, 0:SEQ], source[:, 0:SEQ], w(taps - 1), None, ALU.mult))
                        else:
                            step(dve.tensor_scalar(to[:, 0:SEQ], source[:, 0:SEQ], w(taps - 1), bias, ALU.mult, ALU.add))
                        for back in range(1, taps):
                            settle()
                            step(dve.scalar_tensor_tensor(to[:, back:SEQ], source[:, 0:SEQ - back], w(taps - 1 - back),
                                                          to[:, back:SEQ], ALU.mult, ALU.add))

                    dve.wait_ge(feat_ready, feat_count(*range(XBC, XBC + 6)))
                    for c in range(6):
                        step(dve.tensor_copy(ctx_d[:, c, :, D_CONV - 1], feat[:, XBC + c, SEQ:T]))
                    settle()
                    conv8(dc, ctx_d, "dconv_w", D_CONV, 6, prod_i, "dconv_b")
                    for c in range(6):
                        conv(dc[:, c, :], feat[:, XBC + c, :], "dconv_w", c, D_CONV, pcol("dconv_b", c), 6)
                    settle()
                    dve.sem_inc(conv_d_done, 1)

                    dve.wait_ge(dec_pe, 4)
                    dve.wait_ge(feat_ready, feat_count(GC, GC + 1, BX, BX + 1, GB, GB + 1))
                    for c in range(2):
                        dve.tensor_tensor(feat[:, GC + c, :], feat[:, GC + c, :], feat[:, BX + c, :], ALU.mult).then_inc(gate_in, 1)
                    dve.wait_ge(gate_in, 4)
                    for c in range(2):
                        step(dve.tensor_copy(ctx_b[:, c, :, B_CONV - 1], feat[:, GC + c, SEQ:T]))
                    settle()
                    conv8(feat[:, BX:BX + 2, :], ctx_b, "bconv_w", B_CONV, 2, prod_i, None)
                    for c in range(2):
                        conv(feat[:, BX + c, :], feat[:, GC + c, :], "bconv_w", c, B_CONV, None, 2)
                    settle()
                    for c in range(2):
                        dve.tensor_tensor(feat[:, BX + c, :], feat[:, BX + c, :], feat[:, GB + c, :], ALU.mult).then_inc(b_done, 1)

                    taps_left = list(range(C_CONV))

                    def conv_c_tap():
                        back = taps_left.pop(0)
                        w = pcol("cconv_w", 2 * (C_CONV - 1 - back))
                        acc = feat[:, GG, back:SEQ]
                        if back:
                            settle()
                            step(dve.scalar_tensor_tensor(acc, feat[:, GA, 0:SEQ - back], w, acc, ALU.mult, ALU.add))
                        else:
                            step(dve.tensor_scalar(acc, feat[:, GA, 0:SEQ], w, pcol("cconv_b", 0), ALU.mult, ALU.add))

                    for j in range(len(STEPS) + 1):
                        if j < len(STEPS):
                            blk, h = STEPS[j]
                            keys = (blk + 1) * P
                            dve.wait_ge(logits_summed, j + 1)
                            if j >= 2:
                                dve.wait_ge(prob_turned, j - 1)
                            mask = const("future") if blk == 0 else score[:, blk - 1, 0:keys]
                            step(dve.tensor_tensor_reduce(rect[:, j % 2, 0:keys], bank(3 + j % 3)[:, 0:keys], mask, 1.0, MASKED,
                                                          ALU.add, ALU.max, top_max[:, j % 2:j % 2 + 1]))
                            settle()
                            dve.tensor_scalar(neg_max[:, j % 2:j % 2 + 1], top_max[:, j % 2:j % 2 + 1], -HD ** -0.5, None,
                                              ALU.mult).then_inc(logits_masked, 1)
                        if j >= 1:
                            i = j - 1
                            blk, h = STEPS[i]
                            keys = (blk + 1) * P
                            b2 = slice(i % 2, i % 2 + 1)
                            dve.wait_ge(exp_done, i + 1)
                            step(dve.reciprocal(rden[:, b2], denom[:, b2]))
                            settle()
                            dve.tensor_scalar(rect[:, i % 2, 0:keys], rect[:, i % 2, 0:keys], rden[:, b2], None, ALU.mult)\
                               .then_inc(prob_ready, 1)
                        for _ in range(min(2, len(taps_left))):
                            conv_c_tap()

                    settle()
                    dve.sem_inc(conv_c_done, 1)

                    def lower(part, count, n=KC):
                        dve.wait_ge(part_hi, count)
                        dve.tensor_tensor(w_lo[part % 2][:, 0:n, :], raw[part % 4][:, 0:n, :],
                                          w_hi[part % 2][:, 0:n, :].bitcast(F32), ALU.subtract).then_inc(part_lo, 1)

                    def y_lower(k, source):
                        dve.wait_ge(y_hi_ready, k // 2 + 1)
                        for c in range(2):
                            dve.tensor_tensor(y_lo[k + c][:, 0, :], source[:, c, :], u_hi[:, k + c, :].bitcast(F32), ALU.subtract)\
                               .then_inc(y_lo_ready, 1)

                    lower(0, 1)
                    lower(1, 2)

                    dve.wait_ge(dt_pe, 1)
                    cs4, dt4, we4 = (t.rearrange("p (c h) -> p c h", h=HEADS) for t in (cst_tok, dt_tok, w_end))
                    step(dve.tensor_copy(cst_tok, bank(6)[:, 0:QT * HEADS]))
                    dve.wait_ge(dt_pe, 6)
                    step(dve.tensor_copy(edt.rearrange("p q c b -> p (q c b)"), bank(7)[:, 0:32]))
                    dve.tensor_copy(dsk, bank(7)[:, 32:34]).then_inc(dt_dve, 1)
                    dve.wait_ge(dt_dve, 3)
                    settle()
                    dve.wait_ge(ssd_act, HEADS)
                    for h in range(HEADS):
                        ends = bank(h)[:, P - 1:SEQ:P]
                        step(dve.tensor_tensor(we4[:, :, h], ends, cs4[:, :, h], ALU.subtract))
                    settle()
                    dve.sem_inc(dt_dve, 1)
                    for h in range(HEADS):
                        for c in range(QT):
                            step(dve.scalar_tensor_tensor(decay[:, h * QT + c, :], bank(h)[:, c * P:(c + 1) * P],
                                                          cs4[:, c, h:h + 1], const("later"), ALU.subtract, ALU.add))
                        settle()
                        dve.sem_inc(segments, 1)
                    dve.wait_ge(dt_exp, 4)
                    step(dve.tensor_tensor(w_end, w_end, dt_tok, ALU.mult))
                    settle()
                    dve.wait_ge(mixed, len(STEPS))
                    dve.wait_ge(kv_stored, layer * (16 * N_KV) + 16 * N_KV)
                    for c in range(QT):
                        dve.wait_ge(ssd_act, HEADS + 1 + c)
                        dve.tensor_tensor(xw[:, c, :].rearrange("p (h c) -> p h c", c=HD),
                                          xb_tok[:, c, 0:W].rearrange("p (h c) -> p h c", c=HD),
                                          we4[:, c, :].unsqueeze(2).broadcast_to([P, HEADS, HD]), ALU.mult).then_inc(ssd_dve, 1)
                    dve.wait_ge(ssd_pe, 1)
                    for h in range(HEADS):
                        step(dve.tensor_tensor(read_c[:, h, :], dc[:, 4 + h // 2, 0:SEQ], ecs[:, h, :], ALU.mult))
                    for h in range(HEADS):
                        dve.wait_ge(ssd_act, HEADS + QT + 1 + h)
                        for c in range(QT):
                            m = decay[:, h * QT + c, :]
                            step(dve.scalar_tensor_tensor(m, m, dt4[:, c, h:h + 1], bank(4 + h // 2)[:, c * P:(c + 1) * P],
                                                          ALU.mult, ALU.mult))
                    settle()
                    dve.sem_inc(ssd_dve, 1)
                    flat_h = h_t.rearrange("p h c -> p (h c)")
                    for c in range(QT):
                        if c == 2:
                            dve.wait_ge(cln_pe, 1)
                            for k in range(2):
                                f = halves(feat[:, GG + k, :])
                                step(dve.scalar_tensor_tensor(f, pair(0), -1.0 / W, f, ALU.mult, ALU.add))
                            settle()
                            dve.sem_inc(cln_dve, 1)
                        dve.wait_ge(state_pe, 2 * c + 2)
                        new = bank(6 + c % 2)[:, 0:W]
                        if c == 0:
                            dve.tensor_copy(flat_h, new).then_inc(state_dve, 1)
                        else:
                            end = ecs[:, :, (c + 1) * P - 1].unsqueeze(2).broadcast_to([P, HEADS, HD])
                            step(dve.tensor_tensor(h_t, h_t, end, ALU.mult))
                            settle()
                            dve.tensor_tensor(flat_h, flat_h, new, ALU.add).then_inc(state_dve, 1)
                        dve.wait_ge(state_dve, c + 1)
                    for c in range(2):
                        step(dve.scalar_tensor_tensor(dc[:, c, 0:SEQ], dc[:, c, 0:SEQ], dsk[:, c:c + 1], bank(2 + c), ALU.mult, ALU.add))
                    dve.wait_ge(state_pe, 2 * QT + 1)
                    dve.tensor_copy(ssm_rows.rearrange("p c n -> p (c n)"), bank(6)[:, 0:W]).then_inc(state_dve, 1)
                    dve.wait_ge(decd_pe, 1)
                    dve.tensor_copy(bc_rows, bank(4)[0:NS, :]).then_inc(decd_dve, 1)
                    dve.wait_ge(cln_act, 3)
                    dve.reciprocal(rstd[:, :], root[:, :]).then_inc(cln_dve, 1)
                    dve.wait_ge(cln_dve, 3)
                    for c in range(2):
                        f = feat[:, GG + c, :]
                        dve.scalar_tensor_tensor(f, f, pcol("cln_g", c), rstd[:, :], ALU.mult, ALU.mult).then_inc(cln_dve, 1)
                    y_lower(0, ya)
                    y_lower(2, feat[:, BX:BX + 2, :])
                    step(dve.tensor_tensor(dtx, edt[:, 1], dc[:, 0:2, SEQ:T], ALU.mult))
                    settle()
                    dve.wait_ge(ssm_in, layer * 16 + 16)
                    for b in range(NS):
                        dve.wait_ge(decd_pe, b + 2)
                        bc = bank(4 + b % 2)
                        pr = (prod_n, prod_n2)
                        for c in range(2):
                            step(dve.tensor_scalar(pr[c], bc[:, c * P:(c + 1) * P], dtx[:, c, b:b + 1], None, ALU.mult))
                        settle()
                        for c in range(2):
                            hs = ssm[:, 2 * b + c, :]
                            step(dve.scalar_tensor_tensor(hs, hs, edt[:, 0, c, b:b + 1], pr[c], ALU.mult, ALU.add))
                        settle()
                        for c in range(2):
                            last = dve.tensor_tensor_reduce(pr[c], ssm[:, 2 * b + c, :], bc[:, W + c * P:W + (c + 1) * P], 1.0, 0.0,
                                                            ALU.mult, ALU.add, y_dec[:, c, b:b + 1])
                            if c == 0:
                                step(last)
                        last.then_inc(decd_dve, 1)
                        dve.wait_ge(decd_dve, b + 2)
                    dve.sem_inc(ssm_done, 1)
                    for c in range(2):
                        step(dve.scalar_tensor_tensor(dc[:, c, SEQ:T], dc[:, c, SEQ:T], dsk[:, c:c + 1], y_dec[:, c, :], ALU.mult, ALU.add))
                    settle()
                    for c in range(2):
                        step(dve.tensor_tensor(feat[:, ZG + c, :], feat[:, ZG + c, :], dc[:, c, :], ALU.mult))
                    settle()
                    dve.sem_inc(dn_dve, 1)
                    y_lower(4, feat[:, GG:GG + 2, :])
                    dve.wait_ge(dn_act, 3)
                    dve.wait_ge(cln_dve, 5)
                    step(dve.reciprocal(rstd[:, :], root[:, :]))
                    settle()
                    for c in range(2):
                        f = feat[:, ZG + c, :]
                        dve.scalar_tensor_tensor(f, f, pcol("d_norm", c), rstd[:, :], ALU.mult, ALU.mult).then_inc(dn_dve, 1)
                    y_lower(6, feat[:, ZG:ZG + 2, :])
                    for m in range(KC):
                        lower(m + 2, m + 3)

                    def add_normed(n, u, gain):
                        dve.wait_ge(root_ready, n + 1)
                        step(dve.reciprocal(rstd[:, :], root[:, :]))
                        settle()
                        for k in range(KC):
                            step(dve.scalar_tensor_tensor(u[:, k, :], u[:, k, :], pcol(gain, k), rstd[:, :], ALU.mult, ALU.mult))
                            settle()
                            dve.tensor_tensor(x[:, k, :], x[:, k, :], u[:, k, :], ALU.add).then_inc(x_updated, 1)

                    add_normed(1, mix, "g_post_mix")
                    dve.wait_ge(stored, layer * (16 * N_SSM) + 16 * N_SSM)
                    dve.wait_ge(root_ready, 3)
                    step(dve.reciprocal(rstd[:, :], root[:, :]))
                    settle()
                    for k in range(KC):
                        dve.scalar_tensor_tensor(scaled[:, k, :], x[:, k, :], pcol("g_pre_ffn", k), rstd[:, :],
                                                 ALU.mult, ALU.mult).then_inc(u_scaled, 1)
                        if k:
                            dve.wait_ge(u_hi_ready, k)
                            dve.tensor_tensor(u_lo[:, k - 1, :], scaled[:, k - 1, :], u_hi[:, k - 1, :].bitcast(F32),
                                              ALU.subtract).then_inc(u_lo_ready, 1)
                    dve.wait_ge(u_hi_ready, KC)
                    dve.tensor_tensor(u_lo[:, KC - 1, :], scaled[:, KC - 1, :], u_hi[:, KC - 1, :].bitcast(F32),
                                      ALU.subtract).then_inc(u_lo_ready, 1)
                    dve.wait_ge(u_lo_ready, KC)

                    def hidden_tile(i, c, next_n):
                        lower(2 * c + 2, i * 4 + (GU0 + 2 * c + 3), next_n)
                        dve.wait_ge(gate_ready, i * 2 + (c + 1))
                        dve.wait_ge(up_summed, i * 2 + (c + 1))
                        dve.tensor_tensor(halves(hid_f[:, c, :]), halves(hid_gate[:, c, :]), pair(2 * c + 1), ALU.mult)\
                           .then_inc(hidden_made, 1)
                        lower(2 * c + 3, i * 4 + (GU0 + 2 * c + 4), next_n)
                        dve.wait_ge(hidden_hi, i * 2 + (c + 1))
                        dve.tensor_tensor(hid_lo[:, bass.ds(i * 2 + c, 1), :], hid_f[:, c:c + 1, :],
                                          hid_hi[:, bass.ds(i * 2 + c, 1), :].bitcast(F32), ALU.subtract).then_inc(hidden_lo, 1)

                    with dve.Fori(0, FFC // 2 - 1) as i:
                        for c in range(2):
                            hidden_tile(i, c, KC)
                    hidden_tile(FFC // 2 - 1, 0, KC)
                    hidden_tile(FFC // 2 - 1, 1, DOWN_PARTS[0][1])
                    with dve.Fori(0, KC // 2 - 1) as i:
                        for p in range(2, 10):
                            lower(p, i * 8 + (DN0 + p + 1), DOWN_PARTS[p % 4][1])
                    for p in range(2, 8):
                        lower(p, 4 * KC - 8 + DN0 + p + 1, DOWN_PARTS[p % 4][1])
                    add_normed(3, u, "g_post_ffn")
                    dve.wait_ge(x_updated, 2 * KC)

                @block.gpsimd
                def _(pool):
                    l = layer

                    def tokens(t):
                        return row(t, l)[0:1, 0].rearrange("o (t p) h c -> p (o t) (h c)", p=P) if t.ndim == 5 else \
                            row(t, l)[0:1, 0].rearrange("o (t p) c -> p (o t) c", p=P)

                    pool.dma_start(ssm, row(d["state_ssm"], l).rearrange("o b (c h) p n -> (h p) (o b c) n", c=2))\
                        .then_inc(ssm_in, 16)
                    pool.wait_ge(rope_done, 2)
                    pool.dma_start(tokens(k_prompt), tok_k).then_inc(kv_stored, 16)
                    pool.wait_ge(tok_ready, 14)
                    pool.dma_start(tokens(v_prompt), tok_v).then_inc(kv_stored, 16)
                    pool.wait_ge(rope_done, 5)
                    pool.dma_start(tokens(kidx_prompt), kiw[:, :, 0:ID]).then_inc(kv_stored, 16)
                    for t, at in ((k_sample, W), (v_sample, 2 * W)):
                        pool.dma_start(row(t, l).rearrange("o b s h c -> (o b s) (h c)"), tok8[:, at:at + W]).then_inc(kv_stored, 16)
                    pool.dma_start(row(kidx_sample, l).rearrange("o b s c -> (o b s) c"), tok8[:, 4 * W:4 * W + ID])\
                        .then_inc(kv_stored, 16)
                    for t, name in ((bconv_sample, "state_bconv"), (cconv_sample, "state_cconv"), (dconv_sample, "state_dconv")):
                        n = t.shape[2]
                        pool.dma_start(row(t, l)[:, :, 0:n - 1].rearrange("o b t c -> (o b) t c"),
                                       row(d[name], l)[:, :, 1:n].rearrange("o b t c -> (o b) t c")).then_inc(state_copied, 16)
                    pool.wait_ge(gate_in, 2)
                    pool.wait_ge(cln_dve, 1)
                    made, c = 1, 1
                    w = lambda tap: pcol("cconv_w", 2 * tap + c)
                    pool.tensor_scalar(feat[:, GG + c, 0:SEQ], feat[:, GA + c, 0:SEQ], w(C_CONV - 1), pcol("cconv_b", c),
                                       ALU.mult, ALU.add).then_inc(pool_step, 1)
                    for back in range(1, C_CONV):
                        tap = pool_tmp[back % 2][:, back:SEQ]
                        pool.tensor_scalar(tap, feat[:, GA + c, 0:SEQ - back], w(C_CONV - 1 - back),
                                           None, ALU.mult).then_inc(pool_step, 1)
                        made += 1
                        pool.wait_ge(pool_step, made)
                        acc = feat[:, GG + c, back:SEQ]
                        pool.tensor_tensor(acc, acc, tap, ALU.add).then_inc(pool_step, 1)
                        made += 1
                    pool.wait_ge(pool_step, made)
                    pool.sem_inc(conv_c_done, 1)
                    pool.wait_ge(tails_ready, 4)
                    for src, lo, t_p, t_s in ((tail_b, 2, bconv_prompt, bconv_sample), (tail_c, 30, cconv_prompt, cconv_sample),
                                              (tail_d, 3, dconv_prompt, dconv_sample)):
                        pool.dma_start(row(t_p, l).rearrange("o b t c -> (o b t) c"), src[0:lo, :]).then_inc(tails_stored, 16)
                        pool.dma_start(row(t_s, l)[:, :, lo - 1].rearrange("o b c -> (o b) c"), src[lo:lo + NS, :])\
                            .then_inc(tails_stored, 16)
                    pool.wait_ge(state_dve, QT + 1)
                    pool.dma_start(row(ssm_prompt, l)[0:1, 0].rearrange("o (c h) p n -> (h p) (o c) n", c=2), ssm_rows)\
                        .then_inc(stored, 16)
                    pool.wait_ge(ssm_done, 1)
                    pool.dma_start(row(ssm_sample, l).rearrange("o b (c h) p n -> (h p) (o b c) n", c=2), ssm).then_inc(stored, 16)
                    pool.wait_ge(kv_stored, layer * (16 * N_KV) + 16 * N_KV)
                    pool.wait_ge(state_copied, layer * (16 * N_STATES) + 16 * N_STATES)
                    pool.wait_ge(tails_stored, layer * (16 * N_TAILS) + 16 * N_TAILS)
                    pool.wait_ge(stored, layer * (16 * N_SSM) + 16 * N_SSM)

            nc.all_engine_barrier()
            nc.gpsimd.sem_clear(range(sems[first_layer_sem].num, sems[last_layer_sem - 1].num + 1))
            nc.all_engine_barrier()

        y_turned, y_copied, y_stored = sem("y_turned"), sem("y_copied"), sem("y_stored")
        y_rows = view(arena, 0, QT + 1, D_MODEL)
        with nc.Block() as block:
            @block.tensor
            def _(pe):
                for t in range(QT + 1):
                    m = P if t < QT else NS
                    for q in range(2):
                        n = 2 * t + q
                        if n >= 8:
                            pe.wait_ge(y_copied, n - 7)
                        for c in range(4):
                            last = pe.transpose(bank(n % 8)[0:m, c * P:(c + 1) * P], x[:, 4 * q + c, t * P:t * P + m], ident)
                        last.then_inc(y_turned, 1)

            @block.vector
            def _(dve):
                for t in range(QT + 1):
                    m = P if t < QT else NS
                    for q in range(2):
                        dve.wait_ge(y_turned, 2 * t + q + 1)
                        dve.tensor_copy(y_rows[0:m, t, 512 * q:512 * (q + 1)], bank((2 * t + q) % 8)[0:m, :]).then_inc(y_copied, 1)

            @block.sync
            def _(sp):
                for t in range(QT + 1):
                    sp.wait_ge(y_copied, 2 * t + 2)
                    to = y_prompt[0, t * P:(t + 1) * P, :] if t < QT else y_sample.rearrange("b s f -> (b s) f")
                    sp.dma_start(to, y_rows[0:P if t < QT else NS, t, :]).then_inc(y_stored, 16)
                sp.wait_ge(y_stored, 16 * (QT + 1))
    return nc


_INS = ["x_prompt", "x_sample", "cache_k", "cache_v", "cache_kidx", "page_table", "state_bconv", "state_cconv",
        "state_dconv", "state_ssm", "w_in", "w_out", "g_pre_mix", "g_post_mix", "g_pre_ffn", "g_post_ffn", "bconv_w",
        "cconv_w", "cconv_b", "cln_g", "cln_b", "dconv_w", "dconv_b", "dt_bias", "a_log", "d_skip", "d_norm",
        "ffn_gate", "ffn_up", "ffn_down"]
_XBC = W + 4 * N_STATE
_OUTS = [(1, SEQ, D_MODEL), (NS, 1, D_MODEL), (DEPTH, 1, SEQ, HEADS, HD), (DEPTH, 1, SEQ, HEADS, HD),
         (DEPTH, 1, SEQ, ID), (DEPTH, NS, 1, HEADS, HD), (DEPTH, NS, 1, HEADS, HD), (DEPTH, NS, 1, ID),
         (DEPTH, 1, 2, W), (DEPTH, NS, 2, W), (DEPTH, 1, 30, W), (DEPTH, NS, 30, W), (DEPTH, 1, 3, _XBC),
         (DEPTH, NS, 3, _XBC), (DEPTH, 1, HEADS, HD, N_STATE), (DEPTH, NS, HEADS, HD, N_STATE)]


def kernel(**inputs):
    import concourse.bacc as _bacc
    from concourse.bass_utils import run_bass_kernel_spmd as _run

    nc = _bacc.Bacc("TRN2", target_bir_lowering=False, num_devices=1)
    arrays, dram = {}, {}
    for name in _INS:
        a = np.ascontiguousarray(inputs[name])
        arrays[f"in_{name}"] = a
        dram[name] = nc.dram_tensor(f"in_{name}", a.shape, mybir.dt.from_np(a.dtype), kind="ExternalInput").ap()
    arrays["constants"] = shape_constants()
    dram["constants"] = nc.dram_tensor("constants", arrays["constants"].shape, F32, kind="ExternalInput").ap()
    outs = [nc.dram_tensor(f"out_{i}", shape, F32, kind="ExternalOutput").ap() for i, shape in enumerate(_OUTS)]
    hybrid_decoder(nc, dram, outs)
    r = _run(nc, [arrays], core_ids=[0])
    return tuple(r.results[0][f"out_{i}"] for i in range(len(_OUTS)))
```

```python
from contextlib import ExitStack

import numpy as np
import concourse.bass as bass
from concourse import mybir

F32 = mybir.dt.float32
F32R = mybir.dt.float32r
I32 = mybir.dt.int32
ALU = mybir.AluOpType
ACT = mybir.ActivationFunctionType
AX = mybir.AxisListType

P = 128
D_MODEL, SEQ, DEPTH, NS, PAST, PAGE = 1024, 512, 2, 8, 256, 128
HEADS, HD, IH, ID = 4, 64, 8, 32
TOPK_PROMPT, TOPK_SAMPLE = 128, 64
THETA = 500000.0
B_CONV, C_CONV, D_CONV = 3, 31, 4
D_FF = 2816
N_STATE = 128
W = 256
T = SEQ + NS
HALF = T // 2
QUARTER = T // 4
KC = D_MODEL // P
FFC = D_FF // P
QT = SEQ // P
TOK_W = 4 * W + ID + IH
FEAT0 = TOK_W
DT0 = FEAT0 + 9 * W
RMS_EPS, LN_EPS = 1e-6, 1e-5
MASKED = -1e30
TAKEN = -3e38
SLOTS = 4
SLAB = KC * W

ROWS_A = [("g_pre_mix", 8), ("g_post_mix", 8), ("g_pre_ffn", 8), ("g_post_ffn", 8), ("bconv_w", 6),
          ("cconv_w", 62), ("cconv_b", 2), ("cln_g", 2), ("cln_b", 2), ("d_norm", 2)]
ROWS_B = [("dconv_w", 24), ("dconv_b", 6)]
AT = {}
for _rows, _base in ((ROWS_A, 0), (ROWS_B, sum(n for _, n in ROWS_A))):
    for _name, _n in _rows:
        AT[_name] = _base
        _base += _n
NA_ROWS, NB_ROWS = sum(n for _, n in ROWS_A), sum(n for _, n in ROWS_B)

CONST = {}
_at = 0
for _name, _n in (("ident", 128), ("ones", 128), ("later", 128), ("future", 128), ("upto", 128), ("head_of_row", 4),
                  ("sample_of_row", 8), ("cos", 64), ("nsin", 32), ("sin", 32), ("cos_i", 32),
                  ("nsin_i", 16), ("sin_i", 16), ("cos_d", 16), ("nsin_d", 8), ("sin_d", 8),
                  ("cos_id", 8), ("nsin_id", 4), ("sin_id", 4), ("eps", 2),
                  ("rows_of_sample", 32), ("state_rows", 256)):
    CONST[_name] = (_at, _n)
    _at += _n
N_CONST = _at


def shape_constants():
    c = np.zeros((P, N_CONST), np.float32)

    def put(name, v):
        a, n = CONST[name]
        c[:, a:a + n] = np.asarray(v, np.float32).reshape(P, n)

    i = np.arange(P)
    put("ident", np.eye(P))
    put("ones", np.ones((P, P)))
    put("later", np.where(i[:, None] > i[None, :], MASKED, 0.0))
    put("future", np.where(i[None, :] > i[:, None], MASKED, 0.0))
    put("upto", i[:, None] <= i[None, :])
    put("head_of_row", i[:, None] % HEADS == np.arange(HEADS)[None])
    put("sample_of_row", i[:, None] // HEADS == np.arange(NS)[None])
    put("rows_of_sample", np.arange(32)[None, :] // HEADS == i[:, None])
    put("state_rows", np.arange(2 * P)[None, :] // HD == i[:, None])
    for rot, tail in ((HD // 4, ""), (ID // 4, "_i")):
        half = rot // 2
        inv = np.float32(THETA) ** (-np.arange(half, dtype=np.float32) * np.float32(2.0) / np.float32(rot))
        for pos, d in ((np.arange(SEQ).reshape(QT, P).T, ""), (np.full((P, 1), PAST), "d")):
            ang = pos.astype(np.float32)[:, :, None] * inv
            name = (tail + d) if tail else ("_" + d if d else "")
            put("cos" + name, np.concatenate([np.cos(ang)] * 2, -1))
            put("nsin" + name, -np.sin(ang))
            put("sin" + name, np.sin(ang))
    a, _ = CONST["eps"]
    c[:, a], c[:, a + 1] = RMS_EPS, LN_EPS
    return c


def hybrid_decoder(nc, d, out):
    (y_prompt, y_sample, k_prompt, v_prompt, kidx_prompt, k_sample, v_sample, kidx_sample, bconv_prompt,
     bconv_sample, cconv_prompt, cconv_sample, dconv_prompt, dconv_sample, ssm_prompt, ssm_sample) = out
    ctx = ExitStack()

    address = {}

    def sb(name, shape, dt=F32):
        t = ctx.enter_context(nc.sbuf_tensor(name, shape, dt))
        address[name] = nc.sbuf_base - 4 * int(np.prod(shape[1:]))
        return t

    def over(name, under, at, shape, dt=F32R):
        return nc.alloc_sbuf_tensor_at(name, shape, dt, offset=address[under] + 4 * at)

    sems = []

    def sem(name):
        sems.append(ctx.enter_context(nc.semaphore(name)))
        return sems[-1]

    with ctx:
        cst = sb("cst", [P, N_CONST])
        x = sb("x", [P, KC, T])
        u = sb("u", [P, KC, T])
        ring = sb("ring", [P, SLOTS, SLAB])
        hid = sb("hid", [P, FFC * T])
        all_par = sb("all_par", [P, DEPTH, NA_ROWS + NB_ROWS])
        par = sb("par", [P, 1, NA_ROWS + NB_ROWS])
        small = sb("small", [P, 64])
        pages = sb("pages", [1, 2 * NS], I32)
        tok8 = sb("tok8", [NS, TOK_W])
        ya = sb("ya", [P, 2, T])
        ya8 = sb("ya8", [P, 2, NS])
        ctx_b = sb("ctx_b", [P, 2, NS, B_CONV])
        ctx_c = sb("ctx_c", [P, 2, NS, C_CONV])
        ctx_d = sb("ctx_d", [P, 6, NS, D_CONV])
        root, rstd = sb("root", [P, QUARTER]), sb("rstd", [P, QUARTER])
        dt_tiles = sb("dt_tiles", [P, 6, (QT + 1) * HEADS])
        head_row = sb("head_row", [1, 2 * HEADS])
        head_all = sb("head_all", [P, 2, HEADS])
        arena = sb("arena", [P, FFC * T])
        side = sb("side", [P, 7200])
        u_hi, u_lo = over("u_hi", "u", 0, [P, KC, T]), over("u_lo", "side", 0, [P, KC, T])
        hid_hi, hid_lo = over("hid_hi", "hid", 0, [P, FFC, T]), over("hid_lo", "arena", 0, [P, FFC, T])
        y_lo = [over(f"y_lo{k}", *(("hid", (12 + k) * T) if k < 6 else ("ya", (k - 6) * T)), [P, 1, T]) for k in range(KC)]
        m_lo = [over(f"m_lo{k}", *[("hid", (18 + k) * T), ("ya", (k - 4) * T), ("arena", 9888 + (k - 6) * T)][(k >= 4) + (k >= 6)],
                     [P, 1, T])[:, 0, :] for k in range(KC)]
        tw_hi = [over(f"tw_hi{i}", *at, [P, KC, W]) for i, at in enumerate((("ring", 2 * SLAB), ("hid", 2 * SLAB)))]
        tw_lo = [over(f"tw_lo{i}", *at, [P, KC, W]) for i, at in enumerate((("ring", 3 * SLAB), ("hid", 3 * SLAB)))]
        w_hi = [over(f"w_hi{i}", "ring", (4 + 2 * i) * KC * P, [P, KC, P]) for i in range(2)]
        w_lo = [over(f"w_lo{i}", "ring", (5 + 2 * i) * KC * P, [P, KC, P]) for i in range(2)]
        PS = ctx.enter_context(nc.psum_tensor("PS", [P, 8, 512], F32))

        def view(t, at, *dims):
            n = int(np.prod(dims))
            v = t[:, at:at + n]
            names = "abcd"[:len(dims)]
            if len(dims) == 1:
                return v
            return v.rearrange(f"p ({' '.join(names)}) -> p {' '.join(names)}",
                               **{k: m for k, m in zip(names[:-1], dims[:-1])})

        def const(name):
            a, n = CONST[name]
            return cst[:, a:a + n]

        def pcol(name, i):
            return par[:, 0, AT[name] + i:AT[name] + i + 1]

        ident, ones = const("ident"), const("ones")
        feat = view(hid, 0, 18, T)
        BX, GB, GC, GA, GG, ZG, XBC = 0, 2, 4, 6, 8, 10, 12
        v_cache = view(hid, 0, 2 * NS, W)
        ssm = view(hid, 18 * T, 2 * NS, N_STATE)
        slab_raw = [view(ring[:, i, :], 0, KC, W) for i in range(2)]
        raw = [view(ring[:, i // 2, :], (i % 2) * KC * P, KC, P) for i in range(4)]

        tok_k, tok_v, tok_q = view(arena, 0, QT, W), view(arena, 1024, QT, W), view(arena, 2048, QT, W)
        kiw = view(arena, 3072, QT, ID + IH)
        ki_four = view(arena, 3232, QT, 4, ID)
        turned = view(arena, 3744, 7, SEQ)
        score = view(arena, 7328, 3, SEQ)
        tok_qi = view(arena, 8864, QT, W)
        rect = view(arena, 8864, 2, SEQ)
        prob_t = view(arena, 9888, 2, SEQ)
        rope_a, rope_b = view(arena, 10928, 256), view(arena, 11184, 256)
        squares = view(arena, 3744, KC, T)
        rows_of = [[view(arena, 4096 + (2 * l + q) * P, P) for q in range(2)] for l in range(DEPTH)]
        rows_cc, rows_cb, rows_cd = view(arena, 8160, 2, W), view(arena, 8672, W), view(arena, 8928, 3 * W)
        h_t = view(arena, 2048, HEADS, HD)
        read_c = view(arena, 0, HEADS, SEQ)
        decay = view(arena, 3744, 4 * QT, P)
        ecs = view(arena, 5792, HEADS, SEQ)
        xb_tok = view(arena, 7840, QT, 2 * W)
        xw = view(arena, 9888, QT, W)
        scaled = view(arena, 0, KC, T)
        m_scaled = view(arena, 3744, KC, T)
        hid_gate, hid_f = ya, view(side, KC * T, 2, T)
        ffn_squares = view(side, 0, KC, T)
        OUT_PAIR = [0, 2, 3, 1]
        mix = view(hid, 0, KC, T)

        k_cache = view(side, 0, 2 * NS, W)
        dc = view(side, 0, 6, T)
        dt_rows = view(side, 3120, 2, HEADS, HD)[0:NS]
        temp = view(side, 4096, 4, T)
        ki_cache = view(side, 6176, 2 * NS, ID)
        prod_i = view(side, 6688, 512)
        tails = u[:, 5:8, :].rearrange("p k t -> p (k t)")
        tail_b, tail_c, tail_d = tails[:, 0:256], tails[:, 256:512], tails[:, 512:1280]
        ssm_rows = view(arena, 2304, 2, N_STATE)
        past_s = view(side, 4096, 2, NS)
        past_l = view(side, 4112, 2, NS, HEADS)
        s_row = side[:, 4176:4176 + 257]
        m_row = side[:, 4433:4433 + 261]
        l_row = side[:, 4694:4694 + 257]
        p_row = side[:, 4951:4951 + 257]
        p_col = view(side, 5208, 2, 32)
        self_p, self_pt = side[:, 5272:5280], side[:, 5280:5312]
        sc64, prod8 = side[:, 5312:5376], side[:, 5376:5632]
        best8 = side[:, 5632:5640]
        stat8 = side[:, 5640:5656]
        chunk_best = view(side, 3900, 3, 8)
        pool_tmp = [arena[:, 10928:11440], sb("pool_tmp", [P, SEQ])[:, :]]
        cst_tok = small[:, 0:16]
        dt_v, dt_e, dt_s, dt_z, dt_q, dt_a = (dt_tiles[:, i, :] for i in range(6))
        dt_tok = dt_q[:, 0:QT * HEADS]
        w_end = small[:, 32:48]
        neg_max, denom, rden, top_max = small[:, 48:50], small[:, 50:52], small[:, 52:54], small[:, 54:56]
        dsk = small[:, 56:58]
        d_skip4 = small[0:36, 60:61]
        edt = view(side, 3640, 2, 2, NS)
        dtx = view(side, 3680, 2, NS)
        y_dec = view(side, 3700, 2, NS)
        bc_rows = side[0:NS, 6176:6176 + 512]
        prod_n = view(side, 6688, 2, 2, P)

        def pair(i):
            return PS[:, 2 * i:2 * i + 2, 0:HALF]

        def bank(i):
            return PS[:, i, :]

        def halves(ap):
            return ap.rearrange("p (h n) -> p h n", h=2)

        def sum_tokens(pe, to, first, last, *chunks):
            for n, chunk in enumerate(chunks):
                for g in range(4):
                    ins = pe.matmul(to[32 * g:32 * g + 32, 0, 0:QUARTER], ones[:, 0:32], chunk[:, g * QUARTER:(g + 1) * QUARTER],
                                    start=(first and n == 0), stop=(last and n == len(chunks) - 1))
            return ins

        def row(t, l):
            return t[bass.ds(l, 1)]

        const_in, rows_in, sample_in = sem("const_in"), sem("rows_in"), sem("sample_in")
        params_in, params_turned = sem("params_in"), sem("params_turned")
        x_turned, x_copied, x8_turned = sem("x_turned"), sem("x_copied"), sem("x8_turned")
        x_rows = view(arena, 0, QT, D_MODEL)
        x8 = side[0:NS, 0:D_MODEL]
        x_squares = u
        pages_in, x_squared, x_summed = sem("pages_in"), sem("x_squared"), sem("x_summed")
        with nc.Block() as block:
            @block.sync
            def _(sp):
                sp.dma_start(x8, d["x_sample"].rearrange("b s f -> (b s) f")).then_inc(sample_in, 16)
                sp.dma_start(cst[:, :], d["constants"]).then_inc(const_in, 16)
                for t in range(QT):
                    sp.dma_start(x_rows[:, t, :], d["x_prompt"][0, t * P:(t + 1) * P, :]).then_inc(rows_in, 16)
                sp.dma_start(pages[:, :], d["page_table"].rearrange("(o b) g -> o (b g)", o=1)).then_inc(pages_in, 16)
                for l in range(DEPTH):
                    for rows, tile in zip((ROWS_A, ROWS_B), rows_of[l]):
                        at = 0
                        for name, n in rows:
                            src = d[name][l:l + 1]
                            src = src.rearrange("o (c p) -> (o c) p", p=P) if src.ndim == 2 else \
                                src.rearrange("o t (c p) -> (o t c) p", p=P)
                            sp.dma_start(tile[at:at + n, :], src).then_inc(params_in, 16)
                            at += n
                sp.wait_ge(pages_in, 16)

            @block.tensor
            def _(pe):
                pe.wait_ge(const_in, 16)
                pe.wait_ge(sample_in, 16)
                for c in range(KC):
                    last = pe.transpose(bank(7)[:, c * NS:(c + 1) * NS], x8[:, c * P:(c + 1) * P], ident[0:NS, 0:NS])
                last.then_inc(x8_turned, 1)
                pe.wait_ge(rows_in, 16 * QT)
                for c in range(KC):
                    if c == 7:
                        pe.wait_ge(x_copied, 1)
                    for t in range(QT):
                        last = pe.transpose(bank(c)[:, t * P:(t + 1) * P], x_rows[:, t, c * P:(c + 1) * P], ident)
                    last.then_inc(x_turned, 1)
                pe.wait_ge(params_in, 16 * DEPTH * (len(ROWS_A) + len(ROWS_B)))
                pe.wait_ge(x_copied, DEPTH + 3)
                for l in range(DEPTH):
                    pe.transpose(bank(2 + l)[:, 0:NA_ROWS], rows_of[l][0][0:NA_ROWS, :], ident[0:NA_ROWS, 0:NA_ROWS])
                    pe.transpose(bank(2 + l)[:, NA_ROWS:NA_ROWS + NB_ROWS], rows_of[l][1][0:NB_ROWS, :],
                                 ident[0:NB_ROWS, 0:NB_ROWS]).then_inc(params_turned, 1)
                for k in range(KC):
                    pe.wait_ge(x_squared, k + 1)
                    last = sum_tokens(pe, pair(0), k == 0, k == KC - 1, x_squares[:, k, :])
                last.then_inc(x_summed, 1)
                pe.wait_ge(x_summed, 1)

            @block.scalar
            def _(act):
                for k in range(KC):
                    act.wait_ge(x_copied, k + 2)
                    act.activation(x_squares[:, k, :], x[:, k, :], ACT.Square).then_inc(x_squared, 1)

            @block.vector
            def _(dve):
                dve.wait_ge(x8_turned, 1)
                dve.tensor_copy(x[:, :, SEQ:T], view(PS[:, 7, :], 0, KC, NS)).then_inc(x_copied, 1)
                for c in range(KC):
                    dve.wait_ge(x_turned, c + 1)
                    dve.tensor_copy(x[:, c, 0:SEQ], bank(c)).then_inc(x_copied, 1)
                for l in range(DEPTH):
                    dve.wait_ge(params_turned, l + 1)
                    dve.tensor_copy(all_par[:, l, :], bank(2 + l)[:, 0:NA_ROWS + NB_ROWS]).then_inc(x_copied, 1)
                dve.wait_ge(x_copied, KC + 1 + DEPTH)

        nc.all_engine_barrier()

        kv_stored, stored, state_copied = sem("kv_stored"), sem("stored"), sem("state_copied")
        tails_stored, ssm_in = sem("tails_stored"), sem("ssm_in")
        N_KV, N_STATES, N_TAILS, N_SSM = 6, 3, 6, 2

        first_layer_sem = len(sems)
        scalars_in, states_in = sem("scalars_in"), sem("states_in")
        k_cache_in, v_cache_in, ki_cache_in = sem("k_cache_in"), sem("v_cache_in"), sem("ki_cache_in")
        slab_in = [sem(f"slab_in{i}") for i in range(2)]
        half_in = sem("half_in")
        slab_hi, slab_lo = sem("slab_hi"), sem("slab_lo")
        tile_in = [sem(f"tile_in{i}") for i in range(4)]
        tile_hi, tile_lo = sem("tile_hi"), sem("tile_lo")
        m_scaled_ready, m_hi_ready, m_lo_ready = sem("m_scaled_ready"), sem("m_hi_ready"), sem("m_lo_ready")
        params_ready = sem("params_ready")
        states_turned, states_ready = sem("states_turned"), sem("states_ready")
        rstd_ready, rstd_spread = sem("rstd_ready"), sem("rstd_spread")
        squares_ready, sums_ready, root_ready = sem("squares_ready"), sem("sums_ready"), sem("root_ready")
        x_updated, added = sem("x_updated"), sem("added")
        tok_summed, tok_ready = sem("tok_summed"), sem("tok_ready")
        rope_done, turn_done, turned_ready = sem("rope_done"), sem("turn_done"), sem("turned_ready")
        rows_spread, rows_used = sem("rows_spread"), sem("rows_used")
        feat_summed, feat_ready = sem("feat_summed"), sem("feat_ready")
        dec_pe, dec_dve, dec_max, dec_exp, dec_out = (sem("dec_pe"), sem("dec_dve"), sem("dec_max"), sem("dec_exp"),
                                                      sem("dec_out"))
        idx_summed, idx_rect, idx_added, chosen = sem("idx_summed"), sem("idx_rect"), sem("idx_added"), sem("chosen")
        logits_summed, logits_masked, exp_done, prob_ready = (sem("logits_summed"), sem("logits_masked"),
                                                              sem("exp_done"), sem("prob_ready"))
        prob_turned, prob_t_ready, mixed, mixed_out = (sem("prob_turned"), sem("prob_t_ready"), sem("mixed"),
                                                       sem("mixed_out"))
        vec, pool_step, conv_c_done = sem("vec"), sem("pool_step"), sem("conv_c_done")
        conv_d_done, conv_d_act, segments = sem("conv_d_done"), sem("conv_d_act"), sem("segments")
        dt_pe, dt_exp, dt_low, dt_dve = sem("dt_pe"), sem("dt_exp"), sem("dt_low"), sem("dt_dve")
        dt_w_in = sem("dt_w_in")
        ssd_pe, ssd_act, ssd_dve = sem("ssd_pe"), sem("ssd_act"), sem("ssd_dve")
        state_pe, state_dve = sem("state_pe"), sem("state_dve")
        decd_pe, decd_dve = sem("decd_pe"), sem("decd_dve")
        gate_in, tails_turned, tails_ready = sem("gate_in"), sem("tails_turned"), sem("tails_ready")
        ssm_done = sem("ssm_done")
        cln_pe, cln_act, cln_dve = sem("cln_pe"), sem("cln_act"), sem("cln_dve")
        dn_pe, dn_act, dn_dve = sem("dn_pe"), sem("dn_act"), sem("dn_dve")
        b_done = sem("b_done")
        out_summed, out_ready = sem("out_summed"), sem("out_ready")
        raw_in = [sem(f"raw_in{i}") for i in range(4)]
        part_hi, part_lo = sem("part_hi"), sem("part_lo")
        u_scaled, u_hi_ready, u_lo_ready = sem("u_scaled"), sem("u_hi_ready"), sem("u_lo_ready")
        gate_summed, up_summed, gate_ready = sem("gate_summed"), sem("up_summed"), sem("gate_ready")
        hidden_made, hidden_hi, hidden_lo = sem("hidden_made"), sem("hidden_hi"), sem("hidden_lo")
        y_lo_early = sem("y_lo_early")
        y_hi_ready, y_lo_ready = sem("y_hi_ready"), sem("y_lo_ready")
        down_part, down_ready = sem("down_part"), sem("down_ready")
        last_layer_sem = len(sems)

        FEAT_SLABS = [6, 7, 8, 4, 3, 5, 2, 0, 1]
        N_TOK = 5
        GU0 = KC
        DN0 = GU0 + 2 * FFC
        DOWN_PARTS = [(0, 6), (6, 6), (12, 5), (17, 5)]
        feat_tiles = []
        for s in FEAT_SLABS:
            for c in range(2):
                feat_tiles.append((s, c))
        FEAT_AT = {sc: i for i, sc in enumerate(feat_tiles)}

        def feat_count(*chunks):
            return 1 + max(FEAT_AT[(c // 2, c % 2)] for c in chunks)

        CONV_C_EARLY = 5
        STEPS = [(blk, h) for blk in range(QT) for h in range(HEADS)]
        IDX = [(blk, h) for blk in range(1, QT) for h in range(IH)]

        with nc.Fori(0, DEPTH) as layer:
            with nc.Block() as block:

                @block.sync
                def _(sp):
                    l = layer

                    def slab(n, w):
                        if n == 0:
                            for half in range(2):
                                k = slice(half * KC // 2, (half + 1) * KC // 2)
                                sp.dma_start(slab_raw[0][:, k, :], cols("w_in", 0, W)[:, k, :]).then_inc((slab_in[0], half_in)[half], 16)
                            return
                        if n >= 2:
                            sp.wait_ge(slab_lo, n)
                        sp.dma_start(slab_raw[n % 2][:, :, 0:w], cols("w_in", n * W, w)).then_inc(slab_in[n % 2], 16)

                    def cols(name, a, w):
                        return row(d[name], l).rearrange("o (k p) n -> p (o k) n", p=P)[:, :, a:a + w]

                    for n in range(2):
                        slab(n, W)
                    per = 4 * (C_CONV - 1)
                    for half in range(2):
                        sp.dma_start(rows_cc[0:per, half, :], row(d["state_cconv"], l)[:, 4 * half:4 * half + 4]
                                     .rearrange("o b t c -> (o b t) c")).then_inc(states_in, 16)
                    sp.dma_start(rows_cb[0:2 * NS, :], row(d["state_bconv"], l)
                                 .rearrange("o b t c -> (o b t) c")).then_inc(states_in, 16)
                    sp.dma_start(rows_cd[0:3 * NS, :], row(d["state_dconv"], l)
                                 .rearrange("o b t c -> (o b t) c")).then_inc(states_in, 16)
                    sp.dma_start(d_skip4[0:HEADS, :], row(d["d_skip"], l).rearrange("o h -> h o")).then_inc(scalars_in, 16)
                    for name, at in (("dt_bias", 0), ("a_log", HEADS)):
                        sp.dma_start(head_row[:, at:at + HEADS], row(d[name], l)).then_inc(scalars_in, 16)
                    for n in range(2, 4):
                        slab(n, W)
                    for i in range(2 * NS):
                        page = sp.value_load(pages[0:1, i:i + 1], min_val=0, max_val=d["cache_k"].shape[1] - 1)
                        for name, dst, s in (("cache_kidx", ki_cache, ki_cache_in), ("cache_k", k_cache, k_cache_in),
                                             ("cache_v", v_cache, v_cache_in)):
                            src = row(d[name], l)[:, bass.ds(page, 1)]
                            src = src.rearrange("o g r c -> r (o g c)") if src.ndim == 4 else \
                                src.rearrange("o g r h c -> r (o g h c)")
                            sp.dma_start(dst[:, i, :], src).then_inc(s, 16)
                    slab(4, ID + IH)
                    sp.dma_start(slab_raw[0][:, :, ID + IH:ID + IH + HEADS], cols("w_in", DT0, HEADS)).then_inc(dt_w_in, 16)
                    for f, (s, c) in enumerate(feat_tiles):
                        if f < 4:
                            sp.wait_ge(slab_lo, 5 + f // 2)
                        else:
                            sp.wait_ge(tile_lo, f - 3)
                        sp.dma_start(raw[(f + 2) % 4], cols("w_in", FEAT0 + s * W + c * P, P)).then_inc(tile_in[(f + 2) % 4], 16)
                    for j in range(KC):
                        if j < 4:
                            sp.wait_ge(tile_lo, len(feat_tiles) - 3 + j)
                        else:
                            sp.wait_ge(part_lo, j - 3)
                        sp.dma_start(raw[j % 4], cols("w_out", j * P, P)).then_inc(raw_in[j % 4], 16)

                    def gate_up(j, col):
                        src = row(d["ffn_up" if j % 2 else "ffn_gate"], l)\
                            .rearrange("o (k p) n -> p (o k) n", p=P)[:, :, bass.ds(col, P)]
                        sp.dma_start(raw[j], src).then_inc(raw_in[j], 16)

                    with sp.Fori(0, FFC // 2) as i:
                        for j in range(4):
                            sp.wait_ge(part_lo, i * 4 + (GU0 + j - 3))
                            gate_up(j, i * (2 * P) + (j // 2) * P)

                    def down(q, col):
                        k, n = DOWN_PARTS[q]
                        src = row(d["ffn_down"], l).rearrange("o (k p) n -> p (o k) n", p=P)[:, k:k + n, bass.ds(col, P)]
                        sp.dma_start(raw[q][:, 0:n, :], src).then_inc(raw_in[q], 16)

                    with sp.Fori(0, KC) as m:
                        for q in range(4):
                            sp.wait_ge(part_lo, m * 4 + (DN0 + q - 3))
                            down(q, m * P)

                @block.tensor
                def _(pe):
                    def sum_squares(to, ready, first):
                        for k in range(KC):
                            pe.wait_ge(ready, first + k + 1)
                            last = sum_tokens(pe, to, k == 0, k == KC - 1, squares[:, k, :])
                        last.then_inc(sums_ready, 1)

                    def spread_rstd(to, n):
                        pe.wait_ge(rstd_ready, n)
                        for g in range(4):
                            last = pe.matmul(to[:, g // 2, (g % 2) * QUARTER:(g % 2 + 1) * QUARTER],
                                             ident[:, 32 * g:32 * g + 1].broadcast_to([P, P]), rstd[:, :], start=True, stop=True)
                        last.then_inc(rstd_spread, 1)

                    def sum_added(to, squares, n, ready, value):
                        pe.wait_ge(added, n)
                        pe.wait_ge(ready, value)
                        sum_tokens(pe, to, True, True, squares[:, 0, :], squares[:, KC - 1, :])\
                            .then_inc(sums_ready, 1)

                    chunks = lambda t, n=KC: [t[:, k, :] for k in range(n)]

                    def split_product(to, part, a_hi, a_lo, ks, first, last, base=0):
                        whi, wlo = w_hi[part % 2], w_lo[part % 2]
                        for k in ks:
                            begin, end = first and k == ks[0], last and k == ks[-1]
                            for w, a in ((whi, a_hi), (whi, a_lo), (wlo, a_hi)):
                                for h in range(2):
                                    ins = pe.matmul(to[:, h, :], w[:, k - base, :], a[k][:, h * HALF:(h + 1) * HALF],
                                                    start=(begin and w is whi and a is a_hi), stop=(end and w is wlo))
                        return ins

                    spread_rstd(pair(0), 1)
                    g = 0
                    for s in range(N_TOK):
                        w = W if s < 4 else ID + IH
                        if s == 2:
                            pe.wait_ge(m_lo_ready, KC)
                            pe.wait_ge(states_in, 64)
                            per = 4 * (C_CONV - 1)
                            for c in range(2):
                                for half in range(2):
                                    at = (2 * c + half) * per
                                    pe.transpose(bank(0)[:, at:at + per], rows_cc[0:per, half, c * P:(c + 1) * P],
                                                 ident[0:per, 0:per])
                                pe.transpose(bank(1)[:, c * 16:(c + 1) * 16], rows_cb[0:16, c * P:(c + 1) * P], ident[0:16, 0:16])
                            for c in range(6):
                                last = pe.transpose(bank(1)[:, 32 + c * 24:32 + (c + 1) * 24], rows_cd[0:24, c * P:(c + 1) * P],
                                                    ident[0:24, 0:24])
                            pe.wait_ge(scalars_in, 48)
                            pe.matmul(bank(1)[:, 256:256 + 2 * HEADS], ones[0:1, :], head_row[:, :], start=True, stop=True)\
                              .then_inc(states_turned, 1)
                        if s == 4:
                            w += HEADS
                        if s:
                            pe.wait_ge(slab_lo, s + 2)
                        hi, lo = tw_hi[s % 2][:, :, 0:w], tw_lo[s % 2][:, :, 0:w]
                        for t in range(QT + 1):
                            m = P if t < QT else NS
                            to = bank(2 + g % 6)[0:m, 0:w]
                            if g >= 6:
                                pe.wait_ge(tok_ready, g - 5)
                            for k in range(KC):
                                if s == 0 and t == 0:
                                    pe.wait_ge(m_lo_ready, k + 1)
                                    pe.wait_ge(slab_lo, k // (KC // 2) + 1)
                                u_k, lo_k = u_hi[:, k, t * P:t * P + m], m_lo[k][:, t * P:t * P + m]
                                pe.matmul(to, u_k, hi[:, k, :], start=(k == 0), stop=False)
                                pe.matmul(to, u_k, lo[:, k, :], start=False, stop=False)
                                last = pe.matmul(to, lo_k, hi[:, k, :], start=False, stop=(k == KC - 1))
                            last.then_inc(tok_summed, 1)
                            g += 1

                    pe.wait_ge(tok_ready, g)
                    pe.wait_ge(states_ready, 4)
                    for j, (src, c, need) in enumerate(((tok_q, 0, 1), (tok_q, 1, 1), (tok_k, 0, 2), (tok_k, 1, 2),
                                                        (tok_qi, 0, 3), (tok_qi, 1, 3), (ki_four, 0, 4))):
                        pe.wait_ge(rope_done, need)
                        if j == 0:
                            pe.wait_ge(root_ready, 1)
                        flat = src.rearrange("p t a b -> p t (a b)") if src.ndim == 4 else src
                        for t in range(QT):
                            last = pe.transpose(bank(j)[:, t * P:(t + 1) * P], flat[:, t, c * P:(c + 1) * P], ident)
                        last.then_inc(turn_done, 1)

                    feat_i = [0]

                    def feature_tile():
                        i = feat_i[0]
                        if i >= 2:
                            pe.wait_ge(feat_ready, i - 1)
                        pe.wait_ge(tile_lo, i + 1)
                        last = split_product(pair(i % 2), i, chunks(u_hi), m_lo, range(KC), True, True)
                        last.then_inc(feat_summed, 1)
                        feat_i[0] += 1

                    def spread(b):
                        if b >= 2:
                            pe.wait_ge(rows_used, b - 1)
                        pick = ident[0:NS, b:b + 1].broadcast_to([NS, P])
                        pe.matmul(bank(4 + 2 * (b % 2))[:, 0:W], pick, tok8[:, 0:W], start=True, stop=True)
                        pe.matmul(bank(5 + 2 * (b % 2))[:, 0:TOK_W - 3 * W], pick, tok8[:, 3 * W:TOK_W],
                                  start=True, stop=True).then_inc(rows_spread, 1)

                    pe.wait_ge(turned_ready, 7)
                    pe.wait_ge(rope_done, 5)
                    for b in range(0, NS, 2):
                        spread(b)
                        spread(b + 1)
                        feature_tile()
                    pe.wait_ge(dec_dve, 1)
                    for pg in range(2):
                        pe.transpose(bank(4)[0:NS, pg * P:(pg + 1) * P], past_s[:, pg, :], ident)
                        last = pe.transpose(bank(5)[0:32, pg * P:(pg + 1) * P],
                                            past_l.rearrange("p g b h -> p g (b h)")[:, pg, :], ident)
                    last.then_inc(dec_pe, 1)
                    feature_tile()
                    feature_tile()
                    pe.wait_ge(dec_dve, 2)
                    pe.matmul(bank(6)[0:32, 0:261],
                              const("rows_of_sample")[0:NS, :],
                              m_row[0:NS, :], start=True, stop=True).then_inc(dec_pe, 1)
                    feature_tile()
                    pe.wait_ge(dec_dve, 3)
                    for pg in range(2):
                        pe.transpose(bank(7)[:, pg * 32:(pg + 1) * 32], p_row[0:32, pg * P:(pg + 1) * P], ident[0:32, 0:32])
                    pe.transpose(bank(7)[0:NS, 64:96], self_p[0:32, :], ident[0:32, 0:32]).then_inc(dec_pe, 1)
                    feature_tile()
                    pe.wait_ge(dec_dve, 4)
                    pe.wait_ge(v_cache_in, 16 * 2 * NS)
                    for hp in range(2):
                        pe.matmul(bank(4 + hp)[:, 0:32], tok8[:, 2 * W + hp * P:2 * W + (hp + 1) * P], self_pt[0:NS, :],
                                  start=True, stop=False, skip_group_check=True)
                        for b in range(NS):
                            for pg in range(2):
                                last = pe.matmul(bank(4 + hp)[:, 4 * b:4 * b + 4], v_cache[:, 2 * b + pg, hp * P:(hp + 1) * P],
                                                 p_col[:, pg, 4 * b:4 * b + 4], start=False,
                                                 stop=(b == NS - 1 and pg == 1), skip_group_check=True)
                    last.then_inc(dec_pe, 1)

                    pe.wait_ge(dec_out, 4)
                    for n, (blk, h) in enumerate(IDX):
                        keys = (blk + 1) * P
                        r = 32 * (h % 4)
                        if n >= 4:
                            pe.wait_ge(idx_rect, n - 3)
                        pe.matmul(bank(4 + n % 4)[:, 0:keys], turned[r:r + 32, 4 + h // 4, blk * P:(blk + 1) * P],
                                  turned[r:r + 32, 6, 0:keys], start=True, stop=True).then_inc(idx_summed, 1)
                    while feat_i[0] < len(feat_tiles):
                        feature_tile()

                    pe.wait_ge(gate_in, 4)
                    pe.wait_ge(feat_ready, len(feat_tiles))
                    for c in range(2):
                        pe.transpose(bank(0)[0:10, c * P:(c + 1) * P], feat[:, GC + c, T - 10:T], ident)
                        pe.transpose(bank(0)[0:38, W + c * P:W + (c + 1) * P], feat[:, GA + c, T - 38:T], ident)
                    for c in range(6):
                        to = bank(1)[0:11, c * P:(c + 1) * P] if c < 4 else bank(2)[0:11, (c - 4) * P:(c - 3) * P]
                        last = pe.transpose(to, feat[:, XBC + c, T - 11:T], ident)
                    last.then_inc(tails_turned, 1)

                    pe.wait_ge(idx_rect, len(IDX))
                    for j in range(-1, len(STEPS) + 2):
                        if j + 1 < len(STEPS):
                            blk, h = STEPS[j + 1]
                            r = HD * (h % 2)
                            if j >= 2:
                                pe.wait_ge(logits_masked, j - 1)
                            pe.matmul(bank(3 + (j + 1) % 3)[:, 0:(blk + 1) * P],
                                      turned[r:r + HD, h // 2, blk * P:(blk + 1) * P],
                                      turned[r:r + HD, 2 + h // 2, 0:(blk + 1) * P],
                                      start=True, stop=True).then_inc(logits_summed, 1)
                        if 1 <= j <= len(STEPS):
                            i = j - 1
                            blk, h = STEPS[i]
                            pe.wait_ge(prob_ready, i + 1)
                            if i >= 1:
                                pe.wait_ge(prob_t_ready, i)
                            for kb in range(blk + 1):
                                last = pe.transpose(bank(6)[:, kb * P:(kb + 1) * P], rect[:, i % 2, kb * P:(kb + 1) * P], ident)
                            last.then_inc(prob_turned, 1)
                        if j >= 2:
                            i = j - 2
                            blk, h = STEPS[i]
                            r = HD * (h % 2)
                            pe.wait_ge(prob_t_ready, i + 1)
                            if h == 0 and blk >= 2:
                                pe.wait_ge(mixed_out, blk - 1)
                            at = (blk % 2) * W + (h // 2) * P
                            for kb in range(blk + 1):
                                last = pe.matmul(bank(7)[r:r + HD, at:at + P], tok_v[:, kb, h * HD:(h + 1) * HD],
                                                 prob_t[:, i % 2, kb * P:(kb + 1) * P], start=(kb == 0), stop=(kb == blk))
                            last.then_inc(mixed, 1)

                    pe.wait_ge(tails_ready, 4)
                    pe.wait_ge(mixed_out, QT)
                    pe.wait_ge(dt_dve, 2)
                    upto = const("upto")
                    pe.matmul(bank(6)[:, 0:QT * HEADS], upto, dt_a[:, 0:QT * HEADS], start=True, stop=True)\
                      .then_inc(dt_pe, 1)
                    for h in range(HEADS):
                        for c in range(QT):
                            last = pe.matmul(bank(h)[:, c * P:(c + 1) * P],
                                             dt_a[:, c * HEADS + h:c * HEADS + h + 1].broadcast_to([P, P]), upto,
                                             start=True, stop=True)
                        last.then_inc(dt_pe, 1)
                    for c in range(2):
                        pick = const("state_rows")[0:HEADS, c * P:(c + 1) * P]
                        for q in range(2):
                            pe.transpose(bank(7)[:, 16 * q + 8 * c:16 * q + 8 * c + 8],
                                         dt_rows[:, q, 2 * c:2 * c + 2, :].rearrange("p h c -> p (h c)"), ident[0:NS, 0:NS])
                        last = pe.matmul(bank(7)[:, 32 + c:33 + c],
                                         pick,
                                         d_skip4[0:HEADS, :], start=True, stop=True)
                    last.then_inc(dt_pe, 1)
                    pe.wait_ge(conv_d_act, 6)
                    for gr in range(2):
                        for c in range(QT):
                            last = pe.matmul(bank(4 + gr)[:, c * P:(c + 1) * P], dc[:, 2 + gr, c * P:(c + 1) * P],
                                             dc[:, 4 + gr, c * P:(c + 1) * P], start=True, stop=True)
                    last.then_inc(ssd_pe, 1)
                    pe.wait_ge(dt_dve, 3)
                    for c in range(QT):
                        to = bank(6 + c % 2)
                        if c >= 2:
                            pe.wait_ge(ssd_act, c - 1 + HEADS)
                        for q in range(4):
                            last = pe.transpose(to[:, q * P:(q + 1) * P], dc[:, q, c * P:(c + 1) * P], ident)
                        last.then_inc(ssd_pe, 1)
                    pe.wait_ge(ssd_act, HEADS + QT)
                    for c in range(QT):
                        pe.wait_ge(ssd_dve, c + 1)
                        if c >= 2:
                            pe.wait_ge(state_dve, c - 1)
                        for h in range(HEADS):
                            gr = h // 2
                            last = pe.matmul(bank(6 + c % 2)[:, h * HD:(h + 1) * HD],
                                             xb_tok[:, c, W + gr * P:W + (gr + 1) * P],
                                             xw[:, c, h * HD:(h + 1) * HD], start=True, stop=True)
                        last.then_inc(state_pe, 1)
                        if c == 0:
                            pe.wait_ge(ssd_dve, QT + 1)
                        if c == 1:
                            pe.wait_ge(ssd_dve, QT + 2)
                        if c >= 1:
                            pe.wait_ge(state_dve, c)
                        for h in range(HEADS):
                            r = HD * (h % 2)
                            to = bank(2 + h // 2)[r:r + HD, c * P:(c + 1) * P]
                            last = pe.matmul(to, xb_tok[:, c, h * HD:(h + 1) * HD], decay[:, h * QT + c, :],
                                             start=True, stop=(c == 0))
                            if c >= 1:
                                last = pe.matmul(to, h_t[:, h, :], read_c[:, h, c * P:(c + 1) * P], start=False, stop=True)
                        last.then_inc(state_pe, 1)
                    pe.wait_ge(state_dve, QT)
                    for c in range(2):
                        last = pe.transpose(bank(6)[:, c * P:(c + 1) * P],
                                            h_t.rearrange("p h c -> p (h c)")[:, c * P:(c + 1) * P], ident)
                    last.then_inc(state_pe, 1)
                    for q in range(4):
                        last = pe.transpose(bank(4)[0:NS, q * P:(q + 1) * P], dc[:, 2 + q, SEQ:T], ident)
                    last.then_inc(decd_pe, 1)
                    pe.wait_ge(decd_dve, 1)
                    for b in range(NS):
                        if b == 2:
                            pe.wait_ge(cln_dve, 1)
                            pe.wait_ge(conv_c_done, 2)
                            for k in range(2):
                                for h in range(2):
                                    last = pe.matmul(pair(0)[:, h, :], ones, feat[:, GG + k, h * HALF:(h + 1) * HALF],
                                                     start=(k == 0), stop=(k == 1))
                            last.then_inc(cln_pe, 1)
                        if b == 6:
                            pe.wait_ge(cln_act, 2)
                            sum_tokens(pe, pair(0), True, True, temp[:, 0, :], temp[:, 1, :]).then_inc(cln_pe, 1)
                        if b >= 4:
                            pe.wait_ge(decd_dve, b // 2)
                        pe.matmul(bank(4 + b % 4), ident[0:NS, b:b + 1].broadcast_to([NS, P]), bc_rows,
                                  start=True, stop=True).then_inc(decd_pe, 1)
                    spread_rstd(pair(0), 2)
                    y_lows = [t[:, 0, :] for t in y_lo]
                    pe.wait_ge(cln_dve, 4)
                    pe.wait_ge(decd_dve, NS // 2 + 1)
                    pe.wait_ge(y_lo_early, 4)
                    pe.wait_ge(part_lo, 1)
                    split_product(pair(OUT_PAIR[0]), 0, chunks(u_hi), y_lows, range(4), True, False)
                    pe.wait_ge(dn_act, 2)
                    sum_tokens(pe, pair(1), True, True, temp[:, 2, :], temp[:, 3, :]).then_inc(dn_pe, 1)

                    pe.wait_ge(y_lo_ready, 2)
                    split_product(pair(OUT_PAIR[0]), 0, chunks(u_hi), y_lows, range(4, 6), False, False)
                    spread_rstd(pair(1), 3)
                    pe.wait_ge(part_lo, 2)
                    split_product(pair(OUT_PAIR[1]), 1, chunks(u_hi), y_lows, range(6), True, False)
                    pe.wait_ge(y_lo_ready, 4)
                    for m in range(2):
                        split_product(pair(OUT_PAIR[m]), m, chunks(u_hi), y_lows, range(6, KC), False, True)\
                            .then_inc(out_summed, 1)
                    for m in range(2, KC):
                        if m >= 4:
                            pe.wait_ge(out_ready, 2 * (m - 3))
                        pe.wait_ge(part_lo, m + 1)
                        split_product(pair(OUT_PAIR[m % 4]), m, chunks(u_hi), y_lows, range(KC), True, True)\
                            .then_inc(out_summed, 1)
                    pe.wait_ge(out_ready, 2 * 5)
                    sum_added(pair(0), squares, KC - 2, out_ready, 2 * KC)
                    spread_rstd(pair(0), 4)
                    sum_squares(pair(3), squares_ready, 0)
                    spread_rstd(pair(3), 5)

                    pe.wait_ge(out_ready, 2 * KC)
                    pe.wait_ge(root_ready, 3)

                    def hidden_product(i, c, q, summed):
                        pe.wait_ge(part_lo, i * 4 + (GU0 + 2 * c + q + 1))
                        split_product(pair(2 * c + q), q, chunks(u_hi), chunks(u_lo), range(KC), True, True).then_inc(summed, 1)

                    pe.wait_ge(part_lo, GU0 + 1)
                    for k in range(KC):
                        pe.wait_ge(u_lo_ready, k + 1)
                        last = split_product(pair(0), 0, chunks(u_hi), chunks(u_lo), [k], k == 0, k == KC - 1)
                    last.then_inc(gate_summed, 1)
                    hidden_product(0, 0, 1, up_summed)
                    hidden_product(0, 1, 0, gate_summed)
                    hidden_product(0, 1, 1, up_summed)
                    with pe.Fori(1, FFC // 2) as i:
                        for c in range(2):
                            for q, summed in ((0, gate_summed), (1, up_summed)):
                                hidden_product(i, c, q, summed)

                    pe.wait_ge(hidden_lo, FFC)
                    with pe.Fori(0, KC // 2) as i:
                        for c in range(2):
                            pe.wait_ge(down_ready, i * 4 + (2 * c + 2))
                            for q, (k, n) in enumerate(DOWN_PARTS):
                                pe.wait_ge(part_lo, i * 8 + (DN0 + 4 * c + q + 1))
                                split_product(pair(c), q, chunks(hid_hi, FFC), chunks(hid_lo, FFC), range(k, k + n), q == 0, q == 3, k)\
                                    .then_inc(down_part, 1)
                    sum_added(pair(2), ffn_squares, 2 * (KC - 2), down_ready, 2 * KC + 4)
                    spread_rstd(pair(2), 6)
                    sum_squares(pair(0), squares_ready, KC)

                @block.scalar
                def _(act):
                    def root_of(n, sums, scale, eps):
                        if n:
                            act.wait_ge(sums_ready, n)
                        act.activation(root[:, :], sums[:, 0, 0:QUARTER], ACT.Sqrt, bias=const("eps")[:, eps:eps + 1], scale=scale)\
                           .then_inc(root_ready, 1)

                    def first_upper(half):
                        k = slice(half * KC // 2, (half + 1) * KC // 2)
                        act.wait_ge((slab_in[0], half_in)[half], 16)
                        act.copy(tw_hi[0][:, k, :], slab_raw[0][:, k, :]).then_inc(slab_hi, 1)

                    def slab_upper(s):
                        w = W if s < 4 else ID + IH + HEADS
                        act.wait_ge(slab_in[s % 2], 16 * (s // 2 + 1))
                        if s == 4:
                            act.wait_ge(dt_w_in, 16)
                        if s >= 2:
                            act.wait_ge(tok_summed, (QT + 1) * (s - 1))
                        act.copy(tw_hi[s % 2][:, :, 0:w], slab_raw[s % 2][:, :, 0:w]).then_inc(slab_hi, 1)

                    root_of(0, pair(0), 1.0 / D_MODEL, 0)
                    for k in range(KC):
                        if k in (1, 3):
                            first_upper(k // 2)
                        act.wait_ge(m_scaled_ready, k + 1)
                        act.copy(u_hi[:, k, :], m_scaled[:, k, :]).then_inc(m_hi_ready, 1)
                    slab_upper(1)

                    g = 0
                    act.wait_ge(dt_dve, 1)
                    for s in range(N_TOK):
                        w = W if s < 4 else ID + IH
                        for t in range(QT + 1):
                            act.wait_ge(tok_summed, g + 1)
                            if t < QT:
                                to = (tok_q, tok_k, tok_v, tok_qi, kiw)[s][:, t, :]
                            else:
                                to = tok8[:, s * W:s * W + w]
                            if s == 4:
                                m = to.shape[0]
                                act.copy(dt_v[0:m, t * HEADS:(t + 1) * HEADS], bank(2 + g % 6)[0:m, w:w + HEADS])
                            act.copy(to, bank(2 + g % 6)[0:to.shape[0], 0:w]).then_inc(tok_ready, 1)
                            g += 1
                        if s + 2 < N_TOK:
                            slab_upper(s + 2)

                    def tile_upper(f):
                        act.wait_ge(tile_in[(f + 2) % 4], 16 * ((f + 2) // 4 + (f % 4 < 2)))
                        act.wait_ge(*((tok_summed, g) if f < 2 else (feat_summed, f - 1)))
                        act.copy(w_hi[f % 2][:, :, :], raw[(f + 2) % 4]).then_inc(tile_hi, 1)

                    tile_upper(0)
                    tile_upper(1)
                    for j in range(7):
                        act.wait_ge(turn_done, j + 1)
                        act.copy(turned[:, j, :], bank(j)).then_inc(turned_ready, 1)

                    feat_i = [0]

                    def feature_out(upto):
                        while feat_i[0] < upto:
                            i = feat_i[0]
                            s, c = feat_tiles[i]
                            if i + 2 < len(feat_tiles):
                                tile_upper(i + 2)
                            act.wait_ge(feat_summed, i + 1)
                            func = {GG // 2: ACT.Sigmoid, ZG // 2: ACT.Silu}.get(s, ACT.Copy)
                            act.activation(halves(feat[:, 2 * s + c, :]), pair(i % 2), func).then_inc(feat_ready, 1)
                            feat_i[0] += 1

                    act.wait_ge(dt_low, 1)
                    act.activation(dt_e, dt_e, ACT.Exp).then_inc(dt_exp, 1)
                    act.activation(head_all[:, 1, :], head_all[:, 1, :], ACT.Exp).then_inc(dt_exp, 1)
                    feature_out(6)
                    act.wait_ge(dec_max, 1)
                    act.activation(p_row[0:32, :], l_row[0:32, :], ACT.Exp, bias=stat8[0:32, 1:2], scale=HD ** -0.5,
                                   accum_out=stat8[0:32, 2:3]).then_inc(dec_exp, 1)
                    feature_out(8)
                    act.wait_ge(dec_pe, 4)
                    for hp in range(2):
                        o = bank(4 + hp)[:, 0:32].rearrange("p (b h) -> p b h", h=HEADS)
                        for q in range(2):
                            act.copy(ya8[HD * q:HD * (q + 1), hp, :], o[HD * q:HD * (q + 1), :, 2 * hp + q])\
                               .then_inc(dec_out, 1)
                    for n, (blk, h) in enumerate(IDX):
                        keys = (blk + 1) * P
                        act.wait_ge(idx_summed, n + 1)
                        if n >= 2:
                            act.wait_ge(idx_added, n - 1)
                        act.activation(rect[:, n % 2, 0:keys], bank(4 + n % 4)[:, 0:keys], ACT.Relu,
                                       scale=(ID * IH) ** -0.5).then_inc(idx_rect, 1)
                    feature_out(len(feat_tiles))
                    act.wait_ge(conv_d_done, 1)
                    for c in range(6):
                        act.activation(dc[:, c, :], dc[:, c, :], ACT.Silu).then_inc(conv_d_act, 1)
                    act.wait_ge(tails_turned, 1)
                    act.copy(tail_b[0:10, :], bank(0)[0:10, 0:W]).then_inc(tails_ready, 1)
                    act.copy(tail_c[0:38, :], bank(0)[0:38, W:2 * W]).then_inc(tails_ready, 1)
                    act.copy(tail_d[0:11, 0:512], bank(1)[0:11, :]).then_inc(tails_ready, 1)
                    act.copy(tail_d[0:11, 512:768], bank(2)[0:11, 0:W]).then_inc(tails_ready, 1)
                    def upper(part, free, value, turn, n=KC):
                        act.wait_ge(raw_in[part % 4], turn)
                        act.wait_ge(free, value)
                        act.copy(w_hi[part % 2][:, 0:n, :], raw[part % 4][:, 0:n, :]).then_inc(part_hi, 1)

                    for n in range(2):
                        upper(n, feat_summed, len(feat_tiles), 16)

                    def y_upper(k, source):
                        act.copy(u_hi[:, k:k + 2, :], source).then_inc(y_hi_ready, 1)

                    for j in range(len(STEPS) + 1):
                        if j < len(STEPS):
                            blk, h = STEPS[j]
                            keys = (blk + 1) * P
                            act.wait_ge(logits_masked, j + 1)
                            act.activation(rect[:, j % 2, 0:keys], rect[:, j % 2, 0:keys], ACT.Exp,
                                           bias=neg_max[:, j % 2:j % 2 + 1], scale=HD ** -0.5,
                                           accum_out=denom[:, j % 2:j % 2 + 1]).then_inc(exp_done, 1)
                        if j >= 1:
                            i = j - 1
                            blk, h = STEPS[i]
                            keys = (blk + 1) * P
                            act.wait_ge(prob_turned, i + 1)
                            if i >= 2:
                                act.wait_ge(mixed, i - 1)
                            act.copy(prob_t[:, i % 2, 0:keys], bank(6)[:, 0:keys]).then_inc(prob_t_ready, 1)
                            if h == HEADS - 1:
                                act.wait_ge(mixed, i + 1)
                                act.copy(ya[:, :, blk * P:(blk + 1) * P],
                                         view(PS[:, 7, :], (blk % 2) * W, 2, P)).then_inc(mixed_out, 1)
                    for h in range(HEADS):
                        act.wait_ge(dt_pe, 2 + h)
                        act.activation(ecs[:, h, :], bank(h), ACT.Exp).then_inc(ssd_act, 1)
                    act.wait_ge(dt_dve, 3)
                    act.activation(edt[:, 0], edt[:, 0], ACT.Exp).then_inc(dt_exp, 1)
                    act.wait_ge(dt_dve, 4)
                    act.activation(w_end, w_end, ACT.Exp).then_inc(dt_exp, 1)
                    for c in range(QT):
                        act.wait_ge(ssd_pe, 2 + c)
                        act.copy(xb_tok[:, c, :], bank(6 + c % 2)).then_inc(ssd_act, 1)
                    for h in range(HEADS):
                        act.wait_ge(segments, h + 1)
                        act.activation(decay[:, QT * h:QT * (h + 1), :], decay[:, QT * h:QT * (h + 1), :], ACT.Exp)\
                           .then_inc(ssd_act, 1)
                    act.copy(ya[:, :, SEQ:T], ya8[:, :, :]).then_inc(dec_out, 1)
                    act.wait_ge(dec_out, 5)
                    act.wait_ge(mixed_out, QT)
                    y_upper(0, ya[:, :, :])
                    act.wait_ge(b_done, 2)
                    y_upper(2, feat[:, BX:BX + 2, :])
                    act.wait_ge(cln_dve, 2)
                    for c in range(2):
                        act.activation(temp[:, c, :], feat[:, GG + c, :], ACT.Square).then_inc(cln_act, 1)
                    act.wait_ge(cln_pe, 2)
                    act.activation(root[:, :], pair(0)[:, 0, 0:QUARTER], ACT.Sqrt, bias=const("eps")[:, 1:2], scale=1.0 / W)\
                       .then_inc(cln_act, 1)
                    act.wait_ge(cln_dve, 4)
                    for c in range(2):
                        act.activation(feat[:, GG + c, :], feat[:, GG + c, :], ACT.Silu, bias=pcol("cln_b", c))\
                           .then_inc(cln_act, 1)
                    act.wait_ge(tails_stored, layer * (16 * N_TAILS) + 16 * N_TAILS)
                    act.wait_ge(cln_act, 5)
                    y_upper(4, feat[:, GG:GG + 2, :])
                    act.wait_ge(dn_dve, 1)
                    for c in range(2):
                        act.activation(temp[:, 2 + c, :], feat[:, ZG + c, :], ACT.Square).then_inc(dn_act, 1)
                    act.wait_ge(dn_pe, 1)
                    act.activation(root[:, :], pair(1)[:, 0, 0:QUARTER], ACT.Sqrt, bias=const("eps")[:, 0:1], scale=1.0 / W)\
                       .then_inc(dn_act, 1)
                    act.wait_ge(dn_dve, 3)
                    y_upper(6, feat[:, ZG:ZG + 2, :])
                    for m in range(KC):
                        act.wait_ge(out_summed, m + 1)
                        upper(m + 2, out_summed, m + 1, 16 * ((m + 2) // 4 + 1))
                        act.copy(halves(mix[:, m, :]), pair(OUT_PAIR[m % 4])).then_inc(out_ready, 1)
                        act.activation(halves(squares[:, m, :]), pair(OUT_PAIR[m % 4]), ACT.Square).then_inc(out_ready, 1)
                    root_of(1, pair(0), 1.0 / D_MODEL, 0)

                    for k in range(KC):
                        act.wait_ge(x_updated, k + 1)
                        act.activation(squares[:, k, :], x[:, k, :], ACT.Square).then_inc(squares_ready, 1)
                    root_of(2, pair(3), 1.0 / D_MODEL, 0)
                    for k in range(KC):
                        act.wait_ge(u_scaled, k + 1)
                        act.copy(u_hi[:, k, :], scaled[:, k, :]).then_inc(u_hi_ready, 1)
                    act.wait_ge(stored, layer * (16 * N_SSM) + 16 * N_SSM)

                    def hidden_tile(i, c, next_n):
                        for q, summed in ((0, gate_summed), (1, up_summed)):
                            part = GU0 + 2 * c + q + 2
                            upper(part, summed, i * 2 + (c + 1), i * 16 + 16 * (part // 4 + 1), next_n)
                            if q == 0:
                                act.activation(halves(hid_gate[:, c, :]), pair(2 * c), ACT.Silu).then_inc(gate_ready, 1)
                        act.wait_ge(hidden_made, i * 2 + (c + 1))
                        act.copy(hid_hi[:, bass.ds(i * 2 + c, 1), :], hid_f[:, c:c + 1, :]).then_inc(hidden_hi, 1)

                    with act.Fori(0, FFC // 2 - 1) as i:
                        for c in range(2):
                            hidden_tile(i, c, KC)
                    hidden_tile(FFC // 2 - 1, 0, KC)
                    hidden_tile(FFC // 2 - 1, 1, DOWN_PARTS[0][1])
                    act.sem_inc(down_ready, 4)

                    def down_tile(i, c, parts):
                        for q in parts:
                            part = DN0 + 4 * c + q + 2
                            upper(part, down_part, i * 8 + (4 * c + q + 1), i * 32 + 16 * (part // 4 + 1),
                                  DOWN_PARTS[part % 4][1])
                        act.wait_ge(down_part, i * 8 + (4 * c + 4))
                        act.copy(u[:, bass.ds(i * 2 + c, 1), :].rearrange("p o (h n) -> p (o h) n", h=2), pair(c))\
                           .then_inc(down_ready, 1)
                        act.activation(ffn_squares[:, bass.ds(i * 2 + c, 1), :].rearrange("p o (h n) -> p (o h) n", h=2),
                                       pair(c), ACT.Square).then_inc(down_ready, 1)

                    with act.Fori(0, KC // 2 - 1) as i:
                        down_tile(i, 0, range(4))
                        down_tile(i, 1, range(4))
                    down_tile(KC // 2 - 1, 0, range(4))
                    down_tile(KC // 2 - 1, 1, range(2))
                    root_of(3, pair(2), 1.0 / D_MODEL, 0)
                    for k in range(KC):
                        act.wait_ge(x_updated, KC + k + 1)
                        act.activation(squares[:, k, :], x[:, k, :], ACT.Square).then_inc(squares_ready, 1)

                @block.vector
                def _(dve):
                    made = [0]

                    def step(ins):
                        ins.then_inc(vec, 1)
                        made[0] += 1

                    def settle():
                        dve.wait_ge(vec, made[0])

                    def reciprocal_root(ready, value):
                        dve.wait_ge(ready, value)
                        dve.reciprocal(rstd[:, :], root[:, :]).then_inc(rstd_ready, 1)

                    def normalise(n, gain, to, made_sem, hi_sem, lo_sem, lower):
                        reciprocal_root(root_ready, n + 1)
                        dve.wait_ge(rstd_spread, {0: 1, 2: 5}[n])
                        for k in range(KC + 2):
                            if k < KC:
                                dve.scalar_tensor_tensor(halves(to[:, k, :]), halves(x[:, k, :]), pcol(gain, k), pair({0: 0, 2: 3}[n]),
                                                         ALU.mult, ALU.mult).then_inc(made_sem, 1)
                            if k >= 2:
                                dve.wait_ge(hi_sem, k - 1)
                                dve.tensor_tensor(lower[k - 2], to[:, k - 2, :], u_hi[:, k - 2, :].bitcast(F32),
                                                  ALU.subtract).then_inc(lo_sem, 1)

                    dve.tensor_copy(par[:, :, :], all_par[:, bass.ds(layer, 1), :]).then_inc(params_ready, 1)
                    dve.wait_ge(params_ready, 1)
                    dve.memset(dt_v[:, QT * HEADS:], 0.0).then_inc(dt_dve, 1)
                    normalise(0, "g_pre_mix", m_scaled, m_scaled_ready, m_hi_ready, m_lo_ready, m_lo)
                    def rope(v, heads, rot, tables, p, blocks):
                        half = rot // 2
                        n = blocks * heads
                        a = rope_a[0:p, 0:n * rot].rearrange("p (t h r) -> p t h r", h=heads, r=rot)
                        b = rope_b[0:p, 0:n * rot].rearrange("p (t h r) -> p t h r", h=heads, r=rot)
                        tabs = [const(x)[0:p].rearrange("p (t r) -> p t r", t=blocks).unsqueeze(2) for x in tables]
                        full, part = [p, blocks, heads, rot], [p, blocks, heads, half]
                        for t in range(blocks):
                            step(dve.tensor_tensor(a[:, t], v[:, t], tabs[0][:, t].broadcast_to([p, heads, rot]), ALU.mult))
                            step(dve.tensor_tensor(b[:, t, :, 0:half], v[:, t, :, half:rot],
                                                   tabs[1][:, t].broadcast_to([p, heads, half]), ALU.mult))
                            step(dve.tensor_tensor(b[:, t, :, half:rot], v[:, t, :, 0:half],
                                                   tabs[2][:, t].broadcast_to([p, heads, half]), ALU.mult))
                        settle()
                        for t in range(blocks):
                            last = dve.tensor_tensor(v[:, t], a[:, t], b[:, t], ALU.add)
                            if t < blocks - 1:
                                step(last)
                        return last

                    def take_states():
                        dve.wait_ge(states_turned, 1)
                        dve.tensor_copy(ctx_c[:, :, :, 0:C_CONV - 1].rearrange("p c b t -> p (c b) t"),
                                        view(PS[:, 0, :], 0, 2 * NS, C_CONV - 1)).then_inc(states_ready, 1)
                        dve.tensor_copy(ctx_b[:, :, :, 0:2].rearrange("p c b t -> p (c b) t"),
                                        view(PS[:, 1, :], 0, 2 * NS, 2)).then_inc(states_ready, 1)
                        dve.tensor_copy(ctx_d[:, :, :, 0:3].rearrange("p c b t -> p (c b) t"),
                                        view(PS[:, 1, :], 32, 6 * NS, 3)).then_inc(states_ready, 1)
                        dve.tensor_copy(head_all.rearrange("p q h -> p (q h)"), PS[:, 1, 256:256 + 2 * HEADS]).then_inc(states_ready, 1)

                    tab, tab_i = ("cos", "nsin", "sin"), ("cos_i", "nsin_i", "sin_i")
                    for s, (t, heads, width, rot, tb) in ((0, (tok_q, HEADS, HD, 16, tab)), (1, (tok_k, HEADS, HD, 16, tab)),
                                                          (3, (tok_qi, IH, ID, 8, tab_i)), (4, (kiw, 1, ID, 8, tab_i))):
                        if s == 3:
                            take_states()
                        dve.wait_ge(tok_ready, 5 * s + 4)
                        v = t[:, :, 0:heads * width].rearrange("p t (h c) -> p t h c", c=width)[:, :, :, 0:rot]
                        ins = rope(v, heads, rot, tb, P, QT)
                        if s < 4:
                            ins.then_inc(rope_done, 1)
                            dve.wait_ge(rope_done, 1 + (0, 1, None, 2)[s])
                        else:
                            step(ins)
                            settle()
                            dve.tensor_copy(ki_four, kiw[:, :, 0:ID].unsqueeze(2).broadcast_to([P, QT, 4, ID]))\
                               .then_inc(rope_done, 1)
                    dve.wait_ge(tok_ready, 25)
                    for at, heads, width, rot, tb in ((0, 2 * HEADS, HD, 16, ("cos_d", "nsin_d", "sin_d")),
                                                      (3 * W, IH + 1, ID, 8, ("cos_id", "nsin_id", "sin_id"))):
                        v = tok8[:, at:at + heads * width].rearrange("p (t h c) -> p t h c", t=1, c=width)[:, :, :, 0:rot]
                        step(rope(v, heads, rot, tb, NS, 1))
                        settle()
                    dve.tensor_scalar(tok8[:, TOK_W - IH:TOK_W], tok8[:, TOK_W - IH:TOK_W], (ID * IH) ** -0.5, None, ALU.mult)\
                       .then_inc(rope_done, 1)
                    dve.wait_ge(rope_done, 5)
                    def per_head(t):
                        return t.rearrange("p (b h) -> p b h", h=HEADS)

                    blocks = [P, QT + 1, HEADS]
                    dve.wait_ge(states_ready, 4)
                    step(dve.tensor_tensor(per_head(dt_v), per_head(dt_v), head_all[:, 0:1, :].broadcast_to(blocks), ALU.add))
                    settle()
                    dve.scalar_tensor_tensor(dt_e, dt_v, -1.0, dt_v, ALU.mult, ALU.min).then_inc(dt_low, 1)

                    dve.wait_ge(k_cache_in, 16 * 2 * NS)
                    dve.wait_ge(ki_cache_in, 16 * 2 * NS)
                    for b in range(NS):
                        qb, ib = bank(4 + 2 * (b % 2)), bank(5 + 2 * (b % 2))
                        dve.wait_ge(rows_spread, b + 1)
                        kb = k_cache[:, 2 * b:2 * b + 2, :]
                        step(dve.tensor_tensor(kb, kb, qb[:, 0:W].unsqueeze(1).broadcast_to([P, 2, W]), ALU.mult))
                        pi = prod_i.rearrange("p (g h c) -> p g h c", g=2, c=ID)
                        for pg in range(2):
                            step(dve.tensor_tensor(pi[:, pg], ki_cache[:, 2 * b + pg, :].unsqueeze(1).broadcast_to([P, IH, ID]),
                                                   ib[:, 0:W].rearrange("p (h c) -> p h c", c=ID), ALU.mult))
                        settle()
                        step(dve.tensor_reduce(past_l[:, :, b, :], kb.rearrange("p g (h c) -> p g h c", c=HD), AX.X, ALU.add))
                        s16 = sc64[:, 0:16].rearrange("p (g h) -> p g h", g=2)
                        step(dve.tensor_reduce(s16, pi, AX.X, ALU.add))
                        settle()
                        dve.scalar_tensor_tensor(s16, s16, 0.0, ib[:, W + ID:W + ID + IH].unsqueeze(1).broadcast_to([P, 2, IH]),
                                                 ALU.max, ALU.mult).then_inc(rows_used, 1)
                        dve.wait_ge(rows_used, b + 1)
                        step(dve.tensor_reduce(past_s[:, :, b], s16, AX.X, ALU.add))
                    q8, k8 = tok8[:, 0:W], tok8[:, W:2 * W]
                    settle()
                    step(dve.tensor_tensor(prod8[0:NS, :], q8, k8, ALU.mult))
                    settle()
                    step(dve.tensor_reduce(m_row[0:NS, 257:261], prod8[0:NS, :].rearrange("p (h c) -> p h c", c=HD), AX.X, ALU.add))
                    settle()
                    step(dve.tensor_tensor(prod8[0:NS, :].rearrange("p (h c) -> p h c", c=ID),
                                           tok8[:, 3 * W:4 * W].rearrange("p (h c) -> p h c", c=ID),
                                           tok8[:, 4 * W:4 * W + ID].unsqueeze(1).broadcast_to([NS, IH, ID]), ALU.mult))
                    settle()
                    step(dve.tensor_reduce(sc64[0:NS, 16:24], prod8[0:NS, :].rearrange("p (h c) -> p h c", c=ID), AX.X, ALU.add))
                    settle()
                    step(dve.scalar_tensor_tensor(sc64[0:NS, 24:32], sc64[0:NS, 16:24], 0.0, tok8[:, TOK_W - IH:TOK_W],
                                                  ALU.max, ALU.mult))
                    settle()
                    dve.tensor_reduce(s_row[0:NS, 256:257], sc64[0:NS, 24:32], AX.X, ALU.add).then_inc(dec_dve, 1)
                    dve.wait_ge(dt_exp, 1)
                    step(dve.tensor_scalar(dt_s, dt_e, 2.0, None, ALU.add))
                    settle()
                    step(dve.reciprocal(dt_s, dt_s))
                    settle()
                    step(dve.tensor_tensor(dt_s, dt_s, dt_e, ALU.mult))
                    settle()
                    step(dve.tensor_tensor(dt_z, dt_s, dt_s, ALU.mult))
                    settle()
                    step(dve.tensor_scalar(dt_q, dt_z, 1.0 / 15.0, None, ALU.mult))
                    for n in (13, 11, 9, 7, 5, 3):
                        settle()
                        step(dve.scalar_tensor_tensor(dt_q, dt_q, 1.0 / n, dt_z, ALU.add, ALU.mult))
                    settle()
                    step(dve.scalar_tensor_tensor(dt_q, dt_q, 1.0, dt_s, ALU.add, ALU.mult))
                    step(dve.tensor_scalar(dt_v, dt_v, 0.0, None, ALU.max))
                    settle()
                    step(dve.scalar_tensor_tensor(dt_q, dt_q, 2.0, dt_v, ALU.mult, ALU.add))
                    settle()
                    dve.wait_ge(dt_exp, 2)
                    step(dve.scalar_tensor_tensor(per_head(dt_a), per_head(dt_q), -1.0, head_all[:, 1:2, :].broadcast_to(blocks),
                                                  ALU.mult, ALU.mult))
                    settle()
                    for q, t in ((0, dt_a), (1, dt_q)):
                        last = dve.tensor_copy(dt_rows[:, q], t[0:NS, QT * HEADS:].unsqueeze(2).broadcast_to([NS, HEADS, HD]))
                        if q == 0:
                            step(last)
                    last.then_inc(dt_dve, 1)
                    dve.wait_ge(dec_pe, 1)
                    step(dve.tensor_copy(s_row[0:NS, 0:256], bank(4)[0:NS, 0:256]))
                    step(dve.tensor_copy(l_row[0:32, 0:256], bank(5)[0:32, 0:256]))
                    dve.wait_ge(dec_dve, 1)
                    for r in range(TOPK_SAMPLE // 8):
                        settle()
                        step(dve.max(best8[0:NS, :], s_row[0:NS, :]))
                        settle()
                        step(dve.match_replace(s_row[0:NS, :], best8[0:NS, :], s_row[0:NS, :], TAKEN))
                    settle()
                    dve.tensor_scalar(m_row[0:NS, 0:257], s_row[0:NS, :], TAKEN, MASKED, ALU.not_equal, ALU.mult)\
                       .then_inc(dec_dve, 1)
                    dve.wait_ge(dec_pe, 2)
                    step(dve.tensor_tensor(sc64[0:32, 32:36], bank(6)[0:32, 257:261], const("head_of_row")[0:32, :], ALU.mult))
                    settle()
                    step(dve.tensor_reduce(l_row[0:32, 256:257], sc64[0:32, 32:36], AX.X, ALU.add))
                    settle()
                    step(dve.tensor_tensor(l_row[0:32, :], l_row[0:32, :], bank(6)[0:32, 0:257], ALU.add))
                    settle()
                    step(dve.tensor_reduce(stat8[0:32, 0:1], l_row[0:32, :], AX.X, ALU.max))
                    settle()
                    dve.tensor_scalar(stat8[0:32, 1:2], stat8[0:32, 0:1], -HD ** -0.5, None, ALU.mult).then_inc(dec_max, 1)
                    dve.wait_ge(dec_exp, 1)
                    step(dve.reciprocal(stat8[0:32, 3:4], stat8[0:32, 2:3]))
                    settle()
                    step(dve.tensor_scalar(p_row[0:32, :], p_row[0:32, :], stat8[0:32, 3:4], None, ALU.mult))
                    settle()
                    dve.tensor_scalar(self_p[0:32, :], const("sample_of_row")[0:32, :], p_row[0:32, 256:257], None, ALU.mult)\
                       .then_inc(dec_dve, 1)
                    dve.wait_ge(dec_pe, 3)
                    step(dve.tensor_copy(p_col.rearrange("p g m -> p (g m)"), bank(7)[:, 0:64]))
                    dve.tensor_copy(self_pt[0:NS, :], bank(7)[0:NS, 64:96]).then_inc(dec_dve, 1)

                    def conv(to, source, name, chunk, taps, bias, chunks):
                        w = lambda tap: pcol(name, tap * chunks + chunk)
                        if bias is None:
                            step(dve.tensor_scalar(to[:, 0:SEQ], source[:, 0:SEQ], w(taps - 1), None, ALU.mult))
                        else:
                            step(dve.tensor_scalar(to[:, 0:SEQ], source[:, 0:SEQ], w(taps - 1), bias, ALU.mult, ALU.add))
                        for back in range(1, taps):
                            settle()
                            step(dve.scalar_tensor_tensor(to[:, back:SEQ], source[:, 0:SEQ - back], w(taps - 1 - back),
                                                          to[:, back:SEQ], ALU.mult, ALU.add))

                    def conv8(to, window, name, taps, chunks, scratch, bias):
                        w = par[:, 0, AT[name]:AT[name] + taps * chunks].rearrange("p (t c) -> p c t", c=chunks)
                        pr = scratch[:, 0:chunks * NS * taps].rearrange("p (c b t) -> p c b t", b=NS, t=taps)
                        for c in range(chunks):
                            step(dve.tensor_tensor(pr[:, c], window[:, c], w[:, c].unsqueeze(1).broadcast_to([P, NS, taps]), ALU.mult))
                        settle()
                        for c in range(chunks):
                            step(dve.tensor_reduce(to[:, c, SEQ:T], pr[:, c], AX.X, ALU.add))
                        settle()
                        if bias is not None:
                            for c in range(chunks):
                                step(dve.tensor_scalar(to[:, c, SEQ:T], to[:, c, SEQ:T], pcol(bias, c), None, ALU.add))
                            settle()

                    dve.wait_ge(feat_ready, feat_count(*range(XBC, XBC + 6)))
                    for c in range(6):
                        step(dve.tensor_copy(ctx_d[:, c, :, D_CONV - 1], feat[:, XBC + c, SEQ:T]))
                    settle()
                    conv8(dc, ctx_d, "dconv_w", D_CONV, 6, prod_i, "dconv_b")
                    for c in range(6):
                        conv(dc[:, c, :], feat[:, XBC + c, :], "dconv_w", c, D_CONV, pcol("dconv_b", c), 6)
                    settle()
                    dve.sem_inc(conv_d_done, 1)

                    for n, (blk, h) in enumerate(IDX):
                        keys = (blk + 1) * P
                        w = kiw[:, blk, ID + h:ID + h + 1]
                        s = score[:, blk - 1, 0:keys]
                        dve.wait_ge(idx_rect, n + 1)
                        if h == 0:
                            dve.tensor_scalar(s, rect[:, n % 2, 0:keys], w, None, ALU.mult).then_inc(idx_added, 1)
                        else:
                            dve.wait_ge(idx_added, n)
                            dve.scalar_tensor_tensor(s, rect[:, n % 2, 0:keys], w, s, ALU.mult, ALU.add).then_inc(idx_added, 1)
                    dve.wait_ge(idx_added, len(IDX))
                    for blk in range(1, QT):
                        own = score[:, blk - 1, blk * P:(blk + 1) * P]
                        step(dve.tensor_tensor(own, own, const("future"), ALU.add))
                    def gate_c():
                        dve.wait_ge(feat_ready, feat_count(GA, GA + 1, GG, GG + 1))
                        for c in range(2):
                            dve.tensor_tensor(feat[:, GA + c, :], feat[:, GA + c, :], feat[:, GG + c, :], ALU.mult).then_inc(gate_in, 1)
                        dve.wait_ge(gate_in, 2)
                        for c in range(2):
                            step(dve.tensor_copy(ctx_c[:, c, :, C_CONV - 1], feat[:, GA + c, SEQ:T]))
                        settle()
                        conv8(feat[:, GG:GG + 2, :], ctx_c, "cconv_w", C_CONV, 2, prod_i, "cconv_b")
                        dve.sem_inc(cln_dve, 1)

                    for r in range(TOPK_PROMPT // 8):
                        if r == 4:
                            gate_c()
                        settle()
                        for blk in range(1, QT):
                            step(dve.max(chunk_best[:, blk - 1, :], score[:, blk - 1, 0:(blk + 1) * P]))
                        settle()
                        for blk in range(1, QT):
                            s = score[:, blk - 1, 0:(blk + 1) * P]
                            step(dve.match_replace(s, chunk_best[:, blk - 1, :], s, TAKEN))
                    settle()
                    for blk in range(1, QT):
                        s = score[:, blk - 1, 0:(blk + 1) * P]
                        step(dve.tensor_scalar(s, s, TAKEN, MASKED, ALU.not_equal, ALU.mult))
                    settle()

                    dve.wait_ge(feat_ready, feat_count(GC, GC + 1, BX, BX + 1, GB, GB + 1))
                    for c in range(2):
                        dve.tensor_tensor(feat[:, GC + c, :], feat[:, GC + c, :], feat[:, BX + c, :], ALU.mult).then_inc(gate_in, 1)
                    dve.wait_ge(gate_in, 4)
                    for c in range(2):
                        step(dve.tensor_copy(ctx_b[:, c, :, B_CONV - 1], feat[:, GC + c, SEQ:T]))
                    settle()
                    taps_left = list(range(C_CONV))

                    def conv_c_tap():
                        back = taps_left.pop(0)
                        w = pcol("cconv_w", 2 * (C_CONV - 1 - back))
                        acc = feat[:, GG, back:SEQ]
                        if back:
                            settle()
                            step(dve.scalar_tensor_tensor(acc, feat[:, GA, 0:SEQ - back], w, acc, ALU.mult, ALU.add))
                        else:
                            step(dve.tensor_scalar(acc, feat[:, GA, 0:SEQ], w, pcol("cconv_b", 0), ALU.mult, ALU.add))

                    for j in range(len(STEPS) + 1):
                        if j < len(STEPS):
                            blk, h = STEPS[j]
                            keys = (blk + 1) * P
                            dve.wait_ge(logits_summed, j + 1)
                            if j >= 2:
                                dve.wait_ge(prob_turned, j - 1)
                            mask = const("future") if blk == 0 else score[:, blk - 1, 0:keys]
                            step(dve.tensor_tensor_reduce(rect[:, j % 2, 0:keys], bank(3 + j % 3)[:, 0:keys], mask, 1.0, MASKED,
                                                          ALU.add, ALU.max, top_max[:, j % 2:j % 2 + 1]))
                            settle()
                            dve.tensor_scalar(neg_max[:, j % 2:j % 2 + 1], top_max[:, j % 2:j % 2 + 1], -HD ** -0.5, None,
                                              ALU.mult).then_inc(logits_masked, 1)
                        if j >= 1:
                            i = j - 1
                            blk, h = STEPS[i]
                            keys = (blk + 1) * P
                            b2 = slice(i % 2, i % 2 + 1)
                            dve.wait_ge(exp_done, i + 1)
                            step(dve.reciprocal(rden[:, b2], denom[:, b2]))
                            settle()
                            dve.tensor_scalar(rect[:, i % 2, 0:keys], rect[:, i % 2, 0:keys], rden[:, b2], None, ALU.mult)\
                               .then_inc(prob_ready, 1)
                        for _ in range(min(2, len(taps_left))):
                            conv_c_tap()

                    settle()
                    dve.sem_inc(conv_c_done, 1)

                    def lower(part, count, n=KC):
                        dve.wait_ge(part_hi, count)
                        dve.tensor_tensor(w_lo[part % 2][:, 0:n, :], raw[part % 4][:, 0:n, :],
                                          w_hi[part % 2][:, 0:n, :].bitcast(F32), ALU.subtract).then_inc(part_lo, 1)

                    conv8(feat[:, BX:BX + 2, :], ctx_b, "bconv_w", B_CONV, 2, prod_i, None)
                    for c in range(2):
                        conv(feat[:, BX + c, :], feat[:, GC + c, :], "bconv_w", c, B_CONV, None, 2)
                    settle()
                    for c in range(2):
                        dve.tensor_tensor(feat[:, BX + c, :], feat[:, BX + c, :], feat[:, GB + c, :], ALU.mult).then_inc(b_done, 1)

                    dve.wait_ge(dt_pe, 1)
                    cs4, dt4, we4 = (t.rearrange("p (c h) -> p c h", h=HEADS) for t in (cst_tok, dt_tok, w_end))
                    step(dve.tensor_copy(cst_tok, bank(6)[:, 0:QT * HEADS]))
                    dve.wait_ge(dt_pe, 6)
                    step(dve.tensor_copy(edt.rearrange("p q c b -> p (q c b)"), bank(7)[:, 0:32]))
                    dve.tensor_copy(dsk, bank(7)[:, 32:34]).then_inc(dt_dve, 1)
                    dve.wait_ge(dt_dve, 3)
                    settle()
                    dve.wait_ge(ssd_act, HEADS)
                    for h in range(HEADS):
                        ends = bank(h)[:, P - 1:SEQ:P]
                        step(dve.tensor_tensor(we4[:, :, h], ends, cs4[:, :, h], ALU.subtract))
                    settle()
                    dve.sem_inc(dt_dve, 1)
                    for h in range(HEADS):
                        for c in range(QT):
                            step(dve.scalar_tensor_tensor(decay[:, h * QT + c, :], bank(h)[:, c * P:(c + 1) * P],
                                                          cs4[:, c, h:h + 1], const("later"), ALU.subtract, ALU.add))
                        settle()
                        dve.sem_inc(segments, 1)
                    dve.wait_ge(dt_exp, 4)
                    step(dve.tensor_tensor(w_end, w_end, dt_tok, ALU.mult))
                    settle()
                    dve.wait_ge(mixed, len(STEPS))
                    dve.wait_ge(kv_stored, layer * (16 * N_KV) + 16 * N_KV)
                    for c in range(QT):
                        dve.wait_ge(ssd_act, HEADS + 1 + c)
                        dve.tensor_tensor(xw[:, c, :].rearrange("p (h c) -> p h c", c=HD),
                                          xb_tok[:, c, 0:W].rearrange("p (h c) -> p h c", c=HD),
                                          we4[:, c, :].unsqueeze(2).broadcast_to([P, HEADS, HD]), ALU.mult).then_inc(ssd_dve, 1)
                    dve.wait_ge(ssd_pe, 1)
                    for h in range(HEADS):
                        dve.wait_ge(ssd_act, HEADS + QT + 1 + h)
                        for c in range(QT):
                            m = decay[:, h * QT + c, :]
                            step(dve.scalar_tensor_tensor(m, m, dt4[:, c, h:h + 1], bank(4 + h // 2)[:, c * P:(c + 1) * P],
                                                          ALU.mult, ALU.mult))
                    settle()
                    dve.sem_inc(ssd_dve, 1)
                    for h in range(HEADS):
                        step(dve.tensor_tensor(read_c[:, h, :], dc[:, 4 + h // 2, 0:SEQ], ecs[:, h, :], ALU.mult))
                    settle()
                    dve.sem_inc(ssd_dve, 1)
                    flat_h = h_t.rearrange("p h c -> p (h c)")
                    for c in range(QT):
                        dve.wait_ge(state_pe, 2 * c + 2)
                        new = bank(6 + c % 2)[:, 0:W]
                        if c == 0:
                            dve.tensor_copy(flat_h, new).then_inc(state_dve, 1)
                        else:
                            end = ecs[:, :, (c + 1) * P - 1].unsqueeze(2).broadcast_to([P, HEADS, HD])
                            step(dve.tensor_tensor(h_t, h_t, end, ALU.mult))
                            settle()
                            dve.tensor_tensor(flat_h, flat_h, new, ALU.add).then_inc(state_dve, 1)
                        dve.wait_ge(state_dve, c + 1)
                    for c in range(2):
                        step(dve.scalar_tensor_tensor(dc[:, c, 0:SEQ], dc[:, c, 0:SEQ], dsk[:, c:c + 1], bank(2 + c), ALU.mult, ALU.add))
                    dve.wait_ge(state_pe, 2 * QT + 1)
                    dve.tensor_copy(ssm_rows.rearrange("p c n -> p (c n)"), bank(6)[:, 0:W]).then_inc(state_dve, 1)
                    dve.wait_ge(decd_pe, 1)
                    dve.tensor_copy(bc_rows, bank(4)[0:NS, :]).then_inc(decd_dve, 1)
                    step(dve.tensor_tensor(dtx, edt[:, 1], dc[:, 0:2, SEQ:T], ALU.mult))
                    settle()
                    dve.wait_ge(ssm_in, layer * 16 + 16)
                    for i in range(NS // 2):
                        if i == 1:
                            dve.wait_ge(cln_pe, 1)
                            for k in range(2):
                                f = halves(feat[:, GG + k, :])
                                step(dve.scalar_tensor_tensor(f, pair(0), -1.0 / W, f, ALU.mult, ALU.add))
                            settle()
                            dve.sem_inc(cln_dve, 1)
                        if i == 3:
                            reciprocal_root(cln_act, 3)
                        dve.wait_ge(decd_pe, 2 * i + 3)
                        two = [(q, 2 * i + q, bank(4 + (2 * i + q) % 4), c) for q in range(2) for c in range(2)]
                        for q, b, bc, c in two:
                            step(dve.tensor_scalar(prod_n[:, q, c, :], bc[:, c * P:(c + 1) * P], dtx[:, c, b:b + 1], None, ALU.mult))
                        settle()
                        for q, b, bc, c in two:
                            h = ssm[:, 2 * b + c, :]
                            step(dve.scalar_tensor_tensor(h, h, edt[:, 0, c, b:b + 1], prod_n[:, q, c, :], ALU.mult, ALU.add))
                        settle()
                        for q, b, bc, c in two:
                            step(dve.tensor_tensor_reduce(prod_n[:, q, c, :], ssm[:, 2 * b + c, :], bc[:, W + c * P:W + (c + 1) * P],
                                                          1.0, 0.0, ALU.mult, ALU.add, y_dec[:, c, b:b + 1]))
                        settle()
                        dve.sem_inc(decd_dve, 1)
                    dve.sem_inc(ssm_done, 1)
                    dve.wait_ge(rstd_spread, 2)
                    for c in range(2):
                        f = halves(feat[:, GG + c, :])
                        dve.scalar_tensor_tensor(f, f, pcol("cln_g", c), pair(0), ALU.mult, ALU.mult).then_inc(cln_dve, 1)
                    for c in range(2):
                        step(dve.scalar_tensor_tensor(dc[:, c, SEQ:T], dc[:, c, SEQ:T], dsk[:, c:c + 1], y_dec[:, c, :], ALU.mult, ALU.add))
                    settle()
                    for c in range(2):
                        step(dve.tensor_tensor(feat[:, ZG + c, :], feat[:, ZG + c, :], dc[:, c, :], ALU.mult))
                    settle()
                    dve.sem_inc(dn_dve, 1)
                    def y_lower(k, source):
                        dve.wait_ge(y_hi_ready, k // 2 + 1)
                        for c in range(2):
                            dve.tensor_tensor(y_lo[k + c][:, 0, :], source[:, c, :], u_hi[:, k + c, :].bitcast(F32), ALU.subtract)\
                               .then_inc(y_lo_ready, 1)

                    y_lower(4, feat[:, GG:GG + 2, :])
                    reciprocal_root(dn_act, 3)
                    dve.wait_ge(rstd_spread, 3)
                    for c in range(2):
                        f = halves(feat[:, ZG + c, :])
                        dve.scalar_tensor_tensor(f, f, pcol("d_norm", c), pair(1), ALU.mult, ALU.mult).then_inc(dn_dve, 1)
                    y_lower(6, feat[:, ZG:ZG + 2, :])
                    for m in range(KC):
                        lower(m + 2, m + 3)

                    def add_normed(n, u, gain):
                        reciprocal_root(root_ready, n + 1)
                        dve.wait_ge(rstd_spread, {1: 4, 3: 6}[n])
                        for k in range(KC + 1):
                            if k:
                                before = made[0]
                            if k < KC:
                                step(dve.scalar_tensor_tensor(halves(u[:, k, :]), halves(u[:, k, :]), pcol(gain, k),
                                                              pair({1: 0, 3: 2}[n]), ALU.mult, ALU.mult))
                            if k:
                                dve.wait_ge(vec, before)
                                dve.tensor_tensor(x[:, k - 1, :], x[:, k - 1, :], u[:, k - 1, :], ALU.add).then_inc(x_updated, 1)

                    add_normed(1, mix, "g_post_mix")
                    dve.wait_ge(stored, layer * (16 * N_SSM) + 16 * N_SSM)
                    normalise(2, "g_pre_ffn", scaled, u_scaled, u_hi_ready, u_lo_ready, [u_lo[:, k, :] for k in range(KC)])
                    dve.wait_ge(u_lo_ready, KC)

                    def hidden_tile(i, c, next_n):
                        lower(2 * c + 2, i * 4 + (GU0 + 2 * c + 3), next_n)
                        dve.wait_ge(gate_ready, i * 2 + (c + 1))
                        dve.wait_ge(up_summed, i * 2 + (c + 1))
                        dve.tensor_tensor(halves(hid_f[:, c, :]), halves(hid_gate[:, c, :]), pair(2 * c + 1), ALU.mult)\
                           .then_inc(hidden_made, 1)
                        lower(2 * c + 3, i * 4 + (GU0 + 2 * c + 4), next_n)
                        dve.wait_ge(hidden_hi, i * 2 + (c + 1))
                        dve.tensor_tensor(hid_lo[:, bass.ds(i * 2 + c, 1), :], hid_f[:, c:c + 1, :],
                                          hid_hi[:, bass.ds(i * 2 + c, 1), :].bitcast(F32), ALU.subtract).then_inc(hidden_lo, 1)

                    with dve.Fori(0, FFC // 2 - 1) as i:
                        for c in range(2):
                            hidden_tile(i, c, KC)
                    hidden_tile(FFC // 2 - 1, 0, KC)
                    hidden_tile(FFC // 2 - 1, 1, DOWN_PARTS[0][1])
                    with dve.Fori(0, KC // 2 - 1) as i:
                        for p in range(2, 10):
                            lower(p, i * 8 + (DN0 + p + 1), DOWN_PARTS[p % 4][1])
                    for p in range(2, 8):
                        lower(p, 4 * KC - 8 + DN0 + p + 1, DOWN_PARTS[p % 4][1])
                    add_normed(3, u, "g_post_ffn")
                    dve.wait_ge(x_updated, 2 * KC)

                @block.gpsimd
                def _(pool):
                    l = layer

                    def tokens(t):
                        return row(t, l)[0:1, 0].rearrange("o (t p) h c -> p (o t) (h c)", p=P) if t.ndim == 5 else \
                            row(t, l)[0:1, 0].rearrange("o (t p) c -> p (o t) c", p=P)

                    def tile_lower(f):
                        pool.wait_ge(tile_hi, f + 1)
                        pool.tensor_tensor(w_lo[f % 2][:, :, :], raw[(f + 2) % 4], w_hi[f % 2][:, :, :].bitcast(F32),
                                           ALU.subtract).then_inc(tile_lo, 1)

                    def slab_lower(s):
                        w = W if s < 4 else ID + IH + HEADS
                        pool.wait_ge(slab_hi, s + 2)
                        pool.tensor_tensor(tw_lo[s % 2][:, :, 0:w], slab_raw[s % 2][:, :, 0:w],
                                          tw_hi[s % 2][:, :, 0:w].bitcast(F32), ALU.subtract).then_inc(slab_lo, 1)

                    for half in range(2):
                        k = slice(half * KC // 2, (half + 1) * KC // 2)
                        pool.wait_ge(slab_hi, half + 1)
                        pool.tensor_tensor(tw_lo[0][:, k, :], slab_raw[0][:, k, :], tw_hi[0][:, k, :].bitcast(F32), ALU.subtract)\
                            .then_inc(slab_lo, 1)
                    for s in range(1, 3):
                        slab_lower(s)
                    pool.wait_ge(rope_done, 2)
                    pool.dma_start(tokens(k_prompt), tok_k).then_inc(kv_stored, 16)
                    slab_lower(3)
                    pool.wait_ge(tok_ready, 14)
                    pool.dma_start(tokens(v_prompt), tok_v).then_inc(kv_stored, 16)
                    slab_lower(4)
                    tile_lower(0)
                    tile_lower(1)
                    pool.wait_ge(rope_done, 5)
                    pool.dma_start(tokens(kidx_prompt), kiw[:, :, 0:ID]).then_inc(kv_stored, 16)
                    for t, at in ((k_sample, W), (v_sample, 2 * W)):
                        pool.dma_start(row(t, l).rearrange("o b s h c -> (o b s) (h c)"), tok8[:, at:at + W]).then_inc(kv_stored, 16)
                    pool.dma_start(row(kidx_sample, l).rearrange("o b s c -> (o b s) c"), tok8[:, 4 * W:4 * W + ID])\
                        .then_inc(kv_stored, 16)
                    for t, name in ((bconv_sample, "state_bconv"), (cconv_sample, "state_cconv"), (dconv_sample, "state_dconv")):
                        n = t.shape[2]
                        pool.dma_start(row(t, l)[:, :, 0:n - 1].rearrange("o b t c -> (o b) t c"),
                                       row(d[name], l)[:, :, 1:n].rearrange("o b t c -> (o b) t c")).then_inc(state_copied, 16)
                    def conv_c_tap(back):
                        w = pcol("cconv_w", 2 * (C_CONV - 1 - back) + 1)
                        acc = feat[:, GG + 1, back:SEQ]
                        if back == 0:
                            pool.tensor_scalar(acc, feat[:, GA + 1, 0:SEQ], w, pcol("cconv_b", 1), ALU.mult, ALU.add)\
                                .then_inc(pool_step, 1)
                            return
                        tap = pool_tmp[back % 2][:, back:SEQ]
                        pool.tensor_scalar(tap, feat[:, GA + 1, 0:SEQ - back], w, None, ALU.mult).then_inc(pool_step, 1)
                        pool.wait_ge(pool_step, 2 * back)
                        pool.tensor_tensor(acc, acc, tap, ALU.add).then_inc(pool_step, 1)

                    for f in range(2, len(feat_tiles)):
                        tile_lower(f)
                        if f == len(feat_tiles) - CONV_C_EARLY:
                            pool.wait_ge(gate_in, 2)
                            pool.wait_ge(cln_dve, 1)
                        if f >= len(feat_tiles) - CONV_C_EARLY:
                            conv_c_tap(f - len(feat_tiles) + CONV_C_EARLY)
                    pool.wait_ge(feat_summed, len(feat_tiles))
                    pool.dma_start(ssm, row(d["state_ssm"], l).rearrange("o b (c h) p n -> (h p) (o b c) n", c=2))\
                        .then_inc(ssm_in, 16)
                    for back in range(CONV_C_EARLY, C_CONV):
                        conv_c_tap(back)
                    pool.wait_ge(pool_step, 2 * C_CONV - 1)
                    pool.sem_inc(conv_c_done, 1)
                    pool.wait_ge(tails_ready, 4)
                    for src, lo, t_p, t_s in ((tail_b, 2, bconv_prompt, bconv_sample), (tail_c, 30, cconv_prompt, cconv_sample),
                                              (tail_d, 3, dconv_prompt, dconv_sample)):
                        pool.dma_start(row(t_p, l).rearrange("o b t c -> (o b t) c"), src[0:lo, :]).then_inc(tails_stored, 16)
                        pool.dma_start(row(t_s, l)[:, :, lo - 1].rearrange("o b c -> (o b) c"), src[lo:lo + NS, :])\
                            .then_inc(tails_stored, 16)
                    for n in range(2):
                        pool.wait_ge(part_hi, n + 1)
                        pool.tensor_tensor(w_lo[n][:, :, :], raw[n], w_hi[n][:, :, :].bitcast(F32), ALU.subtract)\
                            .then_inc(part_lo, 1)
                    for k, source in ((0, ya), (2, feat[:, BX:BX + 2, :])):
                        pool.wait_ge(y_hi_ready, k // 2 + 1)
                        for c in range(2):
                            pool.tensor_tensor(y_lo[k + c][:, 0, :], source[:, c, :], u_hi[:, k + c, :].bitcast(F32),
                                               ALU.subtract).then_inc(y_lo_early, 1)
                    pool.wait_ge(state_dve, QT + 1)
                    pool.dma_start(row(ssm_prompt, l)[0:1, 0].rearrange("o (c h) p n -> (h p) (o c) n", c=2), ssm_rows)\
                        .then_inc(stored, 16)
                    pool.wait_ge(ssm_done, 1)
                    pool.dma_start(row(ssm_sample, l).rearrange("o b (c h) p n -> (h p) (o b c) n", c=2), ssm).then_inc(stored, 16)

                    def add_squares(squares, n, ready, first):
                        for m in range(1, KC - 1):
                            pool.wait_ge(ready, first + 2 * (m + 1))
                            if n + m > 1:
                                pool.wait_ge(added, n + m - 1)
                            pool.tensor_tensor(squares[:, 0, :], squares[:, 0, :], squares[:, m, :], ALU.add).then_inc(added, 1)

                    add_squares(squares, 0, out_ready, 0)
                    add_squares(ffn_squares, KC - 2, down_ready, 4)
                    pool.wait_ge(kv_stored, layer * (16 * N_KV) + 16 * N_KV)
                    pool.wait_ge(state_copied, layer * (16 * N_STATES) + 16 * N_STATES)
                    pool.wait_ge(tails_stored, layer * (16 * N_TAILS) + 16 * N_TAILS)
                    pool.wait_ge(stored, layer * (16 * N_SSM) + 16 * N_SSM)

            nc.all_engine_barrier()
            nc.gpsimd.sem_clear(range(sems[first_layer_sem].num, sems[last_layer_sem - 1].num + 1))
            nc.all_engine_barrier()

        y_turned, y_copied, y_stored = sem("y_turned"), sem("y_copied"), sem("y_stored")
        y_rows = view(arena, 0, QT + 1, D_MODEL)
        with nc.Block() as block:
            @block.tensor
            def _(pe):
                for t in range(QT + 1):
                    m = P if t < QT else NS
                    for q in range(2):
                        n = 2 * t + q
                        if n >= 8:
                            pe.wait_ge(y_copied, n - 7)
                        for c in range(4):
                            last = pe.transpose(bank(n % 8)[0:m, c * P:(c + 1) * P], x[:, 4 * q + c, t * P:t * P + m], ident)
                        last.then_inc(y_turned, 1)

            @block.vector
            def _(dve):
                for t in range(QT + 1):
                    m = P if t < QT else NS
                    for q in range(2):
                        dve.wait_ge(y_turned, 2 * t + q + 1)
                        dve.tensor_copy(y_rows[0:m, t, 512 * q:512 * (q + 1)], bank((2 * t + q) % 8)[0:m, :]).then_inc(y_copied, 1)

            @block.sync
            def _(sp):
                for t in range(QT + 1):
                    sp.wait_ge(y_copied, 2 * t + 2)
                    to = y_prompt[0, t * P:(t + 1) * P, :] if t < QT else y_sample.rearrange("b s f -> (b s) f")
                    sp.dma_start(to, y_rows[0:P if t < QT else NS, t, :]).then_inc(y_stored, 16)
                sp.wait_ge(y_stored, 16 * (QT + 1))
    return nc


_INS = ["x_prompt", "x_sample", "cache_k", "cache_v", "cache_kidx", "page_table", "state_bconv", "state_cconv",
        "state_dconv", "state_ssm", "w_in", "w_out", "g_pre_mix", "g_post_mix", "g_pre_ffn", "g_post_ffn", "bconv_w",
        "cconv_w", "cconv_b", "cln_g", "cln_b", "dconv_w", "dconv_b", "dt_bias", "a_log", "d_skip", "d_norm",
        "ffn_gate", "ffn_up", "ffn_down"]
_XBC = W + 4 * N_STATE
_OUTS = [(1, SEQ, D_MODEL), (NS, 1, D_MODEL), (DEPTH, 1, SEQ, HEADS, HD), (DEPTH, 1, SEQ, HEADS, HD),
         (DEPTH, 1, SEQ, ID), (DEPTH, NS, 1, HEADS, HD), (DEPTH, NS, 1, HEADS, HD), (DEPTH, NS, 1, ID),
         (DEPTH, 1, 2, W), (DEPTH, NS, 2, W), (DEPTH, 1, 30, W), (DEPTH, NS, 30, W), (DEPTH, 1, 3, _XBC),
         (DEPTH, NS, 3, _XBC), (DEPTH, 1, HEADS, HD, N_STATE), (DEPTH, NS, HEADS, HD, N_STATE)]


def kernel(**inputs):
    import concourse.bacc as _bacc
    from concourse.bass_utils import run_bass_kernel_spmd as _run

    nc = _bacc.Bacc("TRN2", target_bir_lowering=False, num_devices=1)
    arrays, dram = {}, {}
    for name in _INS:
        a = np.ascontiguousarray(inputs[name])
        arrays[f"in_{name}"] = a
        dram[name] = nc.dram_tensor(f"in_{name}", a.shape, mybir.dt.from_np(a.dtype), kind="ExternalInput").ap()
    arrays["constants"] = shape_constants()
    dram["constants"] = nc.dram_tensor("constants", arrays["constants"].shape, F32, kind="ExternalInput").ap()
    outs = [nc.dram_tensor(f"out_{i}", shape, F32, kind="ExternalOutput").ap() for i, shape in enumerate(_OUTS)]
    hybrid_decoder(nc, dram, outs)
    r = _run(nc, [arrays], core_ids=[0])
    return tuple(r.results[0][f"out_{i}"] for i in range(len(_OUTS)))
```
